# Optimizing a Trainium2 kernel written in Bass

```python
import jax, jax.numpy as jnp
from jax import lax
import numpy as np

D_MODEL = 1024
BATCH = 1
SEQ = 256
DEPTH = 1

CHUNK = 64
EPS = 1e-6

MLA_HEADS = D_MODEL // 128
MLA_NOPE = 64
MLA_ROPE = 32
MLA_V = 64
Q_LORA = D_MODEL // 4
KV_LORA = D_MODEL // 8
ROPE_THETA = 10000.0
Q_BLOCK = 128

CA_HEADS = D_MODEL // 128
CA_DIM = 64
CA_LEFT = 8
CA_BAND = (CA_LEFT + 1) * CHUNK
REL_MAX = 256
REL_SIZE = CHUNK + REL_MAX

MIX_WIDTH = MLA_HEADS * MLA_V + CA_HEADS * CA_DIM
IN_WIDTH = Q_LORA + KV_LORA + MLA_ROPE + 3 * CA_HEADS * CA_DIM

N_EXPERTS = 32
TOP_K = 4
D_EXPERT = D_MODEL
SWIGLU_LIMIT = 7.0
SWIGLU_ALPHA = 1.702
ROW_BLOCK = 256

kernel_name = 'hybrid_mla_chunkattn_moe'

def _rmsnorm(x, g):
    xf = x.astype(jnp.float32)
    y = xf * lax.rsqrt(jnp.mean(xf * xf, axis=-1, keepdims=True) + EPS)
    return (y * g.astype(jnp.float32)).astype(x.dtype)

def _rope(x, cos, sin):
    xf = x.astype(jnp.float32)
    x1, x2 = jnp.split(xf, 2, axis=-1)
    return jnp.concatenate([x1 * cos - x2 * sin, x2 * cos + x1 * sin], axis=-1).astype(x.dtype)

def _mla_attention(q_nope, q_rope, k_nope, k_rope, v):
    bsz, seq, heads, _ = q_nope.shape
    nq = seq // Q_BLOCK
    qn = q_nope.reshape(bsz, nq, Q_BLOCK, heads, MLA_NOPE).transpose(1, 0, 2, 3, 4)
    qr = q_rope.reshape(bsz, nq, Q_BLOCK, heads, MLA_ROPE).transpose(1, 0, 2, 3, 4)
    k_chunk = jnp.arange(seq) // CHUNK
    scale = (MLA_NOPE + MLA_ROPE) ** -0.5

    def block(args):
        qn_b, qr_b, bi = args
        s = (jnp.einsum('bqhd,bkhd->bhqk', qn_b, k_nope)
             + jnp.einsum('bqhr,bkr->bhqk', qr_b, k_rope)).astype(jnp.float32) * scale
        q_chunk = (bi * Q_BLOCK + jnp.arange(Q_BLOCK)) // CHUNK
        mask = k_chunk[None, :] <= q_chunk[:, None]
        s = jnp.where(mask, s, -1e30)
        p = jax.nn.softmax(s, axis=-1).astype(v.dtype)
        return jnp.einsum('bhqk,bkhd->bqhd', p, v)

    o = lax.map(block, (qn, qr, jnp.arange(nq)))
    return o.transpose(1, 0, 2, 3, 4).reshape(bsz, seq, heads * MLA_V)

def _chunk_attention(q, k, v, rel_bias):
    bsz, seq, heads, dh = q.shape
    nc = seq // CHUNK
    qi = jnp.arange(CHUNK)[:, None]
    kk = jnp.arange(CA_BAND)[None, :]
    rel = qi - kk % CHUNK + (CA_LEFT - kk // CHUNK) * CHUNK
    idx = jnp.clip(rel, -(CHUNK - 1), REL_MAX) + (CHUNK - 1)
    bias = rel_bias.astype(jnp.float32)[:, idx]
    chunk_valid = (jnp.arange(nc)[:, None] - CA_LEFT + jnp.arange(CA_LEFT + 1)[None, :]) >= 0
    key_valid = jnp.repeat(chunk_valid, CHUNK, axis=1)
    scale = dh ** -0.5

    def per_seq(args):
        qs, ks, vs = args
        qc = qs.reshape(nc, CHUNK, heads, dh)
        pad = jnp.zeros((CA_LEFT * CHUNK, heads, dh), ks.dtype)
        kp = jnp.concatenate([pad, ks], axis=0).reshape(nc + CA_LEFT, CHUNK, heads, dh)
        vp = jnp.concatenate([pad, vs], axis=0).reshape(nc + CA_LEFT, CHUNK, heads, dh)
        kb = jnp.stack([kp[j:j + nc] for j in range(CA_LEFT + 1)], axis=1).reshape(nc, CA_BAND, heads, dh)
        vb = jnp.stack([vp[j:j + nc] for j in range(CA_LEFT + 1)], axis=1).reshape(nc, CA_BAND, heads, dh)
        s = jnp.einsum('cqhd,ckhd->chqk', qc, kb).astype(jnp.float32) * scale + bias[None]
        s = jnp.where(key_valid[:, None, None, :], s, -1e30)
        p = jax.nn.softmax(s, axis=-1).astype(vs.dtype)
        o = jnp.einsum('chqk,ckhd->cqhd', p, vb)
        return o.reshape(seq, heads * dh)

    return lax.map(per_seq, (q, k, v))

def _moe(h, w_router, b_router, w_gu, b_gu, w_down, b_down):
    bsz, seq, d = h.shape
    t = bsz * seq
    xt = h.reshape(t, d)
    logits = (xt @ w_router + b_router).astype(jnp.float32)
    top_val, top_idx = lax.top_k(logits, TOP_K)
    gates = jax.nn.softmax(top_val, axis=-1)
    m = t * TOP_K
    e = top_idx.reshape(m).astype(jnp.int32)
    tok = jnp.repeat(jnp.arange(t, dtype=jnp.int32), TOP_K)
    g = gates.reshape(m)
    order = jnp.argsort(e, stable=True)
    e_s, tok_s, g_s = e[order], tok[order], g[order]
    counts = jax.ops.segment_sum(jnp.ones((m,), jnp.int32), e, num_segments=N_EXPERTS)
    padded = ((counts + ROW_BLOCK - 1) // ROW_BLOCK) * ROW_BLOCK
    start = jnp.cumsum(counts) - counts
    pend = jnp.cumsum(padded)
    pstart = pend - padded
    dest = pstart[e_s] + jnp.arange(m, dtype=jnp.int32) - start[e_s]
    p_rows = m + N_EXPERTS * ROW_BLOCK
    nb = p_rows // ROW_BLOCK
    row_tok = jnp.full((p_rows,), t, jnp.int32).at[dest].set(tok_s)
    row_gate = jnp.zeros((p_rows,), g_s.dtype).at[dest].set(g_s)
    block_exp = jnp.minimum(jnp.searchsorted(pend, jnp.arange(nb, dtype=jnp.int32) * ROW_BLOCK, side='right'),
                            N_EXPERTS - 1)
    x_pad = jnp.concatenate([xt, jnp.zeros((1, d), xt.dtype)], axis=0)
    xin = x_pad[row_tok].reshape(nb, ROW_BLOCK, d)

    def expert_block(args):
        xb, eb = args
        gu = xb @ w_gu[eb] + b_gu[eb]
        gate = jnp.minimum(gu[:, :D_EXPERT], SWIGLU_LIMIT)
        up = jnp.clip(gu[:, D_EXPERT:], -SWIGLU_LIMIT, SWIGLU_LIMIT)
        glu = gate * jax.nn.sigmoid(gate * SWIGLU_ALPHA)
        return ((up + 1) * glu) @ w_down[eb] + b_down[eb]

    y = lax.map(expert_block, (xin, block_exp)).reshape(p_rows, d)
    y = y * row_gate[:, None].astype(y.dtype)
    out = jax.ops.segment_sum(y, row_tok, num_segments=t + 1)[:t]
    return out.reshape(bsz, seq, d)

def setup_inputs(seed: int = 0) -> dict:
    key = jax.random.key(seed)
    ks = jax.random.split(key, 24)
    L, D, E, F = DEPTH, D_MODEL, N_EXPERTS, D_EXPERT
    nrm = lambda k, shape, s: jax.random.normal(k, shape, jnp.float32) * s
    gain = lambda k, shape: 1.0 + 0.02 * jax.random.normal(k, shape, jnp.float32)
    return {
        'x': nrm(ks[0], (BATCH, SEQ, D), 1.0),
        'c': nrm(ks[1], (BATCH, D), 1.0),
        'w_ada': nrm(ks[2], (L, D, 6 * D), D ** -0.5),
        'b_ada': nrm(ks[3], (L, 6 * D), 0.02),
        'g_pre_mix': gain(ks[4], (L, D)),
        'g_post_mix': gain(ks[5], (L, D)),
        'g_pre_ffn': gain(ks[6], (L, D)),
        'g_post_ffn': gain(ks[7], (L, D)),
        'w_in': nrm(ks[8], (L, D, IN_WIDTH), D ** -0.5),
        'g_q': gain(ks[9], (L, Q_LORA)),
        'w_qb': nrm(ks[10], (L, Q_LORA, MLA_HEADS * (MLA_NOPE + MLA_ROPE)), Q_LORA ** -0.5),
        'g_kv': gain(ks[11], (L, KV_LORA)),
        'w_kvb': nrm(ks[12], (L, KV_LORA, MLA_HEADS * (MLA_NOPE + MLA_V)), KV_LORA ** -0.5),
        'rel_bias': nrm(ks[13], (L, CA_HEADS, REL_SIZE), 0.5),
        'w_o': nrm(ks[14], (L, MIX_WIDTH, D), MIX_WIDTH ** -0.5),
        'w_router': nrm(ks[15], (L, D, E), D ** -0.5),
        'b_router': nrm(ks[16], (L, E), 0.01),
        'w_gu': nrm(ks[17], (L, E, D, 2 * F), D ** -0.5),
        'b_gu': nrm(ks[18], (L, E, 2 * F), 0.02),
        'w_down': nrm(ks[19], (L, E, F, D), F ** -0.5),
        'b_down': nrm(ks[20], (L, E, D), 0.02),
    }

def reference(x, c, w_ada, b_ada, g_pre_mix, g_post_mix, g_pre_ffn, g_post_ffn, w_in, g_q, w_qb,
              g_kv, w_kvb, rel_bias, w_o, w_router, b_router, w_gu, b_gu, w_down, b_down):
    bsz, seq, _ = x.shape
    half = MLA_ROPE // 2
    inv_freq = ROPE_THETA ** (-jnp.arange(half, dtype=jnp.float32) / half)
    ang = jnp.arange(seq, dtype=jnp.float32)[:, None] * inv_freq[None, :]
    cos, sin = jnp.cos(ang), jnp.sin(ang)
    cut = np.cumsum([Q_LORA, KV_LORA, MLA_ROPE, CA_HEADS * CA_DIM, CA_HEADS * CA_DIM]).tolist()
    ca_shape = (bsz, seq, CA_HEADS, CA_DIM)
    for l in range(DEPTH):
        mod = jax.nn.silu(c) @ w_ada[l] + b_ada[l]
        sh1, sc1, gt1, sh2, sc2, gt2 = jnp.split(mod, 6, axis=-1)
        h = _rmsnorm(x, g_pre_mix[l]) * (1 + sc1[:, None, :]) + sh1[:, None, :]
        z = h @ w_in[l]
        cq, ckv, kr, qc, kc, vc = jnp.split(z, cut, axis=-1)
        q = (_rmsnorm(cq, g_q[l]) @ w_qb[l]).reshape(bsz, seq, MLA_HEADS, MLA_NOPE + MLA_ROPE)
        q_nope = q[..., :MLA_NOPE]
        q_rope = _rope(q[..., MLA_NOPE:], cos[:, None, :], sin[:, None, :])
        kv = (_rmsnorm(ckv, g_kv[l]) @ w_kvb[l]).reshape(bsz, seq, MLA_HEADS, MLA_NOPE + MLA_V)
        k_nope, v_mla = kv[..., :MLA_NOPE], kv[..., MLA_NOPE:]
        k_rope = _rope(kr, cos, sin)
        o_a = _mla_attention(q_nope, q_rope, k_nope, k_rope, v_mla)
        o_b = _chunk_attention(qc.reshape(ca_shape), kc.reshape(ca_shape), vc.reshape(ca_shape), rel_bias[l])
        o = jnp.concatenate([o_a, o_b], axis=-1) @ w_o[l]
        x = x + gt1[:, None, :] * _rmsnorm(o, g_post_mix[l])
        h = _rmsnorm(x, g_pre_ffn[l]) * (1 + sc2[:, None, :]) + sh2[:, None, :]
        f = _moe(h, w_router[l], b_router[l], w_gu[l], b_gu[l], w_down[l], b_down[l])
        x = x + gt2[:, None, :] * _rmsnorm(f, g_post_ffn[l])
    return x


_drawn_inputs = setup_inputs


def setup_inputs(seed=0):
    import zlib

    import numpy as np

    out = dict(_drawn_inputs(seed))
    spreads = {}
    factors = {'g_post_ffn': 6.283, 'g_q': 3.543, 'b_gu': 6.095, 'b_down': 8.0}
    for name, (base, spread) in spreads.items():
        noise = np.random.default_rng([zlib.crc32(name.encode()), seed]).standard_normal(out[name].shape)
        drawn = base * np.exp(spread * noise) if base else spread * noise
        out[name] = __import__('jax').numpy.asarray(drawn.astype(out[name].dtype))
    for name, factor in factors.items():
        out[name] = (out[name] * factor).astype(out[name].dtype)
    return out
```

```python
from contextlib import ExitStack

import numpy as np

import concourse.bass as bass
from concourse import mybir

ALU = mybir.AluOpType
ACT = mybir.ActivationFunctionType
AX = mybir.AxisListType
F32 = mybir.dt.float32
BF16 = mybir.dt.bfloat16
I32 = mybir.dt.int32
U32 = mybir.dt.uint32

P = 128
D = 1024
KC = D // P
SEQ = 256
TH = SEQ // P
CHUNK = 64
EPS = 1e-6
HEADS = 8
NOPE, ROPE, VD = 64, 32, 64
QK = NOPE + ROPE
HALF = ROPE // 2
QL, KVL = D // 4, D // 8
ZA = QL + KVL + ROPE
CAW = HEADS * 64
E = 32
F = D
TOPK = 4
LIMIT, ALPHA = 7.0, 1.702
NEG = -1e30

SLOT = 64
MAXBLK = SEQ // SLOT
JOBS = 64
UNIT = 4096
ARENA = 21600
UNITS = 6
GU_UNITS = 4

SH1, SC1, GT1, SH2, SC2, GT2 = range(6)
GAINED = [SC1, GT1, SC2, GT2]
QW = D // 4

C_ID, C_MASK, C_IOTA, C_TRI, C_ROPE, C_TRIE, C_SEL3, C_J, C_EPS, C_END = np.cumsum(
    [0, P, 2 * P, SEQ, P, 2 * 2 * HALF, E + 1, E, 1, 1]).tolist()

GROUPS = []
for mixer in range(2):
    for b in range(TH):
        n = 4 // (b + 1)
        order = list(range(HEADS)) if mixer == 0 else [0, 2, 4, 6, 1, 3, 5, 7]
        GROUPS += [(mixer, b, order[i:i + n]) for i in range(0, HEADS, n)]


def shape_constants():
    c = np.zeros((P, C_END), np.float32)
    p = np.arange(P)
    c[:, C_ID:C_ID + P] = np.eye(P)
    c[:CHUNK, C_MASK + P + CHUNK:C_MASK + 2 * P] = NEG
    c[:, C_IOTA:C_IOTA + SEQ] = np.arange(SEQ)
    c[:, C_TRI:C_TRI + P] = p[:, None] < p[None, :]
    inv = np.float32(10000.0) ** (-np.arange(HALF, dtype=np.float32) / np.float32(HALF))
    ang = np.arange(SEQ, dtype=np.float32)[:, None] * inv[None, :].astype(np.float32)
    for t in range(TH):
        a = ang[t * P:(t + 1) * P]
        c[:, C_ROPE + 2 * HALF * t:C_ROPE + 2 * HALF * (t + 1)] = np.concatenate([np.cos(a), np.sin(a)], 1)
    c[:E, C_TRIE:C_TRIE + E + 1] = np.arange(E)[:, None] < np.arange(E + 1)[None, :]
    c[:3 * E, C_SEL3:C_SEL3 + E] = np.tile(np.eye(E), (3, 1))
    c[:, C_J] = p
    c[:, C_EPS] = EPS
    return c


def build(nc, x, c, w_ada, b_ada, g_pre_mix, g_post_mix, g_pre_ffn, g_post_ffn, w_in, g_q, w_qb,
          g_kv, w_kvb, rel_bias, w_o, w_router, b_router, w_gu, b_gu, w_down, b_down, consts, out):
    ctx = ExitStack()
    with ctx:
        def sb(name, shape, dt=F32):
            return ctx.enter_context(nc.sbuf_tensor(name, shape, dt))

        def sem(name):
            return ctx.enter_context(nc.semaphore(name))

        ctx.enter_context(nc.allow_non_contiguous_dma("gain columns"))

        ring = sb("ring", [P, UNITS, UNIT])
        xs = sb("xs", [P, TH, D])
        cst = sb("cst", [P, C_END])
        mod = sb("mod", [P, 6, QW])
        gain = sb("gain", [P, 4, QW])
        silu_c = sb("silu_c", [P, KC, 32])
        b3 = sb("b3", [3 * E, 2 * F], BF16)
        small = sb("small", [P, 136])
        arena = sb("arena", [P, ARENA])

        ident = cst[:, C_ID:C_ID + P]
        iota = cst[:, C_IOTA:C_IOTA + SEQ]
        tri = cst[:, C_TRI:C_TRI + P]
        eps = cst[:, C_EPS:C_EPS + 1]

        at = [0]

        def take(shape, dt=F32, start=None):
            n = int(np.prod(shape[1:]))
            w = n if dt != BF16 else (n + 1) // 2
            s = at[0] if start is None else start
            if start is None:
                at[0] += w
                assert at[0] <= ARENA, at[0]
            v = arena[0:shape[0], s:s + w]
            if dt != F32:
                v = v.bitcast(dt)
            if len(shape) == 3:
                v = v.rearrange("p (a b) -> p a b", a=shape[1])
            if len(shape) == 4:
                v = v.rearrange("p (a b c) -> p a b c", a=shape[1], b=shape[2])
            return v

        hT = take([P, KC, SEQ])
        base_w = at[0]
        wqb = take([P, QL // P, HEADS * QK])
        wkvb = take([P, HEADS * (NOPE + VD)])
        za = take([P, TH, ZA])
        cqT = take([P, QL // P, SEQ])
        ckvT = take([P, SEQ])
        base_q = at[0]
        q_t = take([P, TH, HEADS, QK])
        k_t = take([P, TH, HEADS, QK])
        v_a = take([P, TH, HEADS * VD])
        v_b = take([P, TH, CAW])
        base_qT = at[0]
        qT = take([QK, HEADS, SEQ])
        kT = take([QK, HEADS, SEQ])
        qcT = take([P, HEADS // 2, SEQ])
        kcT = take([P, HEADS // 2, SEQ])
        bias = take([P, HEADS, SEQ])
        xn = take([P, TH, D], start=base_q)
        s_sb = take([P, 2, 512], start=base_w)
        p_sb = take([P, 2, 512], start=base_w + 1024)
        pT = take([P, 2, 512], start=base_w + 2048)
        o_sb = take([P, TH, D], start=base_q)
        b_gu_f = take([3 * E, 2 * F], start=base_qT)
        rope_t = take([P, 4, HEADS, HALF], start=base_qT)
        oT = hT
        end_mixer = at[0]
        at[0] = 0
        skip_oT = take([P, KC, SEQ])
        h2 = take([P, TH, D])
        bc = take([P, 4, D])
        h2T = take([P, KC, SEQ])
        hb = take([P, TH, 3, D], BF16)
        wr = take([P, KC, E])
        bd = take([E, D])
        at2 = at[0]
        xgT = take([P, KC * SLOT], start=0)
        gm = take([P, 512], start=512)
        sg = take([P, 512], start=1024)
        up1 = take([P, 512], start=1536)
        act_b = take([P, 512], start=2048)
        actT = take([P, 512], start=2560)
        y_sb = take([P, 512], start=3072)
        at[0] = at2
        sel = take([P, TH, SLOT], BF16)
        selG = take([P, TH, 2, SLOT])
        selGT = take([P, SEQ])
        bsel = take([3 * E, SLOT], BF16)
        lg = take([P, TH, E])
        top = take([P, TH, 8])
        topi = take([P, TH, 8], U32)
        topf = take([P, TH, 8])
        gates = take([P, TH, 8])
        M = take([P, TH, E])
        G = take([P, TH, E])
        posm = take([P, TH, E])
        oh = take([P, TH, E])
        brt = take([P, E])
        GT = take([E, SEQ])
        nbc = take([E, 4])
        jt = take([JOBS, 72])
        tab = take([1, 256], I32)
        out_sb = take([P, TH, D], start=2048)

        T_J, T_NB, T_E, T_B = 0, E + 1, 2 * E + 1, 2 * E + 1 + JOBS

        cc, ecc, rcc = small[:, 0:8], small[:, 8:16], small[:, 16:24]
        cols = small[:, 24:40]
        gq_col, gkv_col = small[:, 40:42], small[:, 42:43]
        ssq, rms, rstd = small[:, 44:52], small[:, 52:60], small[:, 60:68]
        nmax = small[:, 68:76]
        rsum = small[:, 76:108]
        rrec = small[:, 108:116]
        nb_neg = small[:, 116:118]
        gsum = small[:, 118:120]
        ones = small[:, 128:129]

        ps = ctx.enter_context(nc.psum_tensor("ps", [P, 8, 512], F32))

        L = {n: sem("in_" + n) for n in (
            "x", "c", "cst", "bada", "gain", "gcol", "wq", "wkv", "relb", "bgu", "adaA", "adaB", "winA", "winQ", "winK",
            "winV", "gt1", "wo", "sh2", "sc2", "gt2", "wr", "bd")}
        S = {n: sem(n) for n in (
            "ones_ok", "bias_mask", "c_exp", "silu", "x_sq", "x_rms", "xn_ok", "xT_ps", "ada_ps", "mod_ok", "col_ps", "col_ok",
            "hT_act", "hT_dve", "za_ps", "qc_ps", "kc_ps", "vc_ps", "qc_sb", "kc_sb", "vc_sb", "za_sb", "lat_sq", "lat_rms",
            "lat_n", "lat_ps", "lat_T", "q_ps", "kv_ps", "q_sb", "k_sb", "v_sb", "q_rot", "qk_ps", "qT_act", "qT_dve",
            "b3_ok", "sc_ps", "sc_sb", "max_ok", "exp_ok", "pT_ps", "pT_act", "pT_dve", "pv_ps", "o_ok", "oT_ps", "oT_act",
            "oT_dve", "bc_ps", "bc_sb", "wo_ps", "o_sq", "o_rms", "x1_ok", "x1_sq", "x1_rms", "h2_ok", "h2T_ps", "h2T_sb", "hb_ok",
            "lg_ps", "g_exp", "gate_ok", "G_ok", "cnt_ps", "nb_ok", "end_ps", "je_ok", "row_ps", "tab_ok", "pos_ok", "GT_ps",
            "GT_sb", "acc_ok", "chain_v", "chain_a", "chain_p",
            "sel_ok", "gath_ps", "xg_ok", "gate_ps", "up_ok", "comb_ps", "selT_ps", "selT_sb", "gm_ok", "sig_ok", "act_ok",
            "actT_ps", "actT_sb", "y_sb", "f_sq", "f_rms", "res_ok", "stored")}
        arrived = [sem(f"unit_arrived{u}") for u in range(UNITS)]
        used = [sem(f"unit_used{u}") for u in range(UNITS)]

        x_v = x[0].rearrange("(t p) d -> p t d", p=P)
        out_v = out[0].rearrange("(t p) d -> p t d", p=P)
        ada_v = w_ada[0].rearrange("(p j) n -> p j n", j=KC)
        win_v = w_in[0].rearrange("(k p) n -> p k n", p=P)
        wo_v = w_o[0].rearrange("(k p) n -> p k n", p=P)
        gu_v = w_gu[0].rearrange("e (k p) n -> e p k n", p=P)
        dn_v = w_down[0].rearrange("e (k p) n -> e p k n", p=P)

        def ada_w(u):
            return ring[:, u:u + 2, :].rearrange("p a b -> p (a b)").rearrange("p (j n) -> p j n", j=KC)

        ada_at = {SH1: 0, SC1: 2, GT1: 2, SH2: 0, SC2: 2, GT2: 0}
        ada_in = {SH1: "adaA", SC1: "adaB", GT1: "gt1", SH2: "sh2", SC2: "sc2", GT2: "gt2"}
        w_za = ring[:, 4, 0:KC * ZA].rearrange("p (k n) -> p k n", k=KC)
        w_q = ring[:, 5, :].rearrange("p (k n) -> p k n", k=KC)
        w_k = ring[:, 0, :].rearrange("p (k n) -> p k n", k=KC)
        w_v = ring[:, 1, :].rearrange("p (k n) -> p k n", k=KC)
        w_om = ring[:, 4:6, :].rearrange("p a b -> p (a b)").rearrange("p (k n) -> p k n", k=KC)
        w_gum = [ring[:, u, :].rearrange("p (k n) -> p k n", k=2) for u in range(GU_UNITS)]
        w_dnm = [ring[:, GU_UNITS + u, :].rearrange("p (k n) -> p k n", k=4) for u in range(2)]

        def unit_src(e, u):
            if u < GU_UNITS:
                return gu_v[e, :, 2 * u:2 * u + 2, :]
            return dn_v[e, :, 4 * (u - GU_UNITS):4 * (u - GU_UNITS) + 4, :]

        def unit_dst(u):
            return w_gum[u] if u < GU_UNITS else w_dnm[u - GU_UNITS]

        block = ctx.enter_context(nc.Block())

        @block.sync
        def _(sp):
            sp.dma_start(xs[:, :, :], x_v).then_inc(L["x"], 16)

            def ada(v):
                sp.dma_start(ada_w(ada_at[v]), ada_v[:, :, v * D:(v + 1) * D]).then_inc(L[ada_in[v]], 16)

            ada(SH1)
            ada(SC1)
            sp.dma_start(w_za, win_v[:, :, 0:ZA]).then_inc(L["winA"], 16)
            sp.dma_start(w_q, win_v[:, :, ZA:ZA + CAW]).then_inc(L["winQ"], 16)
            sp.wait_ge(S["ada_ps"], 1)
            sp.dma_start(w_k, win_v[:, :, ZA + CAW:ZA + 2 * CAW]).then_inc(L["winK"], 16)
            sp.dma_start(w_v, win_v[:, :, ZA + 2 * CAW:ZA + 3 * CAW]).then_inc(L["winV"], 16)
            sp.wait_ge(S["ada_ps"], 2)
            ada(GT1)
            sp.wait_ge(S["za_ps"], 1)
            sp.wait_ge(S["qc_ps"], 1)
            sp.dma_start(w_om, wo_v).then_inc(L["wo"], 16)
            sp.wait_ge(S["kc_ps"], 1)
            sp.wait_ge(S["vc_ps"], 1)
            ada(SH2)
            sp.wait_ge(S["ada_ps"], 3)
            ada(SC2)
            sp.wait_ge(S["ada_ps"], 4)
            ada(GT2)

            def first(u):
                sp.dma_start(unit_dst(u), unit_src(0, u)).then_inc(arrived[u], 16)

            sp.wait_ge(S["ada_ps"], 5)
            first(2)
            first(3)
            sp.wait_ge(S["ada_ps"], 6)
            first(0)
            first(1)
            sp.wait_ge(S["wo_ps"], 2)
            first(4)
            first(5)
            sp.wait_ge(S["tab_ok"], 1)
            with sp.Fori(0, E - 1) as e:
                jobs_done = sp.value_load(tab[0:1, bass.ds(T_J + 1 + e, 1)], min_val=1, max_val=JOBS)
                for u in range(UNITS):
                    sp.wait_ge(used[u], jobs_done)
                    src = (gu_v[bass.ds(e + 1, 1), :, 2 * u:2 * u + 2, :] if u < GU_UNITS else
                           dn_v[bass.ds(e + 1, 1), :, 4 * (u - GU_UNITS):4 * (u - GU_UNITS) + 4, :])
                    sp.dma_start(unit_dst(u), src.rearrange("a p k n -> p (a k) n")).then_inc(arrived[u], 16)
            for t in range(TH):
                sp.wait_ge(S["res_ok"], t + 1)
                sp.dma_start(out_v[:, t, :], out_sb[:, t, :]).then_inc(S["stored"], 16)
            sp.wait_ge(S["stored"], 16 * TH)

        @block.gpsimd
        def _(pool):
            chain = [0]

            def link(ins):
                chain[0] += 1
                ins.then_inc(S["chain_p"], 1)
                pool.wait_ge(S["chain_p"], chain[0])

            link(nc.gpsimd.memset(bias[0:CHUNK, :, 0:CHUNK], NEG))
            nc.gpsimd.memset(ones, 1.0).then_inc(S["ones_ok"], 1)
            pool.wait_ge(S["ones_ok"], 1)

            pool.wait_ge(L["bgu"], 48)
            r = b_gu_f
            link(nc.gpsimd.tensor_copy(b3[:, :], r))
            for first in (E, 2 * E):
                for i in range(first // E, 3):
                    rows = slice(i * E, (i + 1) * E)
                    link(nc.gpsimd.tensor_tensor(r[rows, :], r[rows, :], b3[rows, :], ALU.subtract))
                    link(nc.gpsimd.tensor_copy(b3[rows, :], r[rows, :]))
            nc.gpsimd.memset(small[:, 129:130], 0.0).then_inc(S["b3_ok"], 1)

            pool.wait_ge(S["oT_ps"], 4)
            pool.dma_start(wr, w_router[0].rearrange("(k p) n -> p k n", p=P)).then_inc(L["wr"], 16)
            pool.dma_start(brt, b_router.partition_broadcast(P)[:, 0, :]).then_inc(L["wr"], 16)
            pool.dma_start(bd, b_down[0]).then_inc(L["bd"], 16)

            pool.wait_ge(S["h2_ok"], TH)
            for i in range(3):
                nc.gpsimd.tensor_copy(hb[:, :, i, :], h2).then_inc(S["hb_ok"], 1)
                if i < 2:
                    pool.wait_ge(S["hb_ok"], 2 * i + 1)
                    if i == 0:
                        pool.wait_ge(S["h2T_ps"], 2)
                    nc.gpsimd.tensor_tensor(h2, h2, hb[:, :, i, :], ALU.subtract).then_inc(S["hb_ok"], 1)
                    pool.wait_ge(S["hb_ok"], 2 * i + 2)

        @block.tensor
        def _(pe):
            mm = nc.tensor.matmul

            def transposes(blocks, dst):
                for i, (src, m) in enumerate(blocks):
                    last = nc.tensor.transpose(dst[0:m, i * P:(i + 1) * P], src, ident)
                return last

            def ada(v, bank, col):
                w = ada_w(ada_at[v])
                pe.wait_ge(L[ada_in[v]], 16)
                for j in range(KC):
                    for g in range(4):
                        last = mm(ps[32 * g:32 * g + 32, bank, col:col + QW], silu_c[:, j, :],
                                  w[:, j, g * QW:(g + 1) * QW], start=(j == 0), stop=(j == KC - 1))
                last.then_inc(S["ada_ps"], 1)

            def spread(v, bank):
                for g in range(4):
                    last = mm(ps[:, bank + g // 2, (g % 2) * QW:(g % 2 + 1) * QW],
                              ident[:, 32 * g:32 * g + 1].to_broadcast([P, P]), mod[:, v, :],
                              start=True, stop=True)
                last.then_inc(S["bc_ps"], 1)

            pe.wait_ge(L["cst"], 16)
            pe.wait_ge(S["silu"], 1)
            ada(SH1, 4, 0)
            pe.wait_ge(S["xn_ok"], 1)
            for b in range(4):
                last = transposes([(xn[:, t, (2 * b + i) * P:(2 * b + i + 1) * P], P)
                                   for i in range(2) for t in range(TH)], ps[:, b, :])
                last.then_inc(S["xT_ps"], 1)
            ada(SC1, 5, 0)
            pe.wait_ge(S["mod_ok"], 2)
            for v in (SH1, SC1):
                for k in range(KC):
                    last = mm(ps[:, 6, v * KC + k:v * KC + k + 1], mod[:, v, (k % 2) * P:(k % 2 + 1) * P],
                              ident[:, 32 * (k // 2):32 * (k // 2) + 1], start=True, stop=True)
            last.then_inc(S["col_ps"], 1)

            pe.wait_ge(S["hT_act"], 4)
            pe.wait_ge(S["hT_dve"], 4)
            pe.wait_ge(L["winA"], 16)
            for t in range(TH):
                for k in range(KC):
                    last = mm(ps[:, 6 + t, 0:ZA], hT[:, k, t * P:(t + 1) * P], w_za[:, k, :],
                              start=(k == 0), stop=(k == KC - 1))
            last.then_inc(S["za_ps"], 1)
            for name, w, bank, done in (("winQ", w_q, 0, "qc_ps"), ("winK", w_k, 2, "kc_ps")):
                pe.wait_ge(L[name], 16)
                for hp in range(HEADS // 2):
                    for k in range(KC):
                        last = mm(ps[:, bank + hp // 2, (hp % 2) * SEQ:(hp % 2 + 1) * SEQ],
                                  w[:, k, hp * P:(hp + 1) * P], hT[:, k, :], start=(k == 0), stop=(k == KC - 1))
                last.then_inc(S[done], 1)
            pe.wait_ge(S["lat_n"], 1)
            for i in range(3):
                last = transposes([(za[:, t, i * P:(i + 1) * P], P) for t in range(TH)],
                                  ps[:, 6 + i // 2, (i % 2) * SEQ:(i % 2 + 1) * SEQ])
            last.then_inc(S["lat_ps"], 1)
            pe.wait_ge(L["winV"], 16)
            for t in range(TH):
                for k in range(KC):
                    last = mm(ps[:, 4 + t, :], hT[:, k, t * P:(t + 1) * P], w_v[:, k, :],
                              start=(k == 0), stop=(k == KC - 1))
            last.then_inc(S["vc_ps"], 1)
            pe.wait_ge(S["lat_T"], 1)
            pe.wait_ge(S["qc_sb"], 1)
            pe.wait_ge(S["kc_sb"], 1)
            pe.wait_ge(L["wq"], 16)
            W2 = HEADS * QK // 2
            for t in range(TH):
                for n in range(2):
                    for k in range(QL // P):
                        last = mm(ps[:, 2 * t + n, 0:W2], cqT[:, k, t * P:(t + 1) * P],
                                  wqb[:, k, n * W2:(n + 1) * W2], start=(k == 0), stop=(k == QL // P - 1))
            last.then_inc(S["q_ps"], 1)
            pe.wait_ge(S["vc_sb"], 1)
            pe.wait_ge(L["wkv"], 16)
            for t in range(TH):
                for n in range(2):
                    last = mm(ps[:, 4 + 2 * t + n, :], ckvT[:, t * P:(t + 1) * P],
                              wkvb[:, n * 512:(n + 1) * 512], start=True, stop=True)
            last.then_inc(S["kv_ps"], 1)
            pe.wait_ge(S["q_rot"], 1)
            pe.wait_ge(S["k_sb"], 4)
            pe.wait_ge(S["v_sb"], 1)
            for i, src in enumerate((q_t, k_t)):
                for n in range(2):
                    for t in range(TH):
                        last = transposes([(src[:, t, 4 * n + h, :], QK) for h in range(4)],
                                          ps[:, 4 * i + 2 * n + t, :])
                        last.then_inc(S["qk_ps"], 1)

            pe.wait_ge(S["qT_act"], 4)
            pe.wait_ge(S["qT_dve"], 4)
            ada(GT1, 6, 0)
            ada(SH2, 7, 0)

            def scores(i):
                mixer, b, heads = GROUPS[i]
                K = (b + 1) * P
                if i >= 2:
                    pe.wait_ge(S["sc_sb"], i - 1)
                for n, h in enumerate(heads):
                    if mixer == 0:
                        l, r = qT[:, h, b * P:(b + 1) * P], kT[:, h, 0:K]
                    else:
                        row = 64 * (h % 2)
                        l = qcT[row:row + 64, h // 2, b * P:(b + 1) * P]
                        r = kcT[row:row + 64, h // 2, 0:K]
                    last = mm(ps[:, i % 2, n * K:(n + 1) * K], l, r, start=True, stop=True)
                last.then_inc(S["sc_ps"], 1)

            scores(0)
            scores(1)
            for i, (mixer, b, heads) in enumerate(GROUPS):
                pe.wait_ge(S["exp_ok"], i + 1)
                if i >= 2:
                    pe.wait_ge(S["pT_act" if i % 2 == 0 else "pT_dve"], i // 2)
                transposes([(p_sb[:, i % 2, j * P:(j + 1) * P], P) for j in range(4)],
                           ps[:, 2 + i % 2, :]).then_inc(S["pT_ps"], 1)
                if i + 2 < len(GROUPS):
                    scores(i + 2)
                part = 2 * mixer + b
                if part >= 2 and i and GROUPS[i - 1][:2] != (mixer, b):
                    pe.wait_ge(S["o_ok"], part - 1)
                pe.wait_ge(S["pT_act" if i % 2 == 0 else "pT_dve"], i // 2 + 1)
                vals = v_a if mixer == 0 else v_b
                for n, h in enumerate(heads):
                    for kb in range(b + 1):
                        j = n * (b + 1) + kb
                        last = mm(ps[:, 4 + part % 2, h * VD:(h + 1) * VD], pT[:, i % 2, j * P:(j + 1) * P],
                                  vals[:, kb, h * VD:(h + 1) * VD], start=(kb == 0), stop=(kb == b))
                last.then_inc(S["pv_ps"], 1)
            pe.wait_ge(S["mod_ok"], 4)
            ada(SC2, 6, 256)
            ada(GT2, 7, 256)

            pe.wait_ge(S["o_ok"], 4)
            for b in range(4):
                transposes([(o_sb[:, t, (2 * b + i) * P:(2 * b + i + 1) * P], P) for i in range(2) for t in range(TH)],
                           ps[:, b, :]).then_inc(S["oT_ps"], 1)
            pe.wait_ge(S["oT_act"], 2)
            pe.wait_ge(S["oT_dve"], 2)
            pe.wait_ge(S["mod_ok"], 6)
            spread(GT1, 0)
            spread(SH2, 2)
            pe.wait_ge(L["wo"], 16)
            for t in range(TH):
                for n in range(2):
                    for k in range(KC):
                        last = mm(ps[:, 4 + 2 * t + n, :], oT[:, k, t * P:(t + 1) * P],
                                  w_om[:, k, n * 512:(n + 1) * 512], start=(k == 0), stop=(k == KC - 1))
                last.then_inc(S["wo_ps"], 1)
                pe.wait_ge(S["bc_sb"], t + 1)
                spread(SC2 if t == 0 else GT2, 2 * t)

            pe.wait_ge(S["bc_sb"], 4)
            for t in range(TH):
                pe.wait_ge(S["h2_ok"], t + 1)
                for b in range(2):
                    last = transposes([(h2[:, t, (4 * b + i) * P:(4 * b + i + 1) * P], P) for i in range(4)],
                                      ps[:, 4 + 2 * t + b, :])
                last.then_inc(S["h2T_ps"], 1)
            pe.wait_ge(L["wr"], 32)
            for t in range(TH):
                pe.wait_ge(S["h2T_sb"], 2 * (t + 1))
                for k in range(KC):
                    last = mm(ps[:, 0, t * E:(t + 1) * E], h2T[:, k, t * P:(t + 1) * P], wr[:, k, :],
                              start=(k == 0), stop=(k == KC - 1))
            last.then_inc(S["lg_ps"], 1)

            pe.wait_ge(S["G_ok"], 1)
            for t in range(TH):
                mm(ps[0:E, 1, 0:1], M[:, t, :], ones, start=(t == 0), stop=(t == TH - 1))
            mm(ps[:, 1, E:2 * E], tri, M[:, 0, :], start=True, stop=True)
            mm(ps[:, 1, 2 * E:3 * E], tri, M[:, 1, :], start=True, stop=False)
            mm(ps[:, 1, 2 * E:3 * E], ones.to_broadcast([P, P]), M[:, 0, :], start=False,
               stop=True).then_inc(S["cnt_ps"], 1)
            for t in range(TH):
                last = nc.tensor.transpose(ps[0:E, 2, t * P:(t + 1) * P], G[:, t, :], ident)
            last.then_inc(S["GT_ps"], 1)
            pe.wait_ge(S["nb_ok"], 1)
            nb = nbc[:, 0:1]
            trie = cst[0:E, C_TRIE:C_TRIE + E + 1]
            mm(ps[0:JOBS, 3, 0:E], nb.to_broadcast([E, JOBS]), trie[:, 1:E + 1], start=True, stop=True)
            mm(ps[0:JOBS, 3, E:2 * E], nb.to_broadcast([E, JOBS]), ident[0:E, 0:E], start=True,
               stop=True).then_inc(S["end_ps"], 1)
            pe.wait_ge(S["je_ok"], 1)
            mm(ps[0:1, 4, T_J:T_J + E + 1], nb, trie, start=True, stop=True)
            mm(ps[0:1, 4, T_NB:T_NB + E], nb, ident[0:E, 0:E], start=True, stop=True)
            mm(ps[0:1, 4, T_E:T_E + JOBS], jt[:, 64:65], ident[0:JOBS, 0:JOBS], start=True, stop=True)
            mm(ps[0:1, 4, T_B:T_B + JOBS], jt[:, 65:66], ident[0:JOBS, 0:JOBS], start=True,
               stop=True).then_inc(S["row_ps"], 1)

            pe.wait_ge(S["GT_sb"], 1)
            pe.wait_ge(S["nb_ok"], 1)
            pe.wait_ge(S["pos_ok"], 1)
            pe.wait_ge(L["bd"], 16)
            for t in range(TH):
                for n in range(2):
                    mm(ps[:, 2 * t + n, :], GT[:, t * P:(t + 1) * P], bd[:, n * 512:(n + 1) * 512],
                       start=True, stop=True)

            GATE, UP, Y, TR = 4, 5, 6, 7

            def gather():
                for k in range(KC):
                    n = 0
                    for t in range(TH):
                        for i in range(3):
                            last = mm(ps[:, GATE, k * SLOT:(k + 1) * SLOT], hb[:, t, i, k * P:(k + 1) * P],
                                      sel[:, t, :], start=(n == 0), stop=(n == 5))
                            n += 1
                last.then_inc(S["gath_ps"], 1)

            def combine():
                for t in range(TH):
                    for n in range(2):
                        last = mm(ps[:, 2 * t + n, :], selGT[64 * n:64 * n + 64, t * P:(t + 1) * P],
                                  y_sb[64 * n:64 * n + 64, :], start=False, stop=True, skip_group_check=True)
                return last

            pe.wait_ge(S["hb_ok"], 5)
            pe.wait_ge(S["b3_ok"], 1)
            pe.wait_ge(S["tab_ok"], 1)
            pe.wait_ge(S["sel_ok"], 1)
            gather()
            with pe.Fori(0, E) as e:
                blocks = pe.value_load(tab[0:1, bass.ds(T_NB + e, 1)], min_val=1, max_val=MAXBLK)
                before = pe.value_load(tab[0:1, bass.ds(T_J + e, 1)], min_val=0, max_val=JOBS)
                with pe.Fori(0, blocks) as blk:
                    job = pe.snap(before + blk)
                    pe.wait_ge(S["xg_ok"], job + 1)
                    for bank in range(2):
                        for g in range(2):
                            mm(ps[64 * g:64 * g + 64, GATE + bank, :], bsel,
                               b3[:, bank * F + 512 * g:bank * F + 512 * g + 512], start=True, stop=False)
                    for u in range(GU_UNITS):
                        pe.wait_ge(arrived[u], 16 * (e + 1))
                        last_unit = u == GU_UNITS - 1
                        seq = ([(bank, k) for bank in range(2) for k in range(2)] if last_unit else
                               [(bank, k) for k in range(2) for bank in range(2)])
                        for bank, k in seq:
                            kk = 2 * u + k
                            for g in range(2):
                                last = mm(ps[64 * g:64 * g + 64, GATE + bank, :], xgT[:, kk * SLOT:(kk + 1) * SLOT],
                                          w_gum[u][:, k, bank * F + 512 * g:bank * F + 512 * g + 512],
                                          start=False, stop=(kk == KC - 1))
                            if last_unit and (bank, k) == (0, 1):
                                last.then_inc(S["gate_ps"], 1)
                        last.then_inc(used[u], 1)
                    pe.wait_ge(S["y_sb"], job + 1)
                    pe.wait_ge(S["selT_sb"], job + 1)
                    combine()
                    pe.wait_ge(S["sel_ok"], job + 1)
                    for t in range(TH):
                        last = nc.tensor.transpose(ps[:, Y, t * P:(t + 1) * P],
                                                   selG[:, t, :, :].rearrange("p a s -> p (a s)"), ident)
                    last.then_inc(S["selT_ps"], 1)
                    pe.wait_ge(S["act_ok"], job + 1)
                    transposes([(act_b[:, j * P:(j + 1) * P], P) for j in range(4)],
                               ps[:, TR, :]).then_inc(S["actT_ps"], 1)
                    pe.wait_ge(S["actT_sb"], job + 1)
                    pe.wait_ge(S["selT_sb"], job + 2)
                    for d in range(2):
                        pe.wait_ge(arrived[GU_UNITS + d], 16 * (e + 1))
                        for j in range(4):
                            for n in range(2):
                                last = mm(ps[64 * n:64 * n + 64, Y, :], actT[:, j * P + 64 * d:j * P + 64 * d + 64],
                                          w_dnm[d][:, j, 512 * n:512 * n + 512],
                                          start=(d == 0 and j == 0), stop=(d == 1 and j == 3))
                        last.then_inc(used[GU_UNITS + d], 1)
                        if d == 0:
                            pe.wait_ge(S["sel_ok"], job + 2)
                            gather()
            total = pe.value_load(tab[0:1, T_J + E:T_J + E + 1], min_val=E, max_val=JOBS)
            pe.wait_ge(S["y_sb"], total + 1)
            combine().then_inc(S["comb_ps"], 1)

        @block.scalar
        def _(act):
            a = nc.scalar.activation
            chain = [0]

            def link(ins):
                chain[0] += 1
                ins.then_inc(S["chain_a"], 1)
                act.wait_ge(S["chain_a"], chain[0])

            act.dma_start(cc, c[0].rearrange("(p j) -> p j", j=KC)).then_inc(L["c"], 16)
            act.dma_start(cst[:, :], consts).then_inc(L["cst"], 16)
            for g in range(4):
                act.dma_start(mod[32 * g:32 * g + 32, :, :], b_ada.rearrange("a (v n) -> a v n", v=6)[
                    :, :, g * QW:(g + 1) * QW].partition_broadcast(32)[:, 0]).then_inc(L["bada"], 16)
            for i, src in enumerate((g_pre_mix, g_post_mix, g_pre_ffn, g_post_ffn)):
                for g in range(4):
                    act.dma_start(gain[32 * g:32 * g + 32, i, :],
                                  src[:, g * QW:(g + 1) * QW].partition_broadcast(32)[:, 0]).then_inc(L["gain"], 16)
            act.dma_start(gq_col, g_q[0].rearrange("(k p) -> p k", p=P)).then_inc(L["gcol"], 16)
            act.dma_start(gkv_col, g_kv[0].rearrange("(k p) -> p k", p=P)).then_inc(L["gcol"], 16)

            act.wait_ge(L["c"], 16)
            a(ecc, cc, ACT.Exp, scale=-1.0).then_inc(S["c_exp"], 1)
            act.wait_ge(L["x"], 16)
            act.dma_start(wqb, w_qb[0].rearrange("(k p) n -> p k n", p=P)).then_inc(L["wq"], 16)
            act.dma_start(wkvb, w_kvb[0]).then_inc(L["wkv"], 16)
            for i in range(3):
                act.dma_start(b_gu_f[i * E:(i + 1) * E, :], b_gu[0]).then_inc(L["bgu"], 16)
            act.wait_ge(S["ones_ok"], 1)
            hank = bass.AP(tensor=rel_bias.tensor, offset=rel_bias.offset,
                           ap=[[1, CHUNK], [CHUNK + SEQ, HEADS], [1, SEQ]])
            act.dma_start(bias[CHUNK:P, :, :], hank).then_inc(L["relb"], 16)
            hank = bass.AP(tensor=rel_bias.tensor, offset=rel_bias.offset,
                           ap=[[1, CHUNK], [CHUNK + SEQ, HEADS], [1, SEQ - CHUNK]])
            act.dma_start(bias[0:CHUNK, :, CHUNK:SEQ], hank).then_inc(L["relb"], 16)
            for t in range(TH):
                link(a(xn[:, t, :], xs[:, t, :], ACT.Square, accum_out=ssq[:, t:t + 1]))
            act.wait_ge(L["cst"], 16)
            a(rms[:, 0:2], ssq[:, 0:2], ACT.Sqrt, bias=eps, scale=1.0 / D).then_inc(S["x_rms"], 1)
            act.wait_ge(S["col_ok"], 1)
            act.wait_ge(S["xT_ps"], 4)
            for k in range(4, KC):
                a(hT[:, k, :], ps[:, k // 2, (k % 2) * SEQ:(k % 2 + 1) * SEQ], ACT.Identity,
                  bias=cols[:, k:k + 1], scale=cols[:, KC + k:KC + k + 1]).then_inc(S["hT_act"], 1)
            act.wait_ge(S["za_ps"], 1)
            for t in range(TH):
                last = nc.scalar.copy(za[:, t, :], ps[:, 6 + t, 0:ZA])
            link(last)
            for t in range(TH):
                a(cqT[:, t, :], za[:, t, 0:QL], ACT.Square, accum_out=ssq[:, 2 + t:3 + t])
                last = a(ckvT[:, t * P:(t + 1) * P], za[:, t, QL:QL + KVL], ACT.Square, accum_out=ssq[:, 4 + t:5 + t])
            link(last)
            a(rms[:, 2:4], ssq[:, 2:4], ACT.Sqrt, bias=eps, scale=1.0 / QL)
            a(rms[:, 4:6], ssq[:, 4:6], ACT.Sqrt, bias=eps, scale=1.0 / KVL).then_inc(S["lat_rms"], 1)
            act.wait_ge(S["qc_ps"], 1)
            for b in range(2):
                last = nc.scalar.copy(qcT[:, 2 * b:2 * b + 2, :], ps[:, b, :].rearrange("p (a s) -> p a s", a=2))
            last.then_inc(S["qc_sb"], 1)
            act.wait_ge(S["kc_ps"], 1)
            for b in range(2):
                last = nc.scalar.copy(kcT[:, 2 * b:2 * b + 2, :], ps[:, 2 + b, :].rearrange("p (a s) -> p a s", a=2))
            last.then_inc(S["kc_sb"], 1)
            act.wait_ge(S["vc_ps"], 1)
            for t in range(TH):
                last = nc.scalar.copy(v_b[:, t, :], ps[:, 4 + t, :])
            last.then_inc(S["vc_sb"], 1)
            act.wait_ge(S["q_ps"], 1)
            for t in range(TH):
                for n in range(2):
                    last = nc.scalar.copy(q_t[:, t, 4 * n:4 * n + 4, :],
                                          ps[:, 2 * t + n, 0:4 * QK].rearrange("p (h d) -> p h d", h=4))
            last.then_inc(S["q_sb"], 1)
            for t in range(TH):
                for n in range(2):
                    act.wait_ge(S["k_sb"], 2 * t + n + 1)
                    last = nc.scalar.copy(
                        v_a[:, t, 4 * n * VD:4 * (n + 1) * VD].rearrange("p (h d) -> p h d", h=4),
                        ps[:, 4 + 2 * t + n, :].rearrange("p (h d) -> p h d", h=4)[:, :, NOPE:])
            last.then_inc(S["v_sb"], 1)
            for i in range(4):
                act.wait_ge(S["qk_ps"], 5 + i)
                n, t = i // 2, i % 2
                nc.scalar.copy(kT[:, 4 * n:4 * n + 4, t * P:(t + 1) * P],
                               ps[0:QK, 4 + i, :].rearrange("p (h s) -> p h s", h=4)).then_inc(S["qT_act"], 1)

            def exps(i):
                mixer, b, heads = GROUPS[i]
                K = (b + 1) * P
                act.wait_ge(S["max_ok"], i + 1)
                if i >= 2:
                    act.wait_ge(S["pT_ps"], i - 1)
                for n, h in enumerate(heads):
                    r = (2 * mixer + b) * HEADS + h
                    last = a(p_sb[:, i % 2, n * K:(n + 1) * K], s_sb[:, i % 2, n * K:(n + 1) * K], ACT.Exp,
                             bias=nmax[:, 4 * (i % 2) + n:4 * (i % 2) + n + 1], accum_out=rsum[:, r:r + 1])
                last.then_inc(S["exp_ok"], 1)

            exps(0)
            for i in range(len(GROUPS)):
                if i + 1 < len(GROUPS):
                    exps(i + 1)
                if i % 2 == 0:
                    act.wait_ge(S["pT_ps"], i + 1)
                    if i >= 2:
                        act.wait_ge(S["pv_ps"], i - 1)
                    nc.scalar.copy(pT[:, 0, :], ps[:, 2, :]).then_inc(S["pT_act"], 1)
            for b in range(2):
                act.wait_ge(S["oT_ps"], b + 1)
                nc.scalar.copy(oT[:, 2 * b:2 * b + 2, :], ps[:, b, :].rearrange("p (a s) -> p a s", a=2)).then_inc(S["oT_act"], 1)
            act.wait_ge(S["oT_ps"], 4)
            for i in range(4):
                act.wait_ge(S["bc_ps"], i + 1)
                b = 2 * (i % 2)
                nc.scalar.copy(bc[:, i, 0:512], ps[:, b, :])
                nc.scalar.copy(bc[:, i, 512:D], ps[:, b + 1, :]).then_inc(S["bc_sb"], 1)
            for t in range(TH):
                act.wait_ge(S["wo_ps"], t + 1)
                for n in range(2):
                    last = a(h2[:, t, n * 512:(n + 1) * 512], ps[:, 4 + 2 * t + n, :], ACT.Square,
                             accum_out=ssq[:, 2 * t + n:2 * t + n + 1])
                last.then_inc(S["o_sq"], 1)
                act.wait_ge(S["o_sq"], 2 * t + 2)
                a(rms[:, t:t + 1], ssq[:, 6:7], ACT.Sqrt, bias=eps, scale=1.0 / D).then_inc(S["o_rms"], 1)
                act.wait_ge(S["x1_ok"], t + 1)
                link(a(h2[:, t, :], xs[:, t, :], ACT.Square, accum_out=ssq[:, 7:8]))
                a(rms[:, 2 + t:3 + t], ssq[:, 7:8], ACT.Sqrt, bias=eps, scale=1.0 / D).then_inc(S["x1_rms"], 1)
            for t in range(TH):
                act.wait_ge(S["h2T_ps"], t + 1)
                for b in range(2):
                    nc.scalar.copy(h2T[:, 4 * b:4 * b + 4, t * P:(t + 1) * P],
                                   ps[:, 4 + 2 * t + b, :].rearrange("p (k s) -> p k s", k=4)).then_inc(S["h2T_sb"], 1)
            act.wait_ge(S["gate_ok"], 1)
            for t in range(TH):
                last = a(gates[:, t, 0:TOPK], top[:, t, 0:TOPK], ACT.Exp, bias=nb_neg[:, t:t + 1],
                         accum_out=gsum[:, t:t + 1])
            last.then_inc(S["g_exp"], 1)

            act.wait_ge(S["tab_ok"], 1)
            act.wait_ge(S["gath_ps"], 1)
            act.wait_ge(S["hb_ok"], 5)
            act.wait_ge(S["lg_ps"], 1)
            nc.scalar.copy(xgT, ps[:, 4, :]).then_inc(S["xg_ok"], 1)
            total = act.value_load(tab[0:1, T_J + E:T_J + E + 1], min_val=E, max_val=JOBS)
            with act.Fori(0, total) as job:
                act.wait_ge(S["gm_ok"], job + 1)
                a(sg, gm, ACT.Sigmoid, scale=ALPHA).then_inc(S["sig_ok"], 1)
                act.wait_ge(S["selT_ps"], job + 1)
                nc.scalar.copy(selGT, ps[:, 6, 0:SEQ]).then_inc(S["selT_sb"], 1)
                act.wait_ge(S["gath_ps"], job + 2)
                nc.scalar.copy(xgT, ps[:, 4, :]).then_inc(S["xg_ok"], 1)
                act.wait_ge(used[UNITS - 1], job + 1)
                nc.scalar.copy(y_sb, ps[:, 6, :]).then_inc(S["y_sb"], 1)

            act.wait_ge(S["comb_ps"], 1)
            for t in range(TH):
                for n in range(2):
                    link(a(gm, ps[:, 2 * t + n, :], ACT.Square, accum_out=ssq[:, 2 * t + n:2 * t + n + 1]))
            nc.scalar.copy(small[:, 130:131], ssq[:, 0:1]).then_inc(S["f_sq"], 1)
            act.wait_ge(S["f_sq"], 2)
            a(rms[:, 0:2], ssq[:, 4:6], ACT.Sqrt, bias=eps, scale=1.0 / D).then_inc(S["f_rms"], 1)

        @block.vector
        def _(dve):
            v = nc.vector
            chain = [0]

            def link(ins):
                chain[0] += 1
                ins.then_inc(S["chain_v"], 1)
                dve.wait_ge(S["chain_v"], chain[0])

            dve.wait_ge(S["c_exp"], 1)
            link(v.tensor_scalar(ecc, ecc, 1.0, None, ALU.add))
            link(v.reciprocal(rcc, ecc))
            link(v.tensor_tensor(rcc, rcc, cc, ALU.mult))
            v.tensor_copy(silu_c[:, :, :], rcc.unsqueeze(2).to_broadcast([P, KC, 32])).then_inc(S["silu"], 1)
            dve.wait_ge(S["x_rms"], 1)
            link(v.reciprocal(rstd[:, 0:2], rms[:, 0:2]))
            for t in range(TH):
                last = v.tensor_scalar(xn[:, t, :], xs[:, t, :], rstd[:, t:t + 1], None, ALU.mult)
            last.then_inc(S["xn_ok"], 1)

            def mod_row(i, vec, bank, col):
                dve.wait_ge(S["ada_ps"], i + 1)
                if i == 0:
                    dve.wait_ge(L["bada"], 64)
                    dve.wait_ge(L["gain"], 256)
                first = v.tensor_tensor(mod[:, vec, :], ps[:, bank, col:col + QW], mod[:, vec, :], ALU.add)
                if vec in GAINED:
                    link(first)
                    plus = 1.0 if vec in (SC1, SC2) else 0.0
                    first = v.scalar_tensor_tensor(mod[:, vec, :], mod[:, vec, :], plus,
                                                   gain[:, GAINED.index(vec), :], ALU.add, ALU.mult)
                first.then_inc(S["mod_ok"], 1)

            mod_row(0, SH1, 4, 0)
            mod_row(1, SC1, 5, 0)
            dve.wait_ge(S["col_ps"], 1)
            v.tensor_copy(cols, ps[:, 6, 0:2 * KC]).then_inc(S["col_ok"], 1)
            dve.wait_ge(S["col_ok"], 1)
            dve.wait_ge(S["xT_ps"], 4)
            for k in range(4):
                v.tensor_scalar(hT[:, k, :], ps[:, k // 2, (k % 2) * SEQ:(k % 2 + 1) * SEQ],
                                cols[:, KC + k:KC + k + 1], cols[:, k:k + 1], ALU.mult, ALU.add).then_inc(S["hT_dve"], 1)
            dve.wait_ge(S["lat_rms"], 1)
            link(v.reciprocal(rstd[:, 2:6], rms[:, 2:6]))
            for t in range(TH):
                v.tensor_scalar(za[:, t, 0:QL], za[:, t, 0:QL], rstd[:, 2 + t:3 + t], None, ALU.mult)
                last = v.tensor_scalar(za[:, t, QL:QL + KVL], za[:, t, QL:QL + KVL], rstd[:, 4 + t:5 + t], None, ALU.mult)
            last.then_inc(S["lat_n"], 1)
            dve.wait_ge(S["lat_ps"], 1)
            dve.wait_ge(L["gcol"], 32)
            for k in range(2):
                v.tensor_scalar(cqT[:, k, :], ps[:, 6, k * SEQ:(k + 1) * SEQ], gq_col[:, k:k + 1], None, ALU.mult)
            v.tensor_scalar(ckvT, ps[:, 7, 0:SEQ], gkv_col, None, ALU.mult).then_inc(S["lat_T"], 1)

            def rotate(x1, x2, shape, t, tmp):
                cs = cst[:, C_ROPE + 2 * HALF * t:C_ROPE + 2 * HALF * t + HALF]
                sn = cst[:, C_ROPE + 2 * HALF * t + HALF:C_ROPE + 2 * HALF * (t + 1)]
                if len(shape) == 3:
                    cs, sn = cs.unsqueeze(1).to_broadcast(shape), sn.unsqueeze(1).to_broadcast(shape)
                v.tensor_tensor(tmp[0], x1, cs, ALU.mult)
                v.tensor_tensor(tmp[1], x2, sn, ALU.mult)
                v.tensor_tensor(tmp[2], x2, cs, ALU.mult)
                link(v.tensor_tensor(tmp[3], x1, sn, ALU.mult))
                v.tensor_tensor(x1, tmp[0], tmp[1], ALU.subtract)
                return v.tensor_tensor(x2, tmp[2], tmp[3], ALU.add)

            dve.wait_ge(S["b3_ok"], 1)
            for t in range(TH):
                kr = za[:, t, QL + KVL:ZA]
                link(rotate(kr[:, 0:HALF], kr[:, HALF:ROPE], [P, HALF], t, [rope_t[:, i, 0, :] for i in range(4)]))
            dve.wait_ge(S["q_sb"], 1)
            for t in range(TH):
                last = rotate(q_t[:, t, :, NOPE:NOPE + HALF], q_t[:, t, :, NOPE + HALF:QK], [P, HEADS, HALF], t,
                              [rope_t[:, i] for i in range(4)])
                if t == 0:
                    link(last)
            last.then_inc(S["q_rot"], 1)
            dve.wait_ge(S["kv_ps"], 1)
            for t in range(TH):
                v.tensor_copy(k_t[:, t, :, NOPE:QK],
                              za[:, t, QL + KVL:ZA].unsqueeze(1).to_broadcast([P, HEADS, ROPE]))
                for n in range(2):
                    v.tensor_copy(k_t[:, t, 4 * n:4 * n + 4, 0:NOPE],
                                  ps[:, 4 + 2 * t + n, :].rearrange("p (h d) -> p h d", h=4)[:, :, 0:NOPE]).then_inc(
                                      S["k_sb"], 1)
            for i in range(4):
                dve.wait_ge(S["qk_ps"], 1 + i)
                if i == 0:
                    dve.wait_ge(S["q_rot"], 1)
                n, t = i // 2, i % 2
                v.tensor_copy(qT[:, 4 * n:4 * n + 4, t * P:(t + 1) * P],
                              ps[0:QK, i, :].rearrange("p (h s) -> p h s", h=4)).then_inc(S["qT_dve"], 1)
            mod_row(2, GT1, 6, 0)
            mod_row(3, SH2, 7, 0)

            def soften(i):
                mixer, b, heads = GROUPS[i]
                K, n = (b + 1) * P, len(heads)
                if i == 0:
                    dve.wait_ge(L["relb"], 32)
                dve.wait_ge(S["sc_ps"], i + 1)
                if i >= 2:
                    dve.wait_ge(S["exp_ok"], i - 1)
                if mixer == 0:
                    add = cst[:, C_MASK + (1 - b) * P:C_MASK + 2 * P].unsqueeze(1).to_broadcast([P, n, K])
                    scale = QK ** -0.5
                else:
                    step = heads[1] - heads[0]
                    add = bias[:, heads[0]:heads[-1] + 1:step, K - 1::-1]
                    scale = 64 ** -0.5
                s3 = s_sb[:, i % 2, :].rearrange("p (n k) -> p n k", n=n)
                v.scalar_tensor_tensor(s3, ps[:, i % 2, :].rearrange("p (n k) -> p n k", n=n), scale, add,
                                       ALU.mult, ALU.add).then_inc(S["sc_sb"], 1)
                dve.wait_ge(S["sc_sb"], i + 1)
                v.tensor_reduce(nmax[:, 4 * (i % 2):4 * (i % 2) + n], s3, AX.X, ALU.max,
                                negate=True).then_inc(S["max_ok"], 1)

            soften(0)
            soften(1)
            for i, (mixer, b, heads) in enumerate(GROUPS):
                if i % 2 == 1:
                    dve.wait_ge(S["pT_ps"], i + 1)
                    if i >= 2:
                        dve.wait_ge(S["pv_ps"], i - 1)
                    v.tensor_copy(pT[:, 1, :], ps[:, 3, :]).then_inc(S["pT_dve"], 1)
                if i + 2 < len(GROUPS):
                    soften(i + 2)
                if i + 1 == len(GROUPS) or GROUPS[i + 1][:2] != (mixer, b):
                    part = 2 * mixer + b
                    dve.wait_ge(S["exp_ok"], i + 1)
                    link(v.reciprocal(rrec, rsum[:, part * HEADS:(part + 1) * HEADS]))
                    dve.wait_ge(S["pv_ps"], i + 1)
                    v.tensor_tensor(o_sb[:, b, mixer * 512:(mixer + 1) * 512].rearrange("p (h d) -> p h d", h=HEADS),
                                    ps[:, 4 + part % 2, :].rearrange("p (h d) -> p h d", h=HEADS),
                                    rrec.unsqueeze(2).to_broadcast([P, HEADS, VD]), ALU.mult).then_inc(S["o_ok"], 1)
            mod_row(4, SC2, 6, 256)
            mod_row(5, GT2, 7, 256)
            for b in range(2):
                dve.wait_ge(S["oT_ps"], b + 3)
                v.tensor_copy(oT[:, 4 + 2 * b:6 + 2 * b, :],
                              ps[:, 2 + b, :].rearrange("p (a s) -> p a s", a=2)).then_inc(S["oT_dve"], 1)

            for t in range(TH):
                dve.wait_ge(S["o_sq"], 2 * t + 1)
                v.tensor_tensor(ssq[:, 6:7], ssq[:, 2 * t:2 * t + 1], ssq[:, 2 * t + 1:2 * t + 2],
                                ALU.add).then_inc(S["o_sq"], 1)
                dve.wait_ge(S["o_rms"], t + 1)
                link(v.reciprocal(rstd[:, t:t + 1], rms[:, t:t + 1]))
                dve.wait_ge(S["bc_sb"], 1)
                for n in range(2):
                    last = v.scalar_tensor_tensor(h2[:, t, n * 512:(n + 1) * 512], ps[:, 4 + 2 * t + n, :],
                                                  rstd[:, t:t + 1], bc[:, 0, n * 512:(n + 1) * 512], ALU.mult, ALU.mult)
                link(last)
                v.tensor_tensor(xs[:, t, :], xs[:, t, :], h2[:, t, :], ALU.add).then_inc(S["x1_ok"], 1)
                dve.wait_ge(S["x1_rms"], t + 1)
                link(v.reciprocal(rstd[:, 2 + t:3 + t], rms[:, 2 + t:3 + t]))
                dve.wait_ge(S["bc_sb"], 3)
                link(v.scalar_tensor_tensor(h2[:, t, :], xs[:, t, :], rstd[:, 2 + t:3 + t], bc[:, 2, :],
                                            ALU.mult, ALU.mult))
                v.tensor_tensor(h2[:, t, :], h2[:, t, :], bc[:, 1, :], ALU.add).then_inc(S["h2_ok"], 1)

            dve.wait_ge(S["lg_ps"], 1)
            dve.wait_ge(L["wr"], 32)
            link(v.tensor_tensor(lg, ps[:, 0, 0:TH * E].rearrange("p (t e) -> p t e", t=TH),
                                 brt.unsqueeze(1).to_broadcast([P, TH, E]), ALU.add))
            for t in range(TH):
                last = v.max(top[:, t, :], lg[:, t, :])
            link(last)
            v.tensor_scalar(nb_neg, top[:, :, 0], -1.0, None, ALU.mult).then_inc(S["gate_ok"], 1)
            for t in range(TH):
                last = v.max_index(topi[:, t, :], top[:, t, :], lg[:, t, :])
            link(last)
            link(v.tensor_copy(topf, topi))
            dve.wait_ge(S["g_exp"], 1)
            link(v.reciprocal(gsum, gsum))
            for t in range(TH):
                last = v.tensor_scalar(gates[:, t, 0:TOPK], gates[:, t, 0:TOPK], gsum[:, t:t + 1], None, ALU.mult)
            link(last)
            for j in range(TOPK):
                for t in range(TH):
                    m_out, g_out = (M, G) if j == 0 else (oh, lg)
                    v.tensor_scalar(m_out[:, t, :], iota[:, 0:E], topf[:, t, j:j + 1], None, ALU.is_equal)
                    last = v.tensor_scalar(g_out[:, t, :], iota[:, 0:E], topf[:, t, j:j + 1], gates[:, t, j:j + 1],
                                           ALU.is_equal, ALU.mult)
                link(last)
                if j:
                    v.tensor_tensor(M, M, oh, ALU.add)
                    last = v.tensor_tensor(G, G, lg, ALU.add)
                    if j < TOPK - 1:
                        link(last)
            last.then_inc(S["G_ok"], 1)
            dve.wait_ge(S["cnt_ps"], 1)
            cnt = ps[0:E, 1, 0:1]
            for i in range(1, MAXBLK):
                last = v.tensor_scalar(nbc[:, i:i + 1], cnt, float(SLOT * i), None, ALU.is_gt)
            link(last)
            link(v.tensor_tensor(nbc[:, 1:2], nbc[:, 1:2], nbc[:, 2:3], ALU.add))
            v.scalar_tensor_tensor(nbc[:, 0:1], nbc[:, 1:2], 1.0, nbc[:, 3:4], ALU.add, ALU.add).then_inc(S["nb_ok"], 1)
            link(v.scalar_tensor_tensor(posm, ps[:, 1, E:3 * E].rearrange("p (t e) -> p t e", t=TH), 1.0, M,
                                        ALU.add, ALU.mult))
            v.tensor_scalar(posm, posm, -1.0, None, ALU.add).then_inc(S["pos_ok"], 1)
            dve.wait_ge(S["GT_ps"], 1)
            v.tensor_copy(GT, ps[0:E, 2, 0:SEQ]).then_inc(S["GT_sb"], 1)
            dve.wait_ge(S["end_ps"], 1)
            link(v.tensor_scalar(jt[:, 0:E], ps[0:JOBS, 3, 0:E], cst[0:JOBS, C_J:C_J + 1], None, ALU.is_le))
            link(v.tensor_tensor(jt[:, E:2 * E], jt[:, 0:E], ps[0:JOBS, 3, E:2 * E], ALU.mult))
            link(v.tensor_reduce(jt[:, 64:66], jt[:, 0:2 * E].rearrange("p (a e) -> p a e", a=2), AX.X, ALU.add))
            v.tensor_scalar(jt[:, 64:65], jt[:, 64:65], float(E - 1), None, ALU.min)
            link(v.tensor_tensor(jt[:, 65:66], cst[0:JOBS, C_J:C_J + 1], jt[:, 65:66], ALU.subtract))
            v.tensor_scalar(jt[:, 65:66], jt[:, 65:66], float(MAXBLK - 1), float(SLOT), ALU.min,
                            ALU.mult).then_inc(S["je_ok"], 1)
            dve.wait_ge(S["row_ps"], 1)
            v.tensor_copy(tab[:, 0:T_B + JOBS], ps[0:1, 4, 0:T_B + JOBS]).then_inc(S["tab_ok"], 1)
            dve.wait_ge(S["tab_ok"], 1)
            dve.wait_ge(S["pos_ok"], 1)

            def select(job):
                ex = dve.value_load(tab[0:1, bass.ds(T_E + job, 1)], min_val=0, max_val=E - 1)
                first = dve.value_load(tab[0:1, bass.ds(T_B + job, 1)], min_val=0, max_val=SEQ - SLOT)
                slots = cst[:, bass.ds(C_IOTA + first, SLOT)]
                for t in range(TH):
                    pt = posm[:, t, bass.ds(ex, 1)]
                    gt = G[:, t, bass.ds(ex, 1)]
                    v.tensor_scalar(sel[:, t, :], slots, pt, None, ALU.is_equal)
                    v.tensor_scalar(selG[:, t, :, :], slots.unsqueeze(1).to_broadcast([P, 2, SLOT]), pt, gt,
                                    ALU.is_equal, ALU.mult)
                v.tensor_copy(bsel, cst[0:3 * E, bass.ds(C_SEL3 + ex, 1)].to_broadcast([3 * E, SLOT])).then_inc(
                    S["sel_ok"], 1)

            select(0)
            dve.wait_ge(S["hb_ok"], 5)
            dve.wait_ge(S["lg_ps"], 1)
            v.memset(y_sb, 0.0).then_inc(S["y_sb"], 1)
            v.memset(selGT, 0.0).then_inc(S["selT_sb"], 1)
            total = dve.value_load(tab[0:1, T_J + E:T_J + E + 1], min_val=E, max_val=JOBS)
            with dve.Fori(0, total) as job:
                dve.wait_ge(S["gate_ps"], job + 1)
                v.tensor_scalar(gm, ps[:, 4, :], LIMIT, None, ALU.min).then_inc(S["gm_ok"], 1)
                dve.wait_ge(S["sig_ok"], job + 1)
                v.tensor_tensor(gm, gm, sg, ALU.mult)
                dve.wait_ge(used[GU_UNITS - 1], job + 1)
                v.tensor_scalar(up1, ps[:, 5, :], LIMIT, -LIMIT, ALU.min, ALU.max).then_inc(S["up_ok"], 1)
                dve.wait_ge(S["up_ok"], job + 1)
                v.scalar_tensor_tensor(act_b, up1, 1.0, gm, ALU.add, ALU.mult).then_inc(S["act_ok"], 1)
                dve.wait_ge(S["actT_ps"], job + 1)
                v.tensor_copy(actT, ps[:, 7, :]).then_inc(S["actT_sb"], 1)
                select(job + 1)

            dve.wait_ge(S["f_sq"], 1)
            v.tensor_tensor(ssq[:, 4:6], ssq[:, 0:4:2], ssq[:, 1:4:2], ALU.add).then_inc(S["f_sq"], 1)
            dve.wait_ge(S["f_rms"], 1)
            link(v.reciprocal(rstd[:, 0:2], rms[:, 0:2]))
            for t in range(TH):
                for n in range(2):
                    last = v.scalar_tensor_tensor(out_sb[:, t, n * 512:(n + 1) * 512], ps[:, 2 * t + n, :],
                                                  rstd[:, t:t + 1], bc[:, 3, n * 512:(n + 1) * 512], ALU.mult, ALU.mult)
                link(last)
                v.tensor_tensor(out_sb[:, t, :], out_sb[:, t, :], xs[:, t, :], ALU.add).then_inc(S["res_ok"], 1)


_INS = ['x', 'c', 'w_ada', 'b_ada', 'g_pre_mix', 'g_post_mix', 'g_pre_ffn', 'g_post_ffn', 'w_in', 'g_q', 'w_qb',
        'g_kv', 'w_kvb', 'rel_bias', 'w_o', 'w_router', 'b_router', 'w_gu', 'b_gu', 'w_down', 'b_down']
_OUTS = [((1, SEQ, D), 'float32')]


def kernel(**inputs):
    import numpy as _np
    import concourse.bacc as _bacc
    from concourse import mybir as _mybir
    from concourse.bass_utils import run_bass_kernel_spmd as _run

    nc = _bacc.Bacc("TRN2", target_bir_lowering=False, num_devices=1)
    arrays, args = {}, []
    for name in _INS + ['consts']:
        a = shape_constants() if name == 'consts' else _np.ascontiguousarray(inputs[name])
        arrays[f"in_{name}_dram"] = a
        args.append(nc.dram_tensor(f"in_{name}_dram", a.shape, _mybir.dt.from_np(a.dtype), kind="ExternalInput").ap())
    for i, (shape, dtype) in enumerate(_OUTS):
        dt = _mybir.dt.from_np(_np.dtype(dtype))
        args.append(nc.dram_tensor(f"out_{i}_dram", shape, dt, kind="ExternalOutput").ap())
    build(nc, *args)
    r = _run(nc, [arrays], core_ids=[0])
    got = tuple(r.results[0][f"out_{i}_dram"] for i in range(len(_OUTS)))
    return got[0]
```

```python
from contextlib import ExitStack

import numpy as np

import concourse.bass as bass
from concourse import mybir

ALU = mybir.AluOpType
ACT = mybir.ActivationFunctionType
AX = mybir.AxisListType
F32 = mybir.dt.float32
BF16 = mybir.dt.bfloat16
I32 = mybir.dt.int32
U32 = mybir.dt.uint32

P = 128
D = 1024
KC = D // P
SEQ = 256
TH = SEQ // P
CHUNK = 64
EPS = 1e-6
HEADS = 8
NOPE, ROPE, VD = 64, 32, 64
QK = NOPE + ROPE
HALF = ROPE // 2
QL, KVL = D // 4, D // 8
ZA = QL + KVL + ROPE
CAW = HEADS * 64
E = 32
F = D
TOPK = 4
LIMIT, ALPHA = 7.0, 1.702
NEG = -1e30

SLOT = 64
FEW = SLOT // 2
MAXBLK = SEQ // SLOT
JOBS = 64
UNIT = 4096
ARENA = 21300
UNITS = 6
RING = 9
TURN = 3
GU_UNITS = 4

SH1, SC1, GT1, SH2, SC2, GT2 = range(6)
GAINED = [SC1, GT1, SC2, GT2]
QW = D // 4

C_ID, C_MASK, C_IOTA, C_FEW, C_TRI, C_ROPE, C_TRIE, C_SEL3, C_J, C_EPS, C_END = np.cumsum(
    [0, P, 2 * P, SEQ, SEQ, P, 2 * 2 * HALF, E + 1, E, 1, 1]).tolist()

SC_BANK = [0, 1, 6]

GROUPS = []
for mixer in range(2):
    for b in range(TH):
        n = 4 // (b + 1)
        order = list(range(HEADS)) if mixer == 0 else [0, 2, 4, 6, 1, 3, 5, 7]
        GROUPS += [(mixer, b, order[i:i + n]) for i in range(0, HEADS, n)]


def shape_constants():
    c = np.zeros((P, C_END), np.float32)
    p = np.arange(P)
    c[:, C_ID:C_ID + P] = np.eye(P)
    c[:CHUNK, C_MASK + P + CHUNK:C_MASK + 2 * P] = NEG
    c[:, C_IOTA:C_IOTA + SEQ] = np.arange(SEQ)
    c[:, C_FEW:C_FEW + SEQ] = np.arange(SEQ) // SLOT * SLOT + np.arange(SEQ) % FEW
    c[:, C_TRI:C_TRI + P] = p[:, None] < p[None, :]
    inv = np.float32(10000.0) ** (-np.arange(HALF, dtype=np.float32) / np.float32(HALF))
    ang = np.arange(SEQ, dtype=np.float32)[:, None] * inv[None, :].astype(np.float32)
    for t in range(TH):
        a = ang[t * P:(t + 1) * P]
        c[:, C_ROPE + 2 * HALF * t:C_ROPE + 2 * HALF * (t + 1)] = np.concatenate([np.cos(a), np.sin(a)], 1)
    c[:E, C_TRIE:C_TRIE + E + 1] = np.arange(E)[:, None] < np.arange(E + 1)[None, :]
    c[:3 * E, C_SEL3:C_SEL3 + E] = np.tile(np.eye(E), (3, 1))
    c[:, C_J] = p
    c[:, C_EPS] = EPS
    return c


def build(nc, x, c, w_ada, b_ada, g_pre_mix, g_post_mix, g_pre_ffn, g_post_ffn, w_in, g_q, w_qb,
          g_kv, w_kvb, rel_bias, w_o, w_router, b_router, w_gu, b_gu, w_down, b_down, consts, out):
    ctx = ExitStack()
    with ctx:
        def sb(name, shape, dt=F32):
            return ctx.enter_context(nc.sbuf_tensor(name, shape, dt))

        def sem(name):
            return ctx.enter_context(nc.semaphore(name))

        ctx.enter_context(nc.allow_non_contiguous_dma("gain columns"))

        mem = sb("mem", [P, UNITS * UNIT + ARENA])
        ring = mem[:, 0:RING * UNIT].rearrange("p (u n) -> p u n", u=RING)
        arena = mem[:, UNITS * UNIT:]
        xs = sb("xs", [P, TH, D])
        cst = sb("cst", [P, C_END])
        mod = sb("mod", [P, 6, QW])
        gain = sb("gain", [P, 4, QW])
        silu_c = sb("silu_c", [P, KC, 32])
        b3 = sb("b3", [3 * E, 2 * F], BF16)
        small = sb("small", [P, 136])

        ident = cst[:, C_ID:C_ID + P]
        iota = cst[:, C_IOTA:C_IOTA + SEQ]
        tri = cst[:, C_TRI:C_TRI + P]
        eps = cst[:, C_EPS:C_EPS + 1]

        at = [0]

        def take(shape, dt=F32, start=None):
            n = int(np.prod(shape[1:]))
            w = n if dt != BF16 else (n + 1) // 2
            s = at[0] if start is None else start
            if start is None:
                at[0] += w
                assert at[0] <= ARENA, at[0]
            v = arena[0:shape[0], s:s + w]
            if dt != F32:
                v = v.bitcast(dt)
            if len(shape) == 3:
                v = v.rearrange("p (a b) -> p a b", a=shape[1])
            if len(shape) == 4:
                v = v.rearrange("p (a b c) -> p a b c", a=shape[1], b=shape[2])
            return v

        hT = take([P, KC, SEQ])
        base_w = at[0]
        wqb = take([P, QL // P, HEADS * QK])
        wkvb = take([P, HEADS * (NOPE + VD)])
        za = take([P, TH, ZA])
        cqT = take([P, QL // P, SEQ])
        ckvT = take([P, SEQ])
        base_q = at[0]
        q_t = take([P, TH, HEADS, QK])
        k_t = take([P, TH, HEADS, QK])
        v_a = take([P, TH, HEADS * VD])
        v_b = take([P, TH, CAW])
        base_qT = at[0]
        qT = take([QK, HEADS, SEQ])
        kT = take([QK, HEADS, SEQ])
        qcT = take([P, HEADS // 2, SEQ])
        kcT = take([P, HEADS // 2, SEQ])
        bias = take([P, HEADS, SEQ])
        xn = take([P, TH, D], start=base_q)
        s_sb = take([P, 3, 512], start=base_w)
        p_sb = take([P, 3, 512], start=base_w + 1536)
        pT = take([P, 2, 512], start=base_w + 3072)
        assert base_w + 4096 <= base_q
        o_sb = take([P, TH, D], start=base_q)
        b_gu_f = take([3 * E, 2 * F], start=base_qT)
        rope_t = take([P, 4, HEADS, HALF], start=base_qT)
        oT = hT
        bc01 = take([P, 2, D], start=KC * SEQ)
        h2 = take([P, TH, D], start=UNIT)
        h2T = take([P, KC, SEQ], start=UNIT + TH * D)
        bc2 = take([P, D], start=2 * UNIT)
        bc = [bc01[:, 0, :], bc01[:, 1, :], bc2]
        bd = mod[0:E, 0:4, :].rearrange("p v n -> p (v n)")
        wr = gain[:, 0, :].rearrange("p (k e) -> p k e", k=KC)
        GT = gain[0:E, 1, :]
        at[0] = (RING - UNITS) * UNIT
        base_hb = at[0]
        hb = take([P, TH, 3, D], BF16)
        bc_gt2 = take([P, D])
        xgT = take([P, KC * SLOT])
        gm = take([P, 512])
        sg = take([P, 512])
        base_up = at[0]
        up1 = take([P, 512])
        act_b = take([P, 512])
        actT = take([P, 512])
        y_sb = take([P, 512])
        sel = take([P, TH, SLOT], BF16)
        selG = take([P, TH, 2, SLOT])
        selGT = take([P, SEQ])
        bsel = take([3 * E, SLOT], BF16)
        M = take([P, TH, E])
        G = take([P, TH, E])
        posm = take([P, TH, E])
        brt = take([P, E])
        tab = take([1, 256], I32)
        out_sb = take([P, TH, D], start=base_hb)
        at[0] = base_up
        lg = take([P, TH, E])
        top = take([P, TH, 8])
        topi = take([P, TH, 8], U32)
        topf = take([P, TH, 8])
        gates = take([P, TH, 8])
        eq = take([P, TH, TOPK, E])
        nbc = take([E, 14])
        jt = take([JOBS, 3 * E + 6])
        assert at[0] <= base_up + 2 * 512

        T_J, T_NB, T_E, T_B = 0, E + 1, 2 * E + 1, 2 * E + 1 + JOBS

        cc, ecc, rcc = small[:, 0:8], small[:, 8:16], small[:, 16:24]
        cols = small[:, 24:40]
        gq_col, gkv_col = small[:, 40:42], small[:, 42:43]
        ssq, rms, rstd = small[:, 44:52], small[:, 52:60], small[:, 60:68]
        nmax = small[:, 68:80]
        rsum = small[:, 80:112]
        rrec = small[:, 112:120]
        nb_neg = small[:, 120:122]
        gsum = small[:, 122:124]
        ones = small[:, 128:129]

        ps = ctx.enter_context(nc.psum_tensor("ps", [P, 8, 512], F32))

        L = {n: sem("in_" + n) for n in (
            "x", "c", "cst", "bada", "gain", "gcol", "wq", "wkv", "relb", "bgu", "adaA", "adaB", "winA", "winQ", "winK",
            "winV", "gt1", "wo", "sh2", "sc2", "gt2", "wr", "bd")}
        for n in ("adaA", "adaB", "gt1", "sh2", "sc2", "gt2"):
            L[n] = (L[n], sem("in_" + n + "_end"))
        S = {n: sem(n) for n in (
            "ones_ok", "bias_mask", "c_exp", "silu", "x_sq", "x_rms", "xn_ok", "xT_ps", "ada_ps", "mod_ok", "col_ps", "col_ok",
            "hT_act", "hT_dve", "za_ps", "qc_ps", "kc_ps", "vc_ps", "qc_sb", "kc_sb", "vc_sb", "za_sb", "lat_sq", "lat_rms",
            "lat_n", "lat_ps", "lat_T", "q_ps", "kv_ps", "q_sb", "k_sb", "v_sb", "q_rot", "qk_ps", "qT_act", "qT_dve",
            "b3_ok", "sc_ps", "sc_sb", "max_ok", "exp_ok", "pT_ps", "pT_act", "pT_dve", "pv_ps", "o_ok", "oT_ps", "oT_act",
            "oT_dve", "bc_ps", "bc_sb", "wo_ps", "o_rms", "x1_ok", "x1_sq", "x1_rms", "h2_ok", "h2T_ps", "h2T_sb", "hb_ok", "hb_sub", "rows_clear",
            "lg_ps", "g_exp", "gate_ok", "M_ok", "G_ok", "cnt_ps", "nb_ok", "end_ps", "je_ok", "row_ps", "tab_ok", "pos_ok", "GT_ps",
            "GT_sb", "sum_step", "chain_v", "chain_a", "chain_p",
            "sel_ok", "selG_ok", "gath_ps", "xg_ok", "gate_ps", "up_ok", "comb_ps", "selT_ps", "selT_sb", "gm_ok", "sig_ok", "act_ok",
            "actT_ps", "actT_sb", "y_sb", "f_rms", "res_ok", "stored")}
        arrived = [sem(f"unit_arrived{u}") for u in range(RING)]
        used = [sem(f"unit_used{u}") for u in range(UNITS)]

        x_v = x[0].rearrange("(t p) d -> p t d", p=P)
        out_v = out[0].rearrange("(t p) d -> p t d", p=P)
        ada_v = w_ada[0].rearrange("(p j) n -> p j n", j=KC)
        win_v = w_in[0].rearrange("(k p) n -> p k n", p=P)
        wo_v = w_o[0].rearrange("(k p) n -> p k n", p=P)
        gu_v = w_gu[0].rearrange("e (k p) n -> e p k n", p=P)
        dn_v = w_down[0].rearrange("e (k p) n -> e p k n", p=P)

        def ada_w(u):
            return ring[:, u:u + 2, :].rearrange("p a b -> p (a b)").rearrange("p (j n) -> p j n", j=KC)

        ada_at = {SH1: 0, SC1: 2, GT1: 2, SH2: 0, SC2: 2, GT2: 0}
        ada_in = {SH1: "adaA", SC1: "adaB", GT1: "gt1", SH2: "sh2", SC2: "sc2", GT2: "gt2"}
        w_za = ring[:, 4, 0:KC * ZA].rearrange("p (k n) -> p k n", k=KC)
        w_q = ring[:, 5, :].rearrange("p (k n) -> p k n", k=KC)
        w_k = ring[:, 0, :].rearrange("p (k n) -> p k n", k=KC)
        w_v = ring[:, 1, :].rearrange("p (k n) -> p k n", k=KC)
        w_om = ring[:, 4:6, :].rearrange("p a b -> p (a b)").rearrange("p (k n) -> p k n", k=KC)

        def place(m, u):
            return (UNITS * m + u) % RING

        def arrival(turn, m, u):
            return 16 * (UNITS * TURN // RING * turn + (UNITS * m + u) // RING + 1)

        def weights(m, u):
            return ring[:, place(m, u), :].rearrange("p (k n) -> p k n", k=2 if u < GU_UNITS else 4)

        def load(sp, e, m, u):
            if u < GU_UNITS:
                src = gu_v[bass.ds(e, 1), :, 2 * u:2 * u + 2, :]
            else:
                src = dn_v[bass.ds(e, 1), :, 4 * (u - GU_UNITS):4 * (u - GU_UNITS) + 4, :]
            sp.dma_start(weights(m, u), src.rearrange("a p k n -> p (a k) n")).then_inc(arrived[place(m, u)], 16)

        block = ctx.enter_context(nc.Block())

        @block.sync
        def _(sp):
            def ada(v):
                for half in (slice(0, KC // 2), slice(KC // 2, KC)):
                    sp.dma_start(ada_w(ada_at[v])[:, half, :],
                                 ada_v[:, half, v * D:(v + 1) * D]).then_inc(L[ada_in[v]][half.start // 4], 16)

            sp.dma_start(cc, c[0].rearrange("(p j) -> p j", j=KC)).then_inc(L["c"], 16)
            sp.dma_start(xs[:, :, :], x_v).then_inc(L["x"], 16)
            ada(SH1)
            sp.dma_start(cst[:, :], consts).then_inc(L["cst"], 16)
            sp.wait_ge(S["rows_clear"], 1)
            sp.dma_start(mod[0:P:32, :, :], b_ada[0].rearrange("(v g n) -> g v n", v=6, g=4)).then_inc(L["bada"], 16)
            for i, src in enumerate((g_pre_mix, g_post_mix, g_pre_ffn, g_post_ffn)):
                sp.dma_start(gain[0:P:32, i, :], src[0].rearrange("(g n) -> g n", g=4)).then_inc(L["gain"], 16)
            ada(SC1)
            sp.dma_start(w_za, win_v[:, :, 0:ZA]).then_inc(L["winA"], 16)
            sp.dma_start(w_q, win_v[:, :, ZA:ZA + CAW]).then_inc(L["winQ"], 16)
            sp.wait_ge(S["ada_ps"], 1)
            sp.dma_start(w_k, win_v[:, :, ZA + CAW:ZA + 2 * CAW]).then_inc(L["winK"], 16)
            sp.dma_start(wqb, w_qb[0].rearrange("(k p) n -> p k n", p=P)).then_inc(L["wq"], 16)
            sp.dma_start(wkvb, w_kvb[0]).then_inc(L["wkv"], 16)
            sp.dma_start(w_v, win_v[:, :, ZA + 2 * CAW:ZA + 3 * CAW]).then_inc(L["winV"], 16)
            for i in range(3):
                sp.dma_start(b_gu_f[i * E:(i + 1) * E, :], b_gu[0]).then_inc(L["bgu"], 16)
            sp.wait_ge(S["ada_ps"], 2)
            sp.wait_ge(S["ones_ok"], 1)
            hank = bass.AP(tensor=rel_bias.tensor, offset=rel_bias.offset,
                           ap=[[1, CHUNK], [CHUNK + SEQ, HEADS], [1, SEQ]])
            sp.dma_start(bias[CHUNK:P, :, :], hank).then_inc(L["relb"], 16)
            hank = bass.AP(tensor=rel_bias.tensor, offset=rel_bias.offset,
                           ap=[[1, CHUNK], [CHUNK + SEQ, HEADS], [1, SEQ - CHUNK]])
            sp.dma_start(bias[0:CHUNK, :, CHUNK:SEQ], hank).then_inc(L["relb"], 16)
            ada(GT1)
            sp.wait_ge(S["za_ps"], 1)
            sp.wait_ge(S["qc_ps"], 1)
            sp.dma_start(w_om, wo_v).then_inc(L["wo"], 16)
            sp.wait_ge(S["kc_ps"], 1)
            sp.wait_ge(S["vc_ps"], 1)
            ada(SH2)
            sp.wait_ge(S["ada_ps"], 3)
            ada(SC2)
            sp.wait_ge(S["ada_ps"], 4)
            ada(GT2)
            sp.wait_ge(S["ada_ps"], 5)
            load(sp, 0, 0, 2)
            load(sp, 0, 0, 3)
            sp.wait_ge(S["ada_ps"], 6)
            load(sp, 0, 0, 0)
            load(sp, 0, 0, 1)
            sp.wait_ge(S["wo_ps"], 2)
            load(sp, 0, 0, 4)
            load(sp, 0, 0, 5)
            sp.wait_ge(S["h2_ok"], TH)
            load(sp, 1, 1, 0)
            load(sp, 1, 1, 2)
            sp.wait_ge(S["lg_ps"], 1)
            sp.wait_ge(S["hb_ok"], 3 * TH)
            load(sp, 1, 1, 1)
            sp.wait_ge(S["tab_ok"], 1)

            def follow(e, m):
                jobs_done = sp.value_load(tab[0:1, bass.ds(T_J + 1 + e, 1)], min_val=1, max_val=JOBS)
                for u in range(UNITS):
                    ahead, nu = divmod(u + RING, UNITS)
                    if isinstance(e, int) and e + ahead >= E:
                        break
                    sp.wait_ge(used[u], jobs_done)
                    load(sp, e + ahead, (m + ahead) % TURN, nu)

            with sp.Fori(0, E // TURN) as turn:
                for m in range(TURN):
                    follow(turn * TURN + m, m)
            follow(E // TURN * TURN, 0)
            for t in range(TH):
                sp.wait_ge(S["res_ok"], t + 1)
                sp.dma_start(out_v[:, t, :], out_sb[:, t, :]).then_inc(S["stored"], 16)
            sp.wait_ge(S["stored"], 16 * TH)

        @block.gpsimd
        def _(pool):
            chain = [0]

            def link(ins):
                chain[0] += 1
                ins.then_inc(S["chain_p"], 1)
                pool.wait_ge(S["chain_p"], chain[0])

            link(nc.gpsimd.memset(mod[:, :, :], 0.0))
            link(nc.gpsimd.memset(gain[:, :, :], 0.0))
            nc.gpsimd.memset(small[:, 131:132], 0.0).then_inc(S["rows_clear"], 1)
            pool.wait_ge(S["rows_clear"], 1)
            link(nc.gpsimd.memset(bias[0:CHUNK, :, 0:CHUNK], NEG))
            nc.gpsimd.memset(ones, 1.0).then_inc(S["ones_ok"], 1)
            pool.wait_ge(S["ones_ok"], 1)

            pool.wait_ge(L["bgu"], 48)
            r = b_gu_f
            link(nc.gpsimd.tensor_copy(b3[:, :], r))
            for first in (E, 2 * E):
                for i in range(first // E, 3):
                    rows = slice(i * E, (i + 1) * E)
                    link(nc.gpsimd.tensor_tensor(r[rows, :], r[rows, :], b3[rows, :], ALU.subtract))
                    link(nc.gpsimd.tensor_copy(b3[rows, :], r[rows, :]))
            nc.gpsimd.memset(small[:, 129:130], 0.0).then_inc(S["b3_ok"], 1)

            pool.wait_ge(S["mod_ok"], 6)
            pool.dma_start(wr, w_router[0].rearrange("(k p) n -> p k n", p=P)).then_inc(L["wr"], 16)
            pool.dma_start(brt, b_router.partition_broadcast(P)[:, 0, :]).then_inc(L["wr"], 16)
            pool.wait_ge(S["bc_ps"], 4)
            pool.dma_start(bd, b_down[0]).then_inc(L["bd"], 16)

            for t in range(TH):
                for i in range(2):
                    pool.wait_ge(S["hb_ok"], 3 * t + i + 1)
                    if i == 0:
                        pool.wait_ge(S["h2T_ps"], 2 * t + 2)
                    nc.gpsimd.tensor_tensor(h2[:, t, :], h2[:, t, :], hb[:, t, i, :],
                                            ALU.subtract).then_inc(S["hb_sub"], 1)

        @block.tensor
        def _(pe):
            mm = nc.tensor.matmul

            def transposes(blocks, dst):
                for i, (src, m) in enumerate(blocks):
                    last = nc.tensor.transpose(dst[0:m, i * P:(i + 1) * P], src, ident)
                return last

            def ada(v, bank, col, rows=range(KC)):
                w = ada_w(ada_at[v])
                for j in rows:
                    if j % 4 == 0 or j == rows[0]:
                        pe.wait_ge(L[ada_in[v]][j // 4], 16)
                    for g in range(4):
                        last = mm(ps[32 * g:32 * g + 32, bank, col:col + QW], silu_c[:, j, :],
                                  w[:, j, g * QW:(g + 1) * QW], start=(j == 0), stop=(j == KC - 1))
                if rows[-1] == KC - 1:
                    last.then_inc(S["ada_ps"], 1)

            def spread(v, bank):
                for g in range(4):
                    last = mm(ps[:, bank + g // 2, (g % 2) * QW:(g % 2 + 1) * QW],
                              ident[:, 32 * g:32 * g + 1].to_broadcast([P, P]), mod[:, v, :],
                              start=True, stop=True)
                last.then_inc(S["bc_ps"], 1)

            pe.wait_ge(L["cst"], 16)
            pe.wait_ge(S["silu"], 1)
            ada(SH1, 4, 0)
            pe.wait_ge(S["xn_ok"], 1)
            for b in range(4):
                last = transposes([(xn[:, t, (2 * b + i) * P:(2 * b + i + 1) * P], P)
                                   for i in range(2) for t in range(TH)], ps[:, b, :])
                last.then_inc(S["xT_ps"], 1)
            ada(SC1, 5, 0)
            pe.wait_ge(S["mod_ok"], 2)
            for v in (SH1, SC1):
                for k in range(KC):
                    last = mm(ps[:, 6, v * KC + k:v * KC + k + 1], mod[:, v, (k % 2) * P:(k % 2 + 1) * P],
                              ident[:, 32 * (k // 2):32 * (k // 2) + 1], start=True, stop=True)
            last.then_inc(S["col_ps"], 1)

            pe.wait_ge(S["hT_act"], 4)
            pe.wait_ge(S["hT_dve"], 4)
            pe.wait_ge(L["winA"], 16)
            for t in range(TH):
                for k in range(KC):
                    last = mm(ps[:, 6 + t, 0:ZA], hT[:, k, t * P:(t + 1) * P], w_za[:, k, :],
                              start=(k == 0), stop=(k == KC - 1))
            last.then_inc(S["za_ps"], 1)
            for name, w, bank, done in (("winQ", w_q, 0, "qc_ps"), ("winK", w_k, 2, "kc_ps")):
                pe.wait_ge(L[name], 16)
                for hp in range(HEADS // 2):
                    for k in range(KC):
                        last = mm(ps[:, bank + hp // 2, (hp % 2) * SEQ:(hp % 2 + 1) * SEQ],
                                  w[:, k, hp * P:(hp + 1) * P], hT[:, k, :], start=(k == 0), stop=(k == KC - 1))
                last.then_inc(S[done], 1)
            pe.wait_ge(S["lat_n"], 1)
            for i in range(3):
                last = transposes([(za[:, t, i * P:(i + 1) * P], P) for t in range(TH)],
                                  ps[:, 6 + i // 2, (i % 2) * SEQ:(i % 2 + 1) * SEQ])
            last.then_inc(S["lat_ps"], 1)
            pe.wait_ge(L["winV"], 16)
            for t in range(TH):
                for k in range(KC):
                    last = mm(ps[:, 4 + t, :], hT[:, k, t * P:(t + 1) * P], w_v[:, k, :],
                              start=(k == 0), stop=(k == KC - 1))
            last.then_inc(S["vc_ps"], 1)
            pe.wait_ge(S["lat_T"], 1)
            pe.wait_ge(S["qc_sb"], 1)
            pe.wait_ge(S["kc_sb"], 1)
            pe.wait_ge(L["wq"], 16)
            W2 = HEADS * QK // 2
            for t in range(TH):
                for n in range(2):
                    for k in range(QL // P):
                        last = mm(ps[:, 2 * t + n, 0:W2], cqT[:, k, t * P:(t + 1) * P],
                                  wqb[:, k, n * W2:(n + 1) * W2], start=(k == 0), stop=(k == QL // P - 1))
            last.then_inc(S["q_ps"], 1)
            pe.wait_ge(S["vc_sb"], 1)
            pe.wait_ge(L["wkv"], 16)
            for t in range(TH):
                for n in range(2):
                    last = mm(ps[:, 4 + 2 * t + n, :], ckvT[:, t * P:(t + 1) * P],
                              wkvb[:, n * 512:(n + 1) * 512], start=True, stop=True)
            last.then_inc(S["kv_ps"], 1)
            pe.wait_ge(S["q_sb"], 1)
            ada(GT1, 3, 0)
            pe.wait_ge(S["q_rot"], 1)
            pe.wait_ge(S["k_sb"], 4)
            pe.wait_ge(S["v_sb"], 1)
            for i, src in enumerate((q_t, k_t)):
                for n in range(2):
                    for t in range(TH):
                        if (i, n, t) == (0, 1, 1):
                            pe.wait_ge(S["mod_ok"], 3)
                        last = transposes([(src[:, t, 4 * n + h, :], QK) for h in range(4)],
                                          ps[:, 4 * i + 2 * n + t, :])
                        last.then_inc(S["qk_ps"], 1)

            pe.wait_ge(S["qT_act"], 4)
            pe.wait_ge(S["qT_dve"], 4)

            ada_after = {}
            for first, v, col in ((1, SH2, 0), (5, SC2, 256), (9, GT2, 0)):
                for n, rows in enumerate((range(0, 3), range(3, 6), range(6, KC))):
                    ada_after[first + n] = (v, col, rows)

            def scores(i):
                mixer, b, heads = GROUPS[i]
                K = (b + 1) * P
                if i >= 3:
                    pe.wait_ge(S["sc_sb"], i - 2)
                for n, h in enumerate(heads):
                    if mixer == 0:
                        l, r = qT[:, h, b * P:(b + 1) * P], kT[:, h, 0:K]
                    else:
                        row = 64 * (h % 2)
                        l = qcT[row:row + 64, h // 2, b * P:(b + 1) * P]
                        r = kcT[row:row + 64, h // 2, 0:K]
                    last = mm(ps[:, SC_BANK[i % 3], n * K:(n + 1) * K], l, r, start=True, stop=True)
                last.then_inc(S["sc_ps"], 1)

            for i in range(3):
                scores(i)
            def transposed(i):
                pe.wait_ge(S["exp_ok"], i + 1)
                if i >= 2:
                    pe.wait_ge(S["pT_act" if i % 2 == 0 else "pT_dve"], i // 2)
                transposes([(p_sb[:, i % 3, j * P:(j + 1) * P], P) for j in range(4)],
                           ps[:, 2 + i % 2, :]).then_inc(S["pT_ps"], 1)

            transposed(0)
            for i, (mixer, b, heads) in enumerate(GROUPS):
                if i + 3 < len(GROUPS):
                    scores(i + 3)
                if i + 1 < len(GROUPS):
                    transposed(i + 1)
                if i in ada_after:
                    v, col, rows = ada_after[i]
                    if rows[0] == 0 and v != SH2:
                        pe.wait_ge(S["mod_ok"], 4 if v == SC2 else 5)
                    ada(v, 7, col, rows)
                part = 2 * mixer + b
                if part >= 2 and i and GROUPS[i - 1][:2] != (mixer, b):
                    pe.wait_ge(S["o_ok"], part - 1)
                pe.wait_ge(S["pT_act" if i % 2 == 0 else "pT_dve"], i // 2 + 1)
                vals = v_a if mixer == 0 else v_b
                for n, h in enumerate(heads):
                    for kb in range(b + 1):
                        j = n * (b + 1) + kb
                        last = mm(ps[:, 4 + part % 2, h * VD:(h + 1) * VD], pT[:, i % 2, j * P:(j + 1) * P],
                                  vals[:, kb, h * VD:(h + 1) * VD], start=(kb == 0), stop=(kb == b))
                last.then_inc(S["pv_ps"], 1)

            pe.wait_ge(S["o_ok"], 4)
            for b in range(4):
                transposes([(o_sb[:, t, (2 * b + i) * P:(2 * b + i + 1) * P], P) for i in range(2) for t in range(TH)],
                           ps[:, b, :]).then_inc(S["oT_ps"], 1)
            pe.wait_ge(S["oT_act"], 2)
            pe.wait_ge(S["oT_dve"], 2)
            pe.wait_ge(L["wo"], 16)
            for t in range(TH):
                for n in range(2):
                    for k in range(KC):
                        last = mm(ps[:, 4 + 2 * t + n, :], oT[:, k, t * P:(t + 1) * P],
                                  w_om[:, k, n * 512:(n + 1) * 512], start=(k == 0), stop=(k == KC - 1))
                    if n == 1:
                        last.then_inc(S["wo_ps"], 1)
                    if (t, n) == (0, 0):
                        pe.wait_ge(S["mod_ok"], 6)
                        spread(GT1, 0)
                        spread(SH2, 2)
                    elif (t, n) == (0, 1):
                        pe.wait_ge(S["bc_sb"], 2)
                        spread(SC2, 0)
                        spread(GT2, 2)

            pe.wait_ge(S["bc_sb"], 4)
            pe.wait_ge(L["wr"], 32)
            for t in range(TH):
                pe.wait_ge(S["h2_ok"], t + 1)
                for b in range(2):
                    transposes([(h2[:, t, (4 * b + i) * P:(4 * b + i + 1) * P], P) for i in range(4)],
                               ps[:, 4 + 2 * t + b, :]).then_inc(S["h2T_ps"], 1)
                for k in range(KC):
                    if k % 4 == 0:
                        pe.wait_ge(S["h2T_sb"], 2 * t + k // 4 + 1)
                    last = mm(ps[:, 0, t * E:(t + 1) * E], h2T[:, k, t * P:(t + 1) * P], wr[:, k, :],
                              start=(k == 0), stop=(k == KC - 1))
            last.then_inc(S["lg_ps"], 1)

            pe.wait_ge(S["M_ok"], 1)
            for t in range(TH):
                mm(ps[0:E, 1, 0:1], M[:, t, :], ones, start=(t == 0), stop=(t == TH - 1))
            mm(ps[:, 1, E:2 * E], tri, M[:, 0, :], start=True, stop=True)
            mm(ps[:, 1, 2 * E:3 * E], tri, M[:, 1, :], start=True, stop=False)
            mm(ps[:, 1, 2 * E:3 * E], ones.to_broadcast([P, P]), M[:, 0, :], start=False,
               stop=True).then_inc(S["cnt_ps"], 1)
            pe.wait_ge(S["nb_ok"], 1)
            nb, few_neg = nbc[:, 8:9], nbc[:, 10:11]
            trie = cst[0:E, C_TRIE:C_TRIE + E + 1]
            mm(ps[0:JOBS, 3, 0:E], nb.to_broadcast([E, JOBS]), trie[:, 1:E + 1], start=True, stop=True)
            mm(ps[0:JOBS, 3, E:2 * E], nb.to_broadcast([E, JOBS]), ident[0:E, 0:E], start=True, stop=True)
            mm(ps[0:JOBS, 3, 2 * E:3 * E], nb.to_broadcast([E, JOBS]), trie[:, 1:E + 1], start=True, stop=False)
            mm(ps[0:JOBS, 3, 2 * E:3 * E], few_neg.to_broadcast([E, JOBS]), ident[0:E, 0:E], start=False,
               stop=True).then_inc(S["end_ps"], 1)
            pe.wait_ge(S["G_ok"], 1)
            for t in range(TH):
                last = nc.tensor.transpose(ps[0:E, 2, t * P:(t + 1) * P], G[:, t, :], ident)
            last.then_inc(S["GT_ps"], 1)
            pe.wait_ge(S["je_ok"], 1)
            mm(ps[0:1, 4, T_J:T_J + E + 1], nb, trie, start=True, stop=True)
            mm(ps[0:1, 4, T_NB:T_NB + E], nb, ident[0:E, 0:E], start=True, stop=True)
            mm(ps[0:1, 4, T_E:T_E + JOBS], jt[:, 3 * E:3 * E + 1], ident[0:JOBS, 0:JOBS], start=True, stop=True)
            mm(ps[0:1, 4, T_B:T_B + JOBS], jt[:, 3 * E + 4:3 * E + 5], ident[0:JOBS, 0:JOBS], start=True,
               stop=True).then_inc(S["row_ps"], 1)

            GATE, UP, Y, TR = 4, 5, 6, 7

            def gather(chunks):
                for k in chunks:
                    n = 0
                    for t in range(TH):
                        for i in range(3):
                            last = mm(ps[:, GATE, k * SLOT:(k + 1) * SLOT], hb[:, t, i, k * P:(k + 1) * P],
                                      sel[:, t, :], start=(n == 0), stop=(n == 5))
                            n += 1
                if k == KC - 1:
                    last.then_inc(S["gath_ps"], 1)

            def slots_column(job):
                return pe.value_load(tab[0:1, bass.ds(T_B + job, 1)], min_val=0, max_val=2 * SEQ - SLOT)

            def bias_down(t):
                for n in range(2):
                    mm(ps[:, 2 * t + n, :], GT[:, t * P:(t + 1) * P], bd[:, n * 512:(n + 1) * 512],
                       start=True, stop=True)

            def combine(parts, step, done=None):
                slots, width = P // parts, D // parts
                for t in (range(TH) if parts == 4 else [step]):
                    for half in range(2):
                        n = half if parts == 2 else 2 * half + step
                        col = 0 if parts == 2 else width * step
                        on = slice(slots * n, slots * n + slots)
                        last = mm(ps[:, 2 * t + half, col:col + width], selGT[on, t * P:(t + 1) * P],
                                  y_sb[on, 0:width], start=False, stop=True, skip_group_check=True)
                    if done is not None and (parts == 2 or step == 1):
                        last.then_inc(done, 1)
                return last

            def combine_before(job, step, done=None):
                if step == 0:
                    pe.wait_ge(S["y_sb"], job)
                    pe.wait_ge(S["selT_sb"], job)
                with pe.If(slots_column(job - 1) >= SEQ):
                    if step == 1:
                        pe.wait_ge(S["sum_step"], job)
                    last = combine(4, step, done)
                    if step == 0:
                        last.then_inc(S["sum_step"], 1)
                with pe.Else():
                    last = combine(2, step, done)
                    if step == 0 and done is None:
                        last.then_inc(S["sum_step"], 1)

            def add_before(job, step):
                with pe.If(job < 1):
                    bias_down(step)
                with pe.Else():
                    combine_before(job, step)

            pe.wait_ge(S["hb_ok"], 3 * TH)
            pe.wait_ge(S["b3_ok"], 1)
            pe.wait_ge(S["tab_ok"], 1)
            pe.wait_ge(S["sel_ok"], 1)
            gather(range(KC))
            pe.wait_ge(S["GT_sb"], 1)
            pe.wait_ge(L["bd"], 16)

            def work(turn, m, job, parts):
                slots, width = P // parts, F // parts
                pe.wait_ge(S["xg_ok"], job + 1)
                for bank in range(2):
                    for g in range(parts):
                        mm(ps[slots * g:slots * g + slots, GATE + bank, 0:width], bsel[:, 0:slots],
                           b3[:, bank * F + width * g:bank * F + width * g + width], start=True, stop=False)
                for u in range(GU_UNITS):
                    last_unit = u == GU_UNITS - 1
                    if last_unit:
                        add_before(job, 0)
                    pe.wait_ge(arrived[place(m, u)], arrival(turn, m, u))
                    seq = ([(bank, k) for bank in range(2) for k in range(2)] if last_unit else
                           [(bank, k) for k in range(2) for bank in range(2)])
                    for bank, k in seq:
                        kk = 2 * u + k
                        for g in range(parts):
                            last = mm(ps[slots * g:slots * g + slots, GATE + bank, 0:width],
                                      xgT[:, kk * SLOT:kk * SLOT + slots],
                                      weights(m, u)[:, k, bank * F + width * g:bank * F + width * g + width],
                                      start=False, stop=(kk == KC - 1))
                        if last_unit and (bank, k) == (0, 1):
                            last.then_inc(S["gate_ps"], 1)
                    last.then_inc(used[u], 1)
                add_before(job, 1)
                pe.wait_ge(S["selG_ok"], job + 1)
                for t in range(TH):
                    last = nc.tensor.transpose(ps[:, Y, t * P:(t + 1) * P],
                                               selG[:, t, :, :].rearrange("p a s -> p (a s)"), ident)
                last.then_inc(S["selT_ps"], 1)
                pe.wait_ge(S["sel_ok"], job + 2)
                gather(range(KC // 2))
                pe.wait_ge(S["act_ok"], job + 1)
                transposes([(act_b[:, j * P:(j + 1) * P], P) for j in range(width // P)],
                           ps[:, TR, :]).then_inc(S["actT_ps"], 1)
                gather(range(KC // 2, KC))
                pe.wait_ge(S["actT_sb"], job + 1)
                pe.wait_ge(S["selT_sb"], job + 1)
                for d in range(2):
                    pe.wait_ge(arrived[place(m, GU_UNITS + d)], arrival(turn, m, GU_UNITS + d))
                    for k in range(4):
                        g, j = divmod(4 * d + k, width // P)
                        for n in range(parts):
                            last = mm(ps[slots * n:slots * n + slots, Y, 0:width],
                                      actT[:, j * P + slots * g:j * P + slots * g + slots],
                                      weights(m, GU_UNITS + d)[:, k, width * n:width * n + width],
                                      start=(d == 0 and k == 0), stop=(d == 1 and k == 3))
                    last.then_inc(used[GU_UNITS + d], 1)

            def expert(turn, m):
                e = turn * TURN + m
                blocks = pe.value_load(tab[0:1, bass.ds(T_NB + e, 1)], min_val=1, max_val=MAXBLK)
                before = pe.value_load(tab[0:1, bass.ds(T_J + e, 1)], min_val=0, max_val=JOBS)
                with pe.Fori(0, blocks) as blk:
                    job = pe.snap(before + blk)
                    with pe.If(slots_column(job) >= SEQ):
                        work(turn, m, job, 4)
                    with pe.Else():
                        work(turn, m, job, 2)

            with pe.Fori(0, E // TURN) as turn:
                for m in range(TURN):
                    expert(turn, m)
            for m in range(E % TURN):
                expert(E // TURN, m)
            total = pe.value_load(tab[0:1, T_J + E:T_J + E + 1], min_val=E, max_val=JOBS)
            for step in range(2):
                combine_before(total, step, S["comb_ps"])

        @block.scalar
        def _(act):
            a = nc.scalar.activation
            chain = [0]

            def link(ins):
                chain[0] += 1
                ins.then_inc(S["chain_a"], 1)
                act.wait_ge(S["chain_a"], chain[0])

            act.dma_start(gq_col, g_q[0].rearrange("(k p) -> p k", p=P)).then_inc(L["gcol"], 16)
            act.dma_start(gkv_col, g_kv[0].rearrange("(k p) -> p k", p=P)).then_inc(L["gcol"], 16)

            act.wait_ge(L["c"], 16)
            a(ecc, cc, ACT.Exp, scale=-1.0).then_inc(S["c_exp"], 1)
            act.wait_ge(L["x"], 16)
            for t in range(TH):
                link(a(xn[:, t, :], xs[:, t, :], ACT.Square, accum_out=ssq[:, t:t + 1]))
            act.wait_ge(L["cst"], 16)
            a(rms[:, 0:2], ssq[:, 0:2], ACT.Sqrt, bias=eps, scale=1.0 / D).then_inc(S["x_rms"], 1)
            act.wait_ge(S["col_ok"], 1)
            act.wait_ge(S["xT_ps"], 4)
            for k in range(4, KC):
                a(hT[:, k, :], ps[:, k // 2, (k % 2) * SEQ:(k % 2 + 1) * SEQ], ACT.Identity,
                  bias=cols[:, k:k + 1], scale=cols[:, KC + k:KC + k + 1]).then_inc(S["hT_act"], 1)
            act.wait_ge(S["za_ps"], 1)
            for t in range(TH):
                last = nc.scalar.copy(za[:, t, :], ps[:, 6 + t, 0:ZA])
            link(last)
            for t in range(TH):
                a(cqT[:, t, :], za[:, t, 0:QL], ACT.Square, accum_out=ssq[:, 2 + t:3 + t])
                last = a(ckvT[:, t * P:(t + 1) * P], za[:, t, QL:QL + KVL], ACT.Square, accum_out=ssq[:, 4 + t:5 + t])
            link(last)
            a(rms[:, 2:4], ssq[:, 2:4], ACT.Sqrt, bias=eps, scale=1.0 / QL)
            a(rms[:, 4:6], ssq[:, 4:6], ACT.Sqrt, bias=eps, scale=1.0 / KVL).then_inc(S["lat_rms"], 1)
            act.wait_ge(S["qc_ps"], 1)
            for b in range(2):
                last = nc.scalar.copy(qcT[:, 2 * b:2 * b + 2, :], ps[:, b, :].rearrange("p (a s) -> p a s", a=2))
            last.then_inc(S["qc_sb"], 1)
            act.wait_ge(S["kc_ps"], 1)
            for b in range(2):
                last = nc.scalar.copy(kcT[:, 2 * b:2 * b + 2, :], ps[:, 2 + b, :].rearrange("p (a s) -> p a s", a=2))
            last.then_inc(S["kc_sb"], 1)
            act.wait_ge(S["vc_ps"], 1)
            for t in range(TH):
                last = nc.scalar.copy(v_b[:, t, :], ps[:, 4 + t, :])
            last.then_inc(S["vc_sb"], 1)
            act.wait_ge(S["q_ps"], 1)
            for t in range(TH):
                for n in range(2):
                    last = nc.scalar.copy(q_t[:, t, 4 * n:4 * n + 4, :],
                                          ps[:, 2 * t + n, 0:4 * QK].rearrange("p (h d) -> p h d", h=4))
            last.then_inc(S["q_sb"], 1)
            for t in range(TH):
                for n in range(2):
                    act.wait_ge(S["k_sb"], 2 * t + n + 1)
                    last = nc.scalar.copy(
                        v_a[:, t, 4 * n * VD:4 * (n + 1) * VD].rearrange("p (h d) -> p h d", h=4),
                        ps[:, 4 + 2 * t + n, :].rearrange("p (h d) -> p h d", h=4)[:, :, NOPE:])
            last.then_inc(S["v_sb"], 1)
            for i in range(4):
                act.wait_ge(S["qk_ps"], 5 + i)
                n, t = i // 2, i % 2
                nc.scalar.copy(kT[:, 4 * n:4 * n + 4, t * P:(t + 1) * P],
                               ps[0:QK, 4 + i, :].rearrange("p (h s) -> p h s", h=4)).then_inc(S["qT_act"], 1)

            def exps(i):
                mixer, b, heads = GROUPS[i]
                K = (b + 1) * P
                act.wait_ge(S["max_ok"], i + 1)
                if i >= 3:
                    act.wait_ge(S["pT_ps"], i - 2)
                for n, h in enumerate(heads):
                    r = (2 * mixer + b) * HEADS + h
                    last = a(p_sb[:, i % 3, n * K:(n + 1) * K], s_sb[:, i % 3, n * K:(n + 1) * K], ACT.Exp,
                             bias=nmax[:, 4 * (i % 3) + n:4 * (i % 3) + n + 1], accum_out=rsum[:, r:r + 1])
                last.then_inc(S["exp_ok"], 1)

            exps(0)
            for i in range(len(GROUPS)):
                if i + 1 < len(GROUPS):
                    exps(i + 1)
                if i % 2 == 0:
                    act.wait_ge(S["pT_ps"], i + 1)
                    if i >= 2:
                        act.wait_ge(S["pv_ps"], i - 1)
                    nc.scalar.copy(pT[:, 0, :], ps[:, 2, :]).then_inc(S["pT_act"], 1)
            for b in range(2):
                act.wait_ge(S["oT_ps"], b + 1)
                nc.scalar.copy(oT[:, 2 * b:2 * b + 2, :], ps[:, b, :].rearrange("p (a s) -> p a s", a=2)).then_inc(S["oT_act"], 1)
            act.wait_ge(S["oT_ps"], 4)
            def row(i):
                act.wait_ge(S["bc_ps"], i + 1)
                b, dst = 2 * (i % 2), bc[i] if i < 3 else bc_gt2
                nc.scalar.copy(dst.rearrange("p (n c) -> p n c", n=2), ps[:, b:b + 2, :]).then_inc(S["bc_sb"], 1)

            row(0)
            row(1)
            for t in range(TH):
                act.wait_ge(S["wo_ps"], t + 1)
                link(a(h2[:, t, :].rearrange("p (n c) -> p n c", n=2), ps[:, 4 + 2 * t:6 + 2 * t, :], ACT.Square,
                       accum_out=ssq[:, t:t + 1]))
                a(rms[:, t:t + 1], ssq[:, t:t + 1], ACT.Sqrt, bias=eps, scale=1.0 / D).then_inc(S["o_rms"], 1)
                if t == 0:
                    row(2)
                act.wait_ge(S["x1_ok"], t + 1)
                link(a(h2[:, t, :], xs[:, t, :], ACT.Square, accum_out=ssq[:, 2 + t:3 + t]))
                a(rms[:, 2 + t:3 + t], ssq[:, 2 + t:3 + t], ACT.Sqrt, bias=eps, scale=1.0 / D).then_inc(S["x1_rms"], 1)
                if t == 0:
                    row(3)
                    act.wait_ge(S["h2_ok"], 1)
                    nc.scalar.copy(hb[:, 0, 0, :], h2[:, 0, :]).then_inc(S["hb_ok"], 1)
            for t in range(TH):
                for b in range(2):
                    act.wait_ge(S["h2T_ps"], 2 * t + b + 1)
                    nc.scalar.copy(h2T[:, 4 * b:4 * b + 4, t * P:(t + 1) * P],
                                   ps[:, 4 + 2 * t + b, :].rearrange("p (k s) -> p k s", k=4)).then_inc(S["h2T_sb"], 1)
            for i in range(1, 3):
                act.wait_ge(S["hb_sub"], i)
                nc.scalar.copy(hb[:, 0, i, :], h2[:, 0, :]).then_inc(S["hb_ok"], 1)
            act.wait_ge(S["gate_ok"], 1)
            for t in range(TH):
                last = a(gates[:, t, 0:TOPK], top[:, t, 0:TOPK], ACT.Exp, bias=nb_neg[:, t:t + 1],
                         accum_out=gsum[:, t:t + 1])
            last.then_inc(S["g_exp"], 1)
            nc.scalar.copy(hb[:, 1, 0, :], h2[:, 1, :]).then_inc(S["hb_ok"], 1)
            for i in range(1, 3):
                act.wait_ge(S["hb_sub"], 2 + i)
                nc.scalar.copy(hb[:, 1, i, :], h2[:, 1, :]).then_inc(S["hb_ok"], 1)

            act.wait_ge(S["tab_ok"], 1)
            act.wait_ge(S["gath_ps"], 1)
            nc.scalar.copy(xgT, ps[:, 4, :]).then_inc(S["xg_ok"], 1)
            total = act.value_load(tab[0:1, T_J + E:T_J + E + 1], min_val=E, max_val=JOBS)
            with act.Fori(0, total) as job:
                act.wait_ge(S["gm_ok"], job + 1)
                a(sg, gm, ACT.Sigmoid, scale=ALPHA).then_inc(S["sig_ok"], 1)
                act.wait_ge(S["selT_ps"], job + 1)
                nc.scalar.copy(selGT, ps[:, 6, 0:SEQ]).then_inc(S["selT_sb"], 1)
                act.wait_ge(S["gath_ps"], job + 2)
                nc.scalar.copy(xgT, ps[:, 4, :]).then_inc(S["xg_ok"], 1)
                act.wait_ge(used[UNITS - 1], job + 1)
                nc.scalar.copy(y_sb, ps[:, 6, :]).then_inc(S["y_sb"], 1)

            for t in range(TH):
                act.wait_ge(S["comb_ps"], t + 1)
                link(a(ring[:, 0, t * D:(t + 1) * D].rearrange("p (n c) -> p n c", n=2), ps[:, 2 * t:2 * t + 2, :],
                       ACT.Square, accum_out=ssq[:, t:t + 1]))
                a(rms[:, t:t + 1], ssq[:, t:t + 1], ACT.Sqrt, bias=eps, scale=1.0 / D).then_inc(S["f_rms"], 1)

        @block.vector
        def _(dve):
            v = nc.vector
            chain = [0]

            def link(ins):
                chain[0] += 1
                ins.then_inc(S["chain_v"], 1)
                dve.wait_ge(S["chain_v"], chain[0])

            dve.wait_ge(S["c_exp"], 1)
            link(v.tensor_scalar(ecc, ecc, 1.0, None, ALU.add))
            link(v.reciprocal(rcc, ecc))
            link(v.tensor_tensor(rcc, rcc, cc, ALU.mult))
            v.tensor_copy(silu_c[:, :, :], rcc.unsqueeze(2).to_broadcast([P, KC, 32])).then_inc(S["silu"], 1)
            dve.wait_ge(S["x_rms"], 1)
            link(v.reciprocal(rstd[:, 0:2], rms[:, 0:2]))
            for t in range(TH):
                last = v.tensor_scalar(xn[:, t, :], xs[:, t, :], rstd[:, t:t + 1], None, ALU.mult)
            last.then_inc(S["xn_ok"], 1)

            def mod_row(i, vec, bank, col):
                dve.wait_ge(S["ada_ps"], i + 1)
                if i == 0:
                    dve.wait_ge(L["bada"], 16)
                    dve.wait_ge(L["gain"], 64)
                first = v.tensor_tensor(mod[:, vec, :], ps[:, bank, col:col + QW], mod[:, vec, :], ALU.add)
                if vec in GAINED:
                    link(first)
                    plus = 1.0 if vec in (SC1, SC2) else 0.0
                    first = v.scalar_tensor_tensor(mod[:, vec, :], mod[:, vec, :], plus,
                                                   gain[:, GAINED.index(vec), :], ALU.add, ALU.mult)
                first.then_inc(S["mod_ok"], 1)

            mod_row(0, SH1, 4, 0)
            mod_row(1, SC1, 5, 0)
            dve.wait_ge(S["col_ps"], 1)
            v.tensor_copy(cols, ps[:, 6, 0:2 * KC]).then_inc(S["col_ok"], 1)
            dve.wait_ge(S["col_ok"], 1)
            dve.wait_ge(S["xT_ps"], 4)
            for k in range(4):
                v.tensor_scalar(hT[:, k, :], ps[:, k // 2, (k % 2) * SEQ:(k % 2 + 1) * SEQ],
                                cols[:, KC + k:KC + k + 1], cols[:, k:k + 1], ALU.mult, ALU.add).then_inc(S["hT_dve"], 1)
            dve.wait_ge(S["lat_rms"], 1)
            link(v.reciprocal(rstd[:, 2:6], rms[:, 2:6]))
            for t in range(TH):
                v.tensor_scalar(za[:, t, 0:QL], za[:, t, 0:QL], rstd[:, 2 + t:3 + t], None, ALU.mult)
                last = v.tensor_scalar(za[:, t, QL:QL + KVL], za[:, t, QL:QL + KVL], rstd[:, 4 + t:5 + t], None, ALU.mult)
            last.then_inc(S["lat_n"], 1)
            dve.wait_ge(S["lat_ps"], 1)
            dve.wait_ge(L["gcol"], 32)
            for k in range(2):
                v.tensor_scalar(cqT[:, k, :], ps[:, 6, k * SEQ:(k + 1) * SEQ], gq_col[:, k:k + 1], None, ALU.mult)
            v.tensor_scalar(ckvT, ps[:, 7, 0:SEQ], gkv_col, None, ALU.mult).then_inc(S["lat_T"], 1)

            def rotate(x1, x2, shape, t, tmp):
                cs = cst[:, C_ROPE + 2 * HALF * t:C_ROPE + 2 * HALF * t + HALF]
                sn = cst[:, C_ROPE + 2 * HALF * t + HALF:C_ROPE + 2 * HALF * (t + 1)]
                if len(shape) == 3:
                    cs, sn = cs.unsqueeze(1).to_broadcast(shape), sn.unsqueeze(1).to_broadcast(shape)
                v.tensor_tensor(tmp[0], x1, cs, ALU.mult)
                v.tensor_tensor(tmp[1], x2, sn, ALU.mult)
                v.tensor_tensor(tmp[2], x2, cs, ALU.mult)
                link(v.tensor_tensor(tmp[3], x1, sn, ALU.mult))
                v.tensor_tensor(x1, tmp[0], tmp[1], ALU.subtract)
                return v.tensor_tensor(x2, tmp[2], tmp[3], ALU.add)

            dve.wait_ge(S["b3_ok"], 1)
            for t in range(TH):
                kr = za[:, t, QL + KVL:ZA]
                link(rotate(kr[:, 0:HALF], kr[:, HALF:ROPE], [P, HALF], t, [rope_t[:, i, 0, :] for i in range(4)]))
            dve.wait_ge(S["q_sb"], 1)
            for t in range(TH):
                last = rotate(q_t[:, t, :, NOPE:NOPE + HALF], q_t[:, t, :, NOPE + HALF:QK], [P, HEADS, HALF], t,
                              [rope_t[:, i] for i in range(4)])
                if t == 0:
                    link(last)
            last.then_inc(S["q_rot"], 1)
            dve.wait_ge(S["kv_ps"], 1)
            for t in range(TH):
                v.tensor_copy(k_t[:, t, :, NOPE:QK],
                              za[:, t, QL + KVL:ZA].unsqueeze(1).to_broadcast([P, HEADS, ROPE]))
                for n in range(2):
                    v.tensor_copy(k_t[:, t, 4 * n:4 * n + 4, 0:NOPE],
                                  ps[:, 4 + 2 * t + n, :].rearrange("p (h d) -> p h d", h=4)[:, :, 0:NOPE]).then_inc(
                                      S["k_sb"], 1)
            mod_row(2, GT1, 3, 0)
            for i in range(4):
                dve.wait_ge(S["qk_ps"], 1 + i)
                if i == 0:
                    dve.wait_ge(S["q_rot"], 1)
                n, t = i // 2, i % 2
                v.tensor_copy(qT[:, 4 * n:4 * n + 4, t * P:(t + 1) * P],
                              ps[0:QK, i, :].rearrange("p (h s) -> p h s", h=4)).then_inc(S["qT_dve"], 1)

            def soften(i):
                mixer, b, heads = GROUPS[i]
                K, n = (b + 1) * P, len(heads)
                if i == 0:
                    dve.wait_ge(L["relb"], 32)
                dve.wait_ge(S["sc_ps"], i + 1)
                if i >= 3:
                    dve.wait_ge(S["exp_ok"], i - 2)
                if mixer == 0:
                    add = cst[:, C_MASK + (1 - b) * P:C_MASK + 2 * P].unsqueeze(1).to_broadcast([P, n, K])
                    scale = QK ** -0.5
                else:
                    step = heads[1] - heads[0]
                    add = bias[:, heads[0]:heads[-1] + 1:step, K - 1::-1]
                    scale = 64 ** -0.5
                s3 = s_sb[:, i % 3, :].rearrange("p (n k) -> p n k", n=n)
                v.scalar_tensor_tensor(s3, ps[:, SC_BANK[i % 3], :].rearrange("p (n k) -> p n k", n=n), scale, add,
                                       ALU.mult, ALU.add).then_inc(S["sc_sb"], 1)
                dve.wait_ge(S["sc_sb"], i + 1)
                v.tensor_reduce(nmax[:, 4 * (i % 3):4 * (i % 3) + n], s3, AX.X, ALU.max,
                                negate=True).then_inc(S["max_ok"], 1)

            for i in range(3):
                soften(i)
            for i, (mixer, b, heads) in enumerate(GROUPS):
                if i % 2 == 1:
                    dve.wait_ge(S["pT_ps"], i + 1)
                    if i >= 2:
                        dve.wait_ge(S["pv_ps"], i - 1)
                    v.tensor_copy(pT[:, 1, :], ps[:, 3, :]).then_inc(S["pT_dve"], 1)
                if i + 3 < len(GROUPS):
                    soften(i + 3)
                for after, n, v2, col in ((4, 3, SH2, 0), (8, 4, SC2, 256)):
                    if i == after:
                        mod_row(n, v2, 7, col)
                if i + 1 == len(GROUPS) or GROUPS[i + 1][:2] != (mixer, b):
                    part = 2 * mixer + b
                    dve.wait_ge(S["exp_ok"], i + 1)
                    link(v.reciprocal(rrec, rsum[:, part * HEADS:(part + 1) * HEADS]))
                    dve.wait_ge(S["pv_ps"], i + 1)
                    v.tensor_tensor(o_sb[:, b, mixer * 512:(mixer + 1) * 512].rearrange("p (h d) -> p h d", h=HEADS),
                                    ps[:, 4 + part % 2, :].rearrange("p (h d) -> p h d", h=HEADS),
                                    rrec.unsqueeze(2).to_broadcast([P, HEADS, VD]), ALU.mult).then_inc(S["o_ok"], 1)
            mod_row(5, GT2, 7, 0)
            for b in range(2):
                dve.wait_ge(S["oT_ps"], b + 3)
                v.tensor_copy(oT[:, 4 + 2 * b:6 + 2 * b, :],
                              ps[:, 2 + b, :].rearrange("p (a s) -> p a s", a=2)).then_inc(S["oT_dve"], 1)

            for t in range(TH):
                dve.wait_ge(S["o_rms"], t + 1)
                link(v.reciprocal(rstd[:, t:t + 1], rms[:, t:t + 1]))
                dve.wait_ge(S["bc_sb"], 1)
                link(v.scalar_tensor_tensor(h2[:, t, :].rearrange("p (n c) -> p n c", n=2), ps[:, 4 + 2 * t:6 + 2 * t, :],
                                            rstd[:, t:t + 1], bc[0].rearrange("p (n c) -> p n c", n=2),
                                            ALU.mult, ALU.mult))
                v.tensor_tensor(xs[:, t, :], xs[:, t, :], h2[:, t, :], ALU.add).then_inc(S["x1_ok"], 1)
                dve.wait_ge(S["x1_rms"], t + 1)
                link(v.reciprocal(rstd[:, 2 + t:3 + t], rms[:, 2 + t:3 + t]))
                dve.wait_ge(S["bc_sb"], 3)
                link(v.scalar_tensor_tensor(h2[:, t, :], xs[:, t, :], rstd[:, 2 + t:3 + t], bc[2],
                                            ALU.mult, ALU.mult))
                v.tensor_tensor(h2[:, t, :], h2[:, t, :], bc[1], ALU.add).then_inc(S["h2_ok"], 1)

            dve.wait_ge(S["lg_ps"], 1)
            dve.wait_ge(L["wr"], 32)
            link(v.tensor_tensor(lg, ps[:, 0, 0:TH * E].rearrange("p (t e) -> p t e", t=TH),
                                 brt.unsqueeze(1).to_broadcast([P, TH, E]), ALU.add))
            for t in range(TH):
                last = v.max(top[:, t, :], lg[:, t, :])
            link(last)
            v.tensor_scalar(nb_neg, top[:, :, 0], -1.0, None, ALU.mult).then_inc(S["gate_ok"], 1)
            for t in range(TH):
                last = v.max_index(topi[:, t, :], top[:, t, :], lg[:, t, :])
            link(last)
            link(v.tensor_copy(topf, topi))
            four = [P, TH, TOPK, E]
            link(v.tensor_tensor(eq, iota[:, 0:E].unsqueeze(1).unsqueeze(1).to_broadcast(four),
                                 topf[:, :, 0:TOPK].unsqueeze(3).to_broadcast(four), ALU.is_equal))
            v.tensor_reduce(M, eq.rearrange("p t j e -> p t e j"), AX.X, ALU.add).then_inc(S["M_ok"], 1)
            dve.wait_ge(S["g_exp"], 1)
            link(v.reciprocal(gsum, gsum))
            for t in range(TH):
                last = v.tensor_scalar(gates[:, t, 0:TOPK], gates[:, t, 0:TOPK], gsum[:, t:t + 1], None, ALU.mult)
            link(last)
            link(v.tensor_tensor(eq, eq, gates[:, :, 0:TOPK].unsqueeze(3).to_broadcast(four), ALU.mult))
            v.tensor_reduce(G, eq.rearrange("p t j e -> p t e j"), AX.X, ALU.add).then_inc(S["G_ok"], 1)
            dve.wait_ge(S["cnt_ps"], 1)
            link(v.tensor_copy(nbc[:, 12:13], ps[0:E, 1, 0:1]))
            link(v.tensor_scalar(nbc[:, 0:8], iota[0:E, 0:SEQ:FEW], nbc[:, 12:13], None, ALU.is_lt))
            link(v.tensor_reduce(nbc[:, 8:10], nbc[:, 0:8].rearrange("p (b a) -> p a b", a=2), AX.X, ALU.add))
            link(v.tensor_scalar(nbc[:, 8:9], nbc[:, 8:9], 1.0, None, ALU.max))
            v.tensor_tensor(nbc[:, 10:11], nbc[:, 9:10], nbc[:, 8:9], ALU.subtract).then_inc(S["nb_ok"], 1)
            link(v.scalar_tensor_tensor(posm, ps[:, 1, E:3 * E].rearrange("p (t e) -> p t e", t=TH), 1.0, M,
                                        ALU.add, ALU.mult))
            v.tensor_scalar(posm, posm, -1.0, None, ALU.add).then_inc(S["pos_ok"], 1)
            dve.wait_ge(S["end_ps"], 1)
            j_col = cst[0:JOBS, C_J:C_J + 1]
            j_ex, j_blk, j_few, j_out = (jt[:, 3 * E + i:3 * E + i + 1] for i in (0, 1, 2, 4))
            v.tensor_scalar(jt[:, 2 * E:3 * E], ps[0:JOBS, 3, 2 * E:3 * E], j_col, None, ALU.is_le)
            link(v.tensor_scalar(jt[:, 0:E], ps[0:JOBS, 3, 0:E], j_col, None, ALU.is_le))
            link(v.tensor_tensor(jt[:, E:2 * E], jt[:, 0:E], ps[0:JOBS, 3, E:2 * E], ALU.mult))
            link(v.tensor_reduce(jt[:, 3 * E:3 * E + 3], jt[:, 0:3 * E].rearrange("p (a e) -> p a e", a=3), AX.X,
                                 ALU.add))
            v.tensor_tensor(j_few, j_few, j_ex, ALU.subtract)
            link(v.tensor_tensor(j_blk, j_col, j_blk, ALU.subtract))
            v.tensor_scalar(j_ex, j_ex, float(E - 1), None, ALU.min)
            link(v.tensor_scalar(j_blk, j_blk, float(MAXBLK - 1), float(SLOT), ALU.min, ALU.mult))
            v.scalar_tensor_tensor(j_out, j_few, float(SEQ), j_blk, ALU.mult, ALU.add).then_inc(S["je_ok"], 1)
            dve.wait_ge(S["row_ps"], 1)
            v.tensor_copy(tab[:, 0:T_B + JOBS], ps[0:1, 4, 0:T_B + JOBS]).then_inc(S["tab_ok"], 1)
            dve.wait_ge(S["tab_ok"], 1)
            dve.wait_ge(S["pos_ok"], 1)

            def expert_and_slots(job):
                ex = dve.value_load(tab[0:1, bass.ds(T_E + job, 1)], min_val=0, max_val=E - 1)
                first = dve.value_load(tab[0:1, bass.ds(T_B + job, 1)], min_val=0, max_val=2 * SEQ - SLOT)
                return ex, cst[:, bass.ds(C_IOTA + first, SLOT)]

            def select_tokens(ex, slots):
                v.tensor_copy(bsel, cst[0:3 * E, bass.ds(C_SEL3 + ex, 1)].to_broadcast([3 * E, SLOT]))
                for t in range(TH):
                    last = v.tensor_scalar(sel[:, t, :], slots, posm[:, t, bass.ds(ex, 1)], None, ALU.is_equal)
                last.then_inc(S["sel_ok"], 1)

            def select_gates(ex, slots):
                for t in range(TH):
                    last = v.tensor_scalar(selG[:, t, :, :], slots.unsqueeze(1).to_broadcast([P, 2, SLOT]),
                                           posm[:, t, bass.ds(ex, 1)], G[:, t, bass.ds(ex, 1)], ALU.is_equal, ALU.mult)
                last.then_inc(S["selG_ok"], 1)

            ex, slots = expert_and_slots(0)
            select_tokens(ex, slots)
            dve.wait_ge(S["GT_ps"], 1)
            v.tensor_copy(GT, ps[0:E, 2, 0:SEQ]).then_inc(S["GT_sb"], 1)
            select_gates(ex, slots)
            total = dve.value_load(tab[0:1, T_J + E:T_J + E + 1], min_val=E, max_val=JOBS)
            with dve.Fori(0, total) as job:
                ex, slots = expert_and_slots(job + 1)
                dve.wait_ge(S["gate_ps"], job + 1)
                v.tensor_scalar(gm, ps[:, 4, :], LIMIT, None, ALU.min).then_inc(S["gm_ok"], 1)
                select_tokens(ex, slots)
                dve.wait_ge(S["sig_ok"], job + 1)
                v.tensor_tensor(gm, gm, sg, ALU.mult)
                dve.wait_ge(used[GU_UNITS - 1], job + 1)
                v.tensor_scalar(up1, ps[:, 5, :], LIMIT, -LIMIT, ALU.min, ALU.max).then_inc(S["up_ok"], 1)
                dve.wait_ge(S["up_ok"], job + 1)
                v.scalar_tensor_tensor(act_b, up1, 1.0, gm, ALU.add, ALU.mult).then_inc(S["act_ok"], 1)
                dve.wait_ge(S["actT_ps"], job + 1)
                v.tensor_copy(actT, ps[:, 7, :]).then_inc(S["actT_sb"], 1)
                select_gates(ex, slots)

            for t in range(TH):
                dve.wait_ge(S["f_rms"], t + 1)
                link(v.reciprocal(rstd[:, t:t + 1], rms[:, t:t + 1]))
                link(v.scalar_tensor_tensor(out_sb[:, t, :].rearrange("p (n c) -> p n c", n=2),
                                            ps[:, 2 * t:2 * t + 2, :], rstd[:, t:t + 1],
                                            bc_gt2.rearrange("p (n c) -> p n c", n=2), ALU.mult, ALU.mult))
                v.tensor_tensor(out_sb[:, t, :], out_sb[:, t, :], xs[:, t, :], ALU.add).then_inc(S["res_ok"], 1)


_INS = ['x', 'c', 'w_ada', 'b_ada', 'g_pre_mix', 'g_post_mix', 'g_pre_ffn', 'g_post_ffn', 'w_in', 'g_q', 'w_qb',
        'g_kv', 'w_kvb', 'rel_bias', 'w_o', 'w_router', 'b_router', 'w_gu', 'b_gu', 'w_down', 'b_down']
_OUTS = [((1, SEQ, D), 'float32')]


def kernel(**inputs):
    import numpy as _np
    import concourse.bacc as _bacc
    from concourse import mybir as _mybir
    from concourse.bass_utils import run_bass_kernel_spmd as _run

    nc = _bacc.Bacc("TRN2", target_bir_lowering=False, num_devices=1)
    arrays, args = {}, []
    for name in _INS + ['consts']:
        a = shape_constants() if name == 'consts' else _np.ascontiguousarray(inputs[name])
        arrays[f"in_{name}_dram"] = a
        args.append(nc.dram_tensor(f"in_{name}_dram", a.shape, _mybir.dt.from_np(a.dtype), kind="ExternalInput").ap())
    for i, (shape, dtype) in enumerate(_OUTS):
        dt = _mybir.dt.from_np(_np.dtype(dtype))
        args.append(nc.dram_tensor(f"out_{i}_dram", shape, dt, kind="ExternalOutput").ap())
    build(nc, *args)
    r = _run(nc, [arrays], core_ids=[0])
    got = tuple(r.results[0][f"out_{i}_dram"] for i in range(len(_OUTS)))
    return got[0]
```

```python
from contextlib import ExitStack

import numpy as np

import concourse.bass as bass
from concourse import mybir

ALU = mybir.AluOpType
ACT = mybir.ActivationFunctionType
AX = mybir.AxisListType
F32 = mybir.dt.float32
BF16 = mybir.dt.bfloat16
I32 = mybir.dt.int32
U32 = mybir.dt.uint32

P = 128
D = 1024
KC = D // P
SEQ = 256
TH = SEQ // P
CHUNK = 64
EPS = 1e-6
HEADS = 8
NOPE, ROPE, VD = 64, 32, 64
QK = NOPE + ROPE
HALF = ROPE // 2
QL, KVL = D // 4, D // 8
ZA = QL + KVL + ROPE
CAW = HEADS * 64
E = 32
F = D
TOPK = 4
LIMIT, ALPHA = 7.0, 1.702
NEG = -1e30

SLOT = 64
FEW = SLOT // 2
MAXBLK = SEQ // SLOT
JOBS = 64
UNIT = 4096
ARENA = 21300
UNITS = 6
RING = 9
TURN = 3
GU_UNITS = 4

SH1, SC1, GT1, SH2, SC2, GT2 = range(6)
SPREAD = [GT1, SH2, SC2, GT2]
GAINED = [SC1, GT1, SC2, GT2]
QW = D // 4

C_ID, C_MASK, C_IOTA, C_FEW, C_TRI, C_ROPE, C_TRIE, C_SEL3, C_J, C_EPS, C_END = np.cumsum(
    [0, P, 2 * P, SEQ, SEQ, P, 2 * 2 * HALF, E + 1, E, 1, 1]).tolist()

SC_BANK = [0, 1, 6]

GROUPS = []
for mixer in range(2):
    for b in range(TH):
        n = 4 // (b + 1)
        order = list(range(HEADS)) if mixer == 0 else [0, 2, 4, 6, 1, 3, 5, 7]
        GROUPS += [(mixer, b, order[i:i + n]) for i in range(0, HEADS, n)]


def shape_constants():
    c = np.zeros((P, C_END), np.float32)
    p = np.arange(P)
    c[:, C_ID:C_ID + P] = np.eye(P)
    c[:CHUNK, C_MASK + P + CHUNK:C_MASK + 2 * P] = NEG
    c[:, C_IOTA:C_IOTA + SEQ] = np.arange(SEQ)
    c[:, C_FEW:C_FEW + SEQ] = np.arange(SEQ) // SLOT * SLOT + np.arange(SEQ) % FEW
    c[:, C_TRI:C_TRI + P] = p[:, None] < p[None, :]
    inv = np.float32(10000.0) ** (-np.arange(HALF, dtype=np.float32) / np.float32(HALF))
    ang = np.arange(SEQ, dtype=np.float32)[:, None] * inv[None, :].astype(np.float32)
    for t in range(TH):
        a = ang[t * P:(t + 1) * P]
        c[:, C_ROPE + 2 * HALF * t:C_ROPE + 2 * HALF * (t + 1)] = np.concatenate([np.cos(a), np.sin(a)], 1)
    c[:E, C_TRIE:C_TRIE + E + 1] = np.arange(E)[:, None] < np.arange(E + 1)[None, :]
    c[:3 * E, C_SEL3:C_SEL3 + E] = np.tile(np.eye(E), (3, 1))
    c[:, C_J] = p
    c[:, C_EPS] = EPS
    return c


def build(nc, x, c, w_ada, b_ada, g_pre_mix, g_post_mix, g_pre_ffn, g_post_ffn, w_in, g_q, w_qb,
          g_kv, w_kvb, rel_bias, w_o, w_router, b_router, w_gu, b_gu, w_down, b_down, consts, out):
    ctx = ExitStack()
    with ctx:
        def sb(name, shape, dt=F32):
            return ctx.enter_context(nc.sbuf_tensor(name, shape, dt))

        def sem(name):
            return ctx.enter_context(nc.semaphore(name))

        ctx.enter_context(nc.allow_non_contiguous_dma("gain columns"))

        mem = sb("mem", [P, UNITS * UNIT + ARENA])
        ring = mem[:, 0:RING * UNIT].rearrange("p (u n) -> p u n", u=RING)
        arena = mem[:, UNITS * UNIT:]
        xs = sb("xs", [P, TH, D])
        cst = sb("cst", [P, C_END])
        mod = sb("mod", [P, 6, QW])
        gain = sb("gain", [P, 4, QW])
        silu_c = sb("silu_c", [P, KC, 32])
        b3 = sb("b3", [3 * E, 2 * F], BF16)
        small = sb("small", [P, 136])

        ident = cst[:, C_ID:C_ID + P]
        iota = cst[:, C_IOTA:C_IOTA + SEQ]
        tri = cst[:, C_TRI:C_TRI + P]
        eps = cst[:, C_EPS:C_EPS + 1]

        at = [0]

        def take(shape, dt=F32, start=None):
            n = int(np.prod(shape[1:]))
            w = n if dt != BF16 else (n + 1) // 2
            s = at[0] if start is None else start
            if start is None:
                at[0] += w
                assert at[0] <= ARENA, at[0]
            v = arena[0:shape[0], s:s + w]
            if dt != F32:
                v = v.bitcast(dt)
            if len(shape) == 3:
                v = v.rearrange("p (a b) -> p a b", a=shape[1])
            if len(shape) == 4:
                v = v.rearrange("p (a b c) -> p a b c", a=shape[1], b=shape[2])
            return v

        hT = take([P, KC, SEQ])
        base_w = at[0]
        wqb = take([P, QL // P, HEADS * QK])
        wkvb = take([P, HEADS * (NOPE + VD)])
        za = take([P, TH, ZA])
        cqT = take([P, QL // P, SEQ])
        ckvT = take([P, SEQ])
        base_q = at[0]
        q_t = take([P, TH, HEADS, QK])
        k_t = take([P, TH, HEADS, QK])
        v_a = take([P, TH, HEADS * VD])
        v_b = take([P, TH, CAW])
        base_qT = at[0]
        qT = take([QK, HEADS, SEQ])
        kT = take([QK, HEADS, SEQ])
        qcT = take([P, HEADS // 2, SEQ])
        kcT = take([P, HEADS // 2, SEQ])
        bias = take([P, HEADS, SEQ])
        rope_t = take([P, 4, HEADS, HALF])
        xn = take([P, TH, D], start=base_q)
        s_sb = take([P, 3, 512], start=base_w)
        p_sb = take([P, 3, 512], start=base_w + 1536)
        pT = take([P, 2, 512], start=base_w + 3072)
        assert base_w + 4096 <= base_q
        o_sb = take([P, TH, D], start=base_q)
        b_gu_f = take([3 * E, 2 * F], start=base_qT)
        oT = hT
        bc01 = take([P, 2, D], start=KC * SEQ)
        h2 = take([P, TH, D], start=UNIT)
        h2T = take([P, KC, SEQ], start=UNIT + TH * D)
        bc2 = take([P, D], start=2 * UNIT)
        bd = mod[0:E, 0:4, :].rearrange("p v n -> p (v n)")
        wr = gain[:, 0, :].rearrange("p (k e) -> p k e", k=KC)
        GT = gain[0:E, 1, :]
        at[0] = (RING - UNITS) * UNIT
        base_hb = at[0]
        hb = take([P, TH, 3, D], BF16)
        bc_gt2 = take([P, D])
        bc = {GT1: bc01[:, 0, :], SH2: bc01[:, 1, :], SC2: bc2, GT2: bc_gt2}
        xgT = take([P, KC * SLOT])
        gm = take([P, 512])
        sg = take([P, 512])
        base_up = at[0]
        up1 = take([P, 512])
        act_b = take([P, 512])
        actT = take([P, 512])
        y_sb = take([P, 512])
        sel = take([P, TH, SLOT], BF16)
        selG = take([P, TH, 2, SLOT])
        selGT = take([P, SEQ])
        bsel = take([3 * E, SLOT], BF16)
        M = take([P, TH, E])
        G = take([P, TH, E])
        posm = take([P, TH, E])
        brt = take([P, E])
        tab = take([1, 256], I32)
        out_sb = take([P, TH, D], start=base_hb)
        at[0] = base_up
        lg = take([P, TH, E])
        top = take([P, TH, 8])
        topi = take([P, TH, 8], U32)
        topf = take([P, TH, 8])
        gates = take([P, TH, 8])
        eq = take([P, TH, TOPK, E])
        nbc = take([E, 14])
        jt = take([JOBS, 3 * E + 6])
        assert at[0] <= base_up + 2 * 512

        T_J, T_NB, T_E, T_B = 0, E + 1, 2 * E + 1, 2 * E + 1 + JOBS

        cc, ecc, rcc = small[:, 0:8], small[:, 8:16], small[:, 16:24]
        cols = small[:, 24:40]
        gq_col, gkv_col = small[:, 40:42], small[:, 42:43]
        ssq, rms, rstd = small[:, 44:52], small[:, 52:60], small[:, 60:68]
        nmax = small[:, 68:80]
        rsum = small[:, 80:112]
        rrec = small[:, 112:120]
        nb_neg = small[:, 120:122]
        gsum = small[:, 122:124]
        ones = small[:, 128:129]
        spare = small[:, 132:133]

        ps = ctx.enter_context(nc.psum_tensor("ps", [P, 8, 512], F32))

        L = {n: sem("in_" + n) for n in (
            "x", "c", "cst", "bada", "gain", "gcol", "wq", "wkv", "relb", "bgu", "adaA", "adaB", "winA", "winQ", "winK",
            "winV", "gt1", "wo", "sh2", "sc2", "gt2", "rows", f"bc{GT1}", f"bc{SH2}", f"bc{SC2}", f"bc{GT2}", "wr", "bd")}
        for n in ("adaA", "adaB", "gt1", "sh2", "sc2", "gt2"):
            L[n] = (L[n], sem("in_" + n + "_end"))
        L["adaB"] += (sem("in_adaB_last"),)
        S = {n: sem(n) for n in (
            "ones_ok", "sums_ok", "c_exp", "silu", "x_rms", "xn_ok", "xT_ps", "ada_ps", "mod_ok", "col_ps",
            "col_ok", "hT_act", "hT_dve", "za_ps", "qc_ps", "kc_ps", "vc_ps", "qc_sb", "kc_sb", "vc_sb",
            "lat_rms", "lat_n", "lat_ps", "lat_T", "q_ps", "kv_ps", "q_sb", "k_sb", "v_sb", "q_rot", "qk_ps",
            "qT_act", "qT_dve", "b3_ok", "sc_ps", "sc_sb", "max_ok", "exp_ok", "pT_ps", "pT_act", "pT_dve",
            "pv_ps", "o_ok", "oT_ps", "oT_act", "oT_dve", "wo_ps", "o_rms", "x1_ok", "x1_rms", "h2_ok",
            "h2T_ps", "h2T_sb", "hb_ok", "hb_sub", "rows_clear", "lg_ps", "g_exp", "gate_ok", "M_ok", "G_ok",
            "cnt_ps", "nb_ok", "end_ps", "je_ok", "row_ps", "tab_ok", "pos_ok", "GT_ps", "GT_sb", "sum_step",
            "chain_v", "chain_a", "chain_p", "sel_ok", "selG_ok", "gath_ps", "xg_ok", "gate_ps", "up_ok",
            "comb_ps", "selT_ps", "selT_sb", "gm_ok", "sig_ok", "act_ok", "actT_ps", "actT_sb", "y_sb", "f_rms",
            "res_mul", "res_sum", "res_ok", "stored")}
        arrived = [sem(f"unit_arrived{u}") for u in range(RING)]
        used = [sem(f"unit_used{u}") for u in range(UNITS)]

        rows_dram = nc.dram_tensor("rows", [len(SPREAD), D], F32).ap()
        x_v = x[0].rearrange("(t p) d -> p t d", p=P)
        out_v = out[0].rearrange("(t p) d -> p t d", p=P)
        ada_v = w_ada[0].rearrange("(p j) n -> p j n", j=KC)
        win_v = w_in[0].rearrange("(k p) n -> p k n", p=P)
        wo_v = w_o[0].rearrange("(k p) n -> p k n", p=P)
        gu_v = w_gu[0].rearrange("e (k p) n -> e p k n", p=P)
        dn_v = w_down[0].rearrange("e (k p) n -> e p k n", p=P)

        def ada_w(u):
            return ring[:, u:u + 2, :].rearrange("p a b -> p (a b)").rearrange("p (j n) -> p j n", j=KC)

        ada_at = {SH1: 0, SC1: 2, GT1: 2, SH2: 2, SC2: 0, GT2: 2}
        ada_in = {SH1: "adaA", SC1: "adaB", GT1: "gt1", SH2: "sh2", SC2: "sc2", GT2: "gt2"}

        def ada_starts(v):
            return [0, 4, 6] if v == SC1 else [0, 4]

        w_za = ring[:, 4, 0:KC * ZA].rearrange("p (k n) -> p k n", k=KC)
        w_q = ring[:, 5, :].rearrange("p (k n) -> p k n", k=KC)
        w_k = ring[:, 0, :].rearrange("p (k n) -> p k n", k=KC)
        w_v = ring[:, 1, :].rearrange("p (k n) -> p k n", k=KC)
        w_om = ring[:, 4:6, :].rearrange("p a b -> p (a b)").rearrange("p (k n) -> p k n", k=KC)

        def place(m, u):
            return (UNITS * m + u) % RING

        def arrival(turn, m, u):
            return 16 * (UNITS * TURN // RING * turn + (UNITS * m + u) // RING + 1)

        def weights(m, u):
            return ring[:, place(m, u), :].rearrange("p (k n) -> p k n", k=2 if u < GU_UNITS else 4)

        def load(sp, e, m, u):
            if u < GU_UNITS:
                src = gu_v[bass.ds(e, 1), :, 2 * u:2 * u + 2, :]
            else:
                src = dn_v[bass.ds(e, 1), :, 4 * (u - GU_UNITS):4 * (u - GU_UNITS) + 4, :]
            sp.dma_start(weights(m, u), src.rearrange("a p k n -> p (a k) n")).then_inc(arrived[place(m, u)], 16)

        block = ctx.enter_context(nc.Block())

        @block.sync
        def _(sp):
            def ada(v):
                starts = ada_starts(v)
                for i, (lo, hi) in enumerate(zip(starts, starts[1:] + [KC])):
                    sp.dma_start(ada_w(ada_at[v])[:, lo:hi, :],
                                 ada_v[:, lo:hi, v * D:(v + 1) * D]).then_inc(L[ada_in[v]][i], 16)

            sp.dma_start(cc, c[0].rearrange("(p j) -> p j", j=KC)).then_inc(L["c"], 16)
            sp.dma_start(xs[:, :, :], x_v).then_inc(L["x"], 16)
            ada(SH1)
            sp.dma_start(cst[:, :], consts).then_inc(L["cst"], 16)
            sp.wait_ge(S["rows_clear"], 1)
            sp.dma_start(mod[0:P:32, :, :], b_ada[0].rearrange("(v g n) -> g v n", v=6, g=4)).then_inc(L["bada"], 16)
            for i, src in enumerate((g_pre_mix, g_post_mix, g_pre_ffn, g_post_ffn)):
                sp.dma_start(gain[0:P:32, i, :], src[0].rearrange("(g n) -> g n", g=4)).then_inc(L["gain"], 16)
            ada(SC1)
            sp.dma_start(w_za, win_v[:, :, 0:ZA]).then_inc(L["winA"], 16)
            sp.dma_start(w_q, win_v[:, :, ZA:ZA + CAW]).then_inc(L["winQ"], 16)
            sp.wait_ge(S["ada_ps"], 1)
            sp.dma_start(w_k, win_v[:, :, ZA + CAW:ZA + 2 * CAW]).then_inc(L["winK"], 16)
            sp.dma_start(wqb, w_qb[0].rearrange("(k p) n -> p k n", p=P)).then_inc(L["wq"], 16)
            sp.dma_start(wkvb, w_kvb[0]).then_inc(L["wkv"], 16)
            sp.dma_start(w_v, win_v[:, :, ZA + 2 * CAW:ZA + 3 * CAW]).then_inc(L["winV"], 16)
            for i in range(3):
                sp.dma_start(b_gu_f[i * E:(i + 1) * E, :], b_gu[0]).then_inc(L["bgu"], 16)
            sp.wait_ge(S["ada_ps"], 2)
            sp.wait_ge(S["ones_ok"], 1)
            hank = bass.AP(tensor=rel_bias.tensor, offset=rel_bias.offset,
                           ap=[[1, CHUNK], [CHUNK + SEQ, HEADS], [1, SEQ]])
            sp.dma_start(bias[CHUNK:P, :, :], hank).then_inc(L["relb"], 16)
            hank = bass.AP(tensor=rel_bias.tensor, offset=rel_bias.offset,
                           ap=[[1, CHUNK], [CHUNK + SEQ, HEADS], [1, SEQ - CHUNK]])
            sp.dma_start(bias[0:CHUNK, :, CHUNK:SEQ], hank).then_inc(L["relb"], 16)
            ada(GT1)
            sp.wait_ge(S["za_ps"], 1)
            sp.wait_ge(S["qc_ps"], 1)
            sp.dma_start(w_om, wo_v).then_inc(L["wo"], 16)
            sp.wait_ge(S["ada_ps"], 3)
            ada(SH2)
            sp.wait_ge(S["kc_ps"], 1)
            sp.wait_ge(S["vc_ps"], 1)
            ada(SC2)
            sp.wait_ge(S["ada_ps"], 4)
            ada(GT2)
            sp.wait_ge(S["ada_ps"], 5)
            load(sp, 0, 0, 0)
            load(sp, 0, 0, 1)
            sp.wait_ge(S["ada_ps"], 6)
            load(sp, 0, 0, 2)
            load(sp, 0, 0, 3)
            sp.wait_ge(S["wo_ps"], 2)
            load(sp, 0, 0, 4)
            load(sp, 0, 0, 5)
            sp.wait_ge(S["h2_ok"], 2 * TH)
            load(sp, 1, 1, 0)
            load(sp, 1, 1, 2)
            sp.wait_ge(S["lg_ps"], 1)
            sp.wait_ge(S["hb_ok"], 3 * TH)
            load(sp, 1, 1, 1)
            sp.wait_ge(S["tab_ok"], 1)

            def follow(e, m):
                jobs_done = sp.value_load(tab[0:1, bass.ds(T_J + 1 + e, 1)], min_val=1, max_val=JOBS)
                for u in range(UNITS):
                    ahead, nu = divmod(u + RING, UNITS)
                    if isinstance(e, int) and e + ahead >= E:
                        break
                    sp.wait_ge(used[u], jobs_done)
                    load(sp, e + ahead, (m + ahead) % TURN, nu)

            with sp.Fori(0, E // TURN) as turn:
                for m in range(TURN):
                    follow(turn * TURN + m, m)
            follow(E // TURN * TURN, 0)
            for t in range(TH):
                sp.wait_ge(S["res_sum" if t == 0 else "res_ok"], 1)
                sp.dma_start(out_v[:, t, :], out_sb[:, t, :]).then_inc(S["stored"], 16)
            sp.wait_ge(S["stored"], 16 * TH)

        @block.gpsimd
        def _(pool):
            chain = [0]

            def link(ins):
                chain[0] += 1
                ins.then_inc(S["chain_p"], 1)
                pool.wait_ge(S["chain_p"], chain[0])

            link(nc.gpsimd.memset(mod[:, :, :], 0.0))
            link(nc.gpsimd.memset(gain[:, :, :], 0.0))
            nc.gpsimd.memset(small[:, 131:132], 0.0).then_inc(S["rows_clear"], 1)
            pool.wait_ge(S["rows_clear"], 1)
            link(nc.gpsimd.memset(bias[0:CHUNK, :, 0:CHUNK], NEG))
            nc.gpsimd.memset(ones, 1.0).then_inc(S["ones_ok"], 1)
            pool.wait_ge(S["ones_ok"], 1)

            pool.wait_ge(L["bgu"], 48)
            r = b_gu_f
            link(nc.gpsimd.tensor_copy(b3[:, :], r))
            for first in (E, 2 * E):
                for i in range(first // E, 3):
                    rows = slice(i * E, (i + 1) * E)
                    link(nc.gpsimd.tensor_tensor(r[rows, :], r[rows, :], b3[rows, :], ALU.subtract))
                    link(nc.gpsimd.tensor_copy(b3[rows, :], r[rows, :]))
            nc.gpsimd.memset(small[:, 129:130], 0.0).then_inc(S["b3_ok"], 1)

            for i, v in enumerate(SPREAD):
                pool.wait_ge(S["mod_ok"], 3 + i)
                pool.dma_start(rows_dram[i].rearrange("(g n) -> g n", g=4), mod[0:P:32, v, :]).then_inc(L["rows"], 16)
            pool.wait_ge(L["rows"], 16 * len(SPREAD))
            pool.wait_ge(S["oT_ps"], 4)
            for i, v in enumerate(SPREAD):
                pool.dma_start(bc[v], rows_dram[i].partition_broadcast(P)).then_inc(L[f"bc{v}"], 16)
            pool.dma_start(wr, w_router[0].rearrange("(k p) n -> p k n", p=P)).then_inc(L["wr"], 16)
            pool.dma_start(brt, b_router.partition_broadcast(P)[:, 0, :]).then_inc(L["wr"], 16)
            pool.dma_start(bd, b_down[0]).then_inc(L["bd"], 16)

            for t in range(TH):
                for i in range(2):
                    pool.wait_ge(S["hb_ok"], 3 * t + i + 1)
                    if (t, i) == (1, 0):
                        pool.wait_ge(S["hb_ok"], 4)
                    if i == 0:
                        pool.wait_ge(S["h2T_ps"], 2 * t + 2)
                    nc.gpsimd.tensor_tensor(h2[:, t, :], h2[:, t, :], hb[:, t, i, :],
                                            ALU.subtract).then_inc(S["hb_sub"], 1)

            pool.wait_ge(S["res_mul"], 1)
            nc.gpsimd.tensor_tensor(out_sb[:, 0, :], out_sb[:, 0, :], xs[:, 0, :], ALU.add).then_inc(S["res_sum"], 1)

        @block.tensor
        def _(pe):
            mm = nc.tensor.matmul

            def transposes(blocks, dst):
                for i, (src, m) in enumerate(blocks):
                    last = nc.tensor.transpose(dst[0:m, i * P:(i + 1) * P], src, ident)
                return last

            def ada(v, bank, col, rows=range(KC)):
                w = ada_w(ada_at[v])
                for j in rows:
                    if j in ada_starts(v) or j == rows[0]:
                        pe.wait_ge(L[ada_in[v]][sum(j >= lo for lo in ada_starts(v)) - 1], 16)
                    for g in range(4):
                        last = mm(ps[32 * g:32 * g + 32, bank, col:col + QW], silu_c[:, j, :],
                                  w[:, j, g * QW:(g + 1) * QW], start=(j == 0), stop=(j == KC - 1))
                if rows[-1] == KC - 1:
                    last.then_inc(S["ada_ps"], 1)

            def ada_end(v, bank):
                w = ada_w(ada_at[v])
                for g in range(4):
                    last = mm(ps[32 * g:32 * g + 32, bank, 0:QW], ones.to_broadcast([P, 32]),
                              w[:, 0, g * QW:(g + 1) * QW], start=True, stop=True)
                last.then_inc(S["ada_ps"], 1)

            pe.wait_ge(S["silu"], 1)
            ada(SH1, 4, 0)
            pe.wait_ge(L["cst"], 16)
            pe.wait_ge(S["xn_ok"], 1)
            for b in range(4):
                last = transposes([(xn[:, t, (2 * b + i) * P:(2 * b + i + 1) * P], P)
                                   for i in range(2) for t in range(TH)], ps[:, b, :])
                last.then_inc(S["xT_ps"], 1)
            for v in (SH1, SC1):
                if v == SC1:
                    ada(SC1, 5, 0)
                pe.wait_ge(S["mod_ok"], v + 1)
                for k in range(KC):
                    last = mm(ps[:, 6, v * KC + k:v * KC + k + 1], mod[:, v, (k % 2) * P:(k % 2 + 1) * P],
                              ident[:, 32 * (k // 2):32 * (k // 2) + 1], start=True, stop=True)
            last.then_inc(S["col_ps"], 1)

            pe.wait_ge(L["winA"], 16)
            for t in range(TH):
                for i in range(KC):
                    k = i // 2 + 4 * (i % 2)
                    if t == 0:
                        pe.wait_ge(S["hT_act" if i % 2 else "hT_dve"], i // 2 + 1)
                    last = mm(ps[:, 6 + t, 0:ZA], hT[:, k, t * P:(t + 1) * P], w_za[:, k, :],
                              start=(i == 0), stop=(i == KC - 1))
            last.then_inc(S["za_ps"], 1)
            for name, w, bank, done in (("winQ", w_q, 0, "qc_ps"), ("winK", w_k, 2, "kc_ps")):
                pe.wait_ge(L[name], 16)
                for hp in range(HEADS // 2):
                    for k in range(KC):
                        last = mm(ps[:, bank + hp // 2, (hp % 2) * SEQ:(hp % 2 + 1) * SEQ],
                                  w[:, k, hp * P:(hp + 1) * P], hT[:, k, :], start=(k == 0), stop=(k == KC - 1))
                last.then_inc(S[done], 1)
            pe.wait_ge(S["lat_n"], 1)
            for i in range(3):
                last = transposes([(za[:, t, i * P:(i + 1) * P], P) for t in range(TH)],
                                  ps[:, 6 + i // 2, (i % 2) * SEQ:(i % 2 + 1) * SEQ])
            last.then_inc(S["lat_ps"], 1)
            pe.wait_ge(S["qc_sb"], 1)
            pe.wait_ge(S["sums_ok"], 1)
            pe.wait_ge(S["ones_ok"], 1)
            ada_end(GT1, 0)
            pe.wait_ge(L["winV"], 16)
            for t in range(TH):
                for k in range(KC):
                    last = mm(ps[:, 4 + t, :], hT[:, k, t * P:(t + 1) * P], w_v[:, k, :],
                              start=(k == 0), stop=(k == KC - 1))
            last.then_inc(S["vc_ps"], 1)
            pe.wait_ge(S["lat_T"], 1)
            pe.wait_ge(S["mod_ok"], 3)
            pe.wait_ge(S["kc_sb"], 1)
            pe.wait_ge(L["wq"], 16)
            W2 = HEADS * QK // 2
            for t in range(TH):
                for n in range(2):
                    for k in range(QL // P):
                        last = mm(ps[:, 2 * t + n, 0:W2], cqT[:, k, t * P:(t + 1) * P],
                                  wqb[:, k, n * W2:(n + 1) * W2], start=(k == 0), stop=(k == QL // P - 1))
            last.then_inc(S["q_ps"], 1)
            pe.wait_ge(S["vc_sb"], 1)
            pe.wait_ge(L["wkv"], 16)
            for t in range(TH):
                for n in range(2):
                    last = mm(ps[:, 4 + 2 * t + n, :], ckvT[:, t * P:(t + 1) * P],
                              wkvb[:, n * 512:(n + 1) * 512], start=True, stop=True)
            last.then_inc(S["kv_ps"], 1)
            pe.wait_ge(S["q_sb"], 1)
            pe.wait_ge(S["sums_ok"], 2)
            ada_end(SH2, 3)
            pe.wait_ge(S["q_rot"], 1)
            pe.wait_ge(S["b3_ok"], 1)
            for i, src in enumerate((q_t, k_t)):
                if i == 1:
                    pe.wait_ge(S["k_sb"], 4)
                for n in range(2):
                    for t in range(TH):
                        if (i, n, t) == (0, 1, 1):
                            pe.wait_ge(S["mod_ok"], 4)
                        last = transposes([(src[:, t, 4 * n + h, :], QK) for h in range(4)],
                                          ps[:, 4 * i + 2 * n + t, :])
                        last.then_inc(S["qk_ps"], 1)

            pe.wait_ge(S["qT_act"], 4)
            pe.wait_ge(S["qT_dve"], 4)

            ada_after = {}
            for first, v, col in ((1, SC2, 0), (5, GT2, QW)):
                for n, rows in enumerate((range(0, 3), range(3, 6), range(6, KC))):
                    ada_after[first + n] = (v, col, rows)

            def scores(i):
                mixer, b, heads = GROUPS[i]
                K = (b + 1) * P
                if i >= 3:
                    pe.wait_ge(S["sc_sb"], i - 2)
                for n, h in enumerate(heads):
                    if mixer == 0:
                        l, r = qT[:, h, b * P:(b + 1) * P], kT[:, h, 0:K]
                    else:
                        row = 64 * (h % 2)
                        l = qcT[row:row + 64, h // 2, b * P:(b + 1) * P]
                        r = kcT[row:row + 64, h // 2, 0:K]
                    last = mm(ps[:, SC_BANK[i % 3], n * K:(n + 1) * K], l, r, start=True, stop=True)
                last.then_inc(S["sc_ps"], 1)

            for i in range(3):
                scores(i)
            def transposed(i):
                pe.wait_ge(S["exp_ok"], i + 1)
                if i >= 2:
                    pe.wait_ge(S["pT_act" if i % 2 == 0 else "pT_dve"], i // 2)
                transposes([(p_sb[:, i % 3, j * P:(j + 1) * P], P) for j in range(4)],
                           ps[:, 2 + i % 2, :]).then_inc(S["pT_ps"], 1)

            def outputs_turned(b):
                transposes([(o_sb[:, t, (2 * b + i) * P:(2 * b + i + 1) * P], P) for i in range(2) for t in range(TH)],
                           ps[:, b, :]).then_inc(S["oT_ps"], 1)

            def project(t, n, rows):
                for k in rows:
                    last = mm(ps[:, 4 + 2 * t + n, :], oT[:, k, t * P:(t + 1) * P],
                              w_om[:, k, n * 512:(n + 1) * 512], start=(k == 0), stop=(k == KC - 1))
                return last

            transposed(0)
            for i, (mixer, b, heads) in enumerate(GROUPS):
                if i + 3 < len(GROUPS):
                    scores(i + 3)
                if i + 1 < len(GROUPS):
                    transposed(i + 1)
                if i in ada_after:
                    v, col, rows = ada_after[i]
                    if v == GT2 and rows[0] == 0:
                        pe.wait_ge(S["mod_ok"], 5)
                    ada(v, 7, col, rows)
                if i == len(GROUPS) - 2:
                    pe.wait_ge(S["sc_sb"], len(GROUPS))
                    pe.wait_ge(S["o_ok"], 2)
                    outputs_turned(0)
                    outputs_turned(1)
                part = 2 * mixer + b
                if part >= 2 and i and GROUPS[i - 1][:2] != (mixer, b):
                    pe.wait_ge(S["o_ok"], part - 1)
                pe.wait_ge(S["pT_act" if i % 2 == 0 else "pT_dve"], i // 2 + 1)
                vals = v_a if mixer == 0 else v_b
                for n, h in enumerate(heads):
                    for kb in range(b + 1):
                        j = n * (b + 1) + kb
                        last = mm(ps[:, 4 + part % 2, h * VD:(h + 1) * VD], pT[:, i % 2, j * P:(j + 1) * P],
                                  vals[:, kb, h * VD:(h + 1) * VD], start=(kb == 0), stop=(kb == b))
                last.then_inc(S["pv_ps"], 1)

            pe.wait_ge(S["oT_act"], 2)
            pe.wait_ge(S["o_ok"], 3)
            pe.wait_ge(L["wo"], 16)
            project(0, 0, range(KC // 2))
            pe.wait_ge(S["o_ok"], 4)
            outputs_turned(2)
            outputs_turned(3)
            project(0, 1, range(KC // 2))
            pe.wait_ge(S["oT_dve"], 2)
            project(0, 0, range(KC // 2, KC))
            project(0, 1, range(KC // 2, KC)).then_inc(S["wo_ps"], 1)
            pe.wait_ge(S["mod_ok"], 6)
            project(1, 0, range(KC))
            project(1, 1, range(KC)).then_inc(S["wo_ps"], 1)

            def keep_clock(n, bank):
                for _ in range(n):
                    mm(ps[:, bank, :], ident, cst[:, 0:512], start=True, stop=True)

            pe.wait_ge(L["wr"], 32)
            for t in range(TH):
                for b in range(2):
                    pe.wait_ge(S["h2_ok"], 2 * t + b + 1)
                    transposes([(h2[:, t, (4 * b + i) * P:(4 * b + i + 1) * P], P) for i in range(4)],
                               ps[:, 4 + 2 * t + b, :]).then_inc(S["h2T_ps"], 1)
                if t == 0:
                    keep_clock(6, 3)
                for k in range(KC):
                    if k % 4 == 0:
                        pe.wait_ge(S["h2T_sb"], 2 * t + k // 4 + 1)
                    last = mm(ps[:, 0, t * E:(t + 1) * E], h2T[:, k, t * P:(t + 1) * P], wr[:, k, :],
                              start=(k == 0), stop=(k == KC - 1))
            last.then_inc(S["lg_ps"], 1)

            GATE, UP, Y, TR = 4, 5, 6, 7

            def gather(chunks):
                for k in chunks:
                    n = 0
                    for t in range(TH):
                        for i in range(3):
                            last = mm(ps[:, GATE, k * SLOT:(k + 1) * SLOT], hb[:, t, i, k * P:(k + 1) * P],
                                      sel[:, t, :], start=(n == 0), stop=(n == 5))
                            n += 1
                if k == KC - 1:
                    last.then_inc(S["gath_ps"], 1)

            keep_clock(2, 3)
            pe.wait_ge(S["M_ok"], 1)
            for t in range(TH):
                mm(ps[0:E, 1, 0:1], M[:, t, :], ones, start=(t == 0), stop=(t == TH - 1))
            mm(ps[:, 1, E:2 * E], tri, M[:, 0, :], start=True, stop=True)
            mm(ps[:, 1, 2 * E:3 * E], tri, M[:, 1, :], start=True, stop=False)
            mm(ps[:, 1, 2 * E:3 * E], ones.to_broadcast([P, P]), M[:, 0, :], start=False,
               stop=True).then_inc(S["cnt_ps"], 1)
            keep_clock(1, 3)
            pe.wait_ge(S["nb_ok"], 1)
            nb, few_neg = nbc[:, 8:9], nbc[:, 10:11]
            trie = cst[0:E, C_TRIE:C_TRIE + E + 1]
            mm(ps[0:JOBS, 3, 0:E], nb.to_broadcast([E, JOBS]), trie[:, 1:E + 1], start=True, stop=True)
            mm(ps[0:JOBS, 3, E:2 * E], nb.to_broadcast([E, JOBS]), ident[0:E, 0:E], start=True, stop=True)
            mm(ps[0:JOBS, 3, 2 * E:3 * E], nb.to_broadcast([E, JOBS]), trie[:, 1:E + 1], start=True, stop=False)
            mm(ps[0:JOBS, 3, 2 * E:3 * E], few_neg.to_broadcast([E, JOBS]), ident[0:E, 0:E], start=False,
               stop=True).then_inc(S["end_ps"], 1)
            pe.wait_ge(S["G_ok"], 1)
            for t in range(TH):
                last = nc.tensor.transpose(ps[0:E, 2, t * P:(t + 1) * P], G[:, t, :], ident)
            last.then_inc(S["GT_ps"], 1)
            pe.wait_ge(S["hb_ok"], 3 * TH)
            pe.wait_ge(S["sel_ok"], 1)
            gather(range(KC))
            pe.wait_ge(S["je_ok"], 1)
            mm(ps[0:1, 5, T_J:T_J + E + 1], nb, trie, start=True, stop=True)
            mm(ps[0:1, 5, T_NB:T_NB + E], nb, ident[0:E, 0:E], start=True, stop=True)
            mm(ps[0:1, 5, T_E:T_E + JOBS], jt[:, 3 * E:3 * E + 1], ident[0:JOBS, 0:JOBS], start=True, stop=True)
            mm(ps[0:1, 5, T_B:T_B + JOBS], jt[:, 3 * E + 4:3 * E + 5], ident[0:JOBS, 0:JOBS], start=True,
               stop=True).then_inc(S["row_ps"], 1)
            keep_clock(2, 3)

            def slots_column(job):
                return pe.value_load(tab[0:1, bass.ds(T_B + job, 1)], min_val=0, max_val=2 * SEQ - SLOT)

            def bias_down(t):
                for n in range(2):
                    mm(ps[:, 2 * t + n, :], GT[:, t * P:(t + 1) * P], bd[:, n * 512:(n + 1) * 512],
                       start=True, stop=True)

            def combine(parts, step, done=None):
                slots, width = P // parts, D // parts
                for t in (range(TH) if parts == 4 else [step]):
                    for half in range(2):
                        n = half if parts == 2 else 2 * half + step
                        col = 0 if parts == 2 else width * step
                        on = slice(slots * n, slots * n + slots)
                        last = mm(ps[:, 2 * t + half, col:col + width], selGT[on, t * P:(t + 1) * P],
                                  y_sb[on, 0:width], start=False, stop=True, skip_group_check=True)
                    if done is not None and (parts == 2 or step == 1):
                        last.then_inc(done, 1)
                return last

            def combine_before(job, step, done=None):
                if step == 0:
                    pe.wait_ge(S["y_sb"], job)
                    pe.wait_ge(S["selT_sb"], job)
                with pe.If(slots_column(job - 1) >= SEQ):
                    if step == 1:
                        pe.wait_ge(S["sum_step"], job)
                    last = combine(4, step, done)
                    if step == 0:
                        last.then_inc(S["sum_step"], 1)
                with pe.Else():
                    last = combine(2, step, done)
                    if step == 0 and done is None:
                        last.then_inc(S["sum_step"], 1)

            def add_before(job, step):
                with pe.If(job < 1):
                    pe.wait_ge(S["GT_sb"], 1)
                    pe.wait_ge(L["bd"], 16)
                    bias_down(step)
                with pe.Else():
                    combine_before(job, step)

            def work(turn, m, job, parts, ends=False):
                slots, width = P // parts, F // parts
                pe.wait_ge(S["xg_ok"], job + 1)
                for bank in range(2):
                    for g in range(parts):
                        mm(ps[slots * g:slots * g + slots, GATE + bank, 0:width], bsel[:, 0:slots],
                           b3[:, bank * F + width * g:bank * F + width * g + width], start=True, stop=False)
                for u in range(GU_UNITS):
                    last_unit = u == GU_UNITS - 1
                    if ends and u >= 2:
                        keep_clock(2, TR)
                    if last_unit:
                        add_before(job, 0)
                    pe.wait_ge(arrived[place(m, u)], arrival(turn, m, u))
                    seq = ([(bank, k) for bank in range(2) for k in range(2)] if last_unit else
                           [(bank, k) for k in range(2) for bank in range(2)])
                    for bank, k in seq:
                        kk = 2 * u + k
                        for g in range(parts):
                            last = mm(ps[slots * g:slots * g + slots, GATE + bank, 0:width],
                                      xgT[:, kk * SLOT:kk * SLOT + slots],
                                      weights(m, u)[:, k, bank * F + width * g:bank * F + width * g + width],
                                      start=False, stop=(kk == KC - 1))
                        if last_unit and (bank, k) == (0, 1):
                            last.then_inc(S["gate_ps"], 1)
                    last.then_inc(used[u], 1)
                add_before(job, 1)
                pe.wait_ge(S["selG_ok"], job + 1)
                for t in range(TH):
                    last = nc.tensor.transpose(ps[:, Y, t * P:(t + 1) * P],
                                               selG[:, t, :, :].rearrange("p a s -> p (a s)"), ident)
                last.then_inc(S["selT_ps"], 1)
                pe.wait_ge(S["sel_ok"], job + 2)
                gather(range(KC // 2))
                pe.wait_ge(S["act_ok"], job + 1)
                transposes([(act_b[:, j * P:(j + 1) * P], P) for j in range(width // P)],
                           ps[:, TR, :]).then_inc(S["actT_ps"], 1)
                gather(range(KC // 2, KC))
                pe.wait_ge(S["actT_sb"], job + 1)
                pe.wait_ge(S["selT_sb"], job + 1)
                for d in range(2):
                    if ends:
                        keep_clock(1 + d, TR)
                    pe.wait_ge(arrived[place(m, GU_UNITS + d)], arrival(turn, m, GU_UNITS + d))
                    for k in range(4):
                        g, j = divmod(4 * d + k, width // P)
                        for n in range(parts):
                            last = mm(ps[slots * n:slots * n + slots, Y, 0:width],
                                      actT[:, j * P + slots * g:j * P + slots * g + slots],
                                      weights(m, GU_UNITS + d)[:, k, width * n:width * n + width],
                                      start=(d == 0 and k == 0), stop=(d == 1 and k == 3))
                    last.then_inc(used[GU_UNITS + d], 1)

            def expert(turn, m, ends=False):
                e = turn * TURN + m
                blocks = pe.value_load(tab[0:1, bass.ds(T_NB + e, 1)], min_val=1, max_val=MAXBLK)
                before = pe.value_load(tab[0:1, bass.ds(T_J + e, 1)], min_val=0, max_val=JOBS)
                with pe.Fori(0, blocks) as blk:
                    job = pe.snap(before + blk)
                    with pe.If(slots_column(job) >= SEQ):
                        work(turn, m, job, 4, ends)
                    with pe.Else():
                        work(turn, m, job, 2, ends)

            pe.wait_ge(S["tab_ok"], 1)
            with pe.Fori(0, E // TURN) as turn:
                for m in range(TURN):
                    expert(turn, m)
            for m in range(E % TURN):
                expert(E // TURN, m, m == E % TURN - 1)
            keep_clock(1, TR)
            total = pe.value_load(tab[0:1, T_J + E:T_J + E + 1], min_val=E, max_val=JOBS)
            for step in range(2):
                combine_before(total, step, S["comb_ps"])

        @block.scalar
        def _(act):
            a = nc.scalar.activation
            chain = [0]

            def link(ins):
                chain[0] += 1
                ins.then_inc(S["chain_a"], 1)
                act.wait_ge(S["chain_a"], chain[0])

            act.dma_start(gq_col, g_q[0].rearrange("(k p) -> p k", p=P)).then_inc(L["gcol"], 16)
            act.dma_start(gkv_col, g_kv[0].rearrange("(k p) -> p k", p=P)).then_inc(L["gcol"], 16)

            act.wait_ge(L["c"], 16)
            a(ecc, cc, ACT.Exp, scale=-1.0).then_inc(S["c_exp"], 1)
            act.wait_ge(L["x"], 16)
            for t in range(TH):
                link(a(xn[:, t, :], xs[:, t, :], ACT.Square, accum_out=ssq[:, t:t + 1]))
            act.wait_ge(L["cst"], 16)
            a(rms[:, 0:2], ssq[:, 0:2], ACT.Sqrt, bias=eps, scale=1.0 / D).then_inc(S["x_rms"], 1)
            act.wait_ge(S["col_ok"], 1)
            act.wait_ge(S["xT_ps"], 4)
            for k in range(4, KC):
                a(hT[:, k, :], ps[:, k // 2, (k % 2) * SEQ:(k % 2 + 1) * SEQ], ACT.Identity,
                  bias=cols[:, k:k + 1], scale=cols[:, KC + k:KC + k + 1]).then_inc(S["hT_act"], 1)
            act.wait_ge(S["za_ps"], 1)
            for t in range(TH):
                last = nc.scalar.copy(za[:, t, :], ps[:, 6 + t, 0:ZA])
            link(last)
            for t in range(TH):
                a(cqT[:, t, :], za[:, t, 0:QL], ACT.Square, accum_out=ssq[:, 2 + t:3 + t])
                last = a(ckvT[:, t * P:(t + 1) * P], za[:, t, QL:QL + KVL], ACT.Square, accum_out=ssq[:, 4 + t:5 + t])
            link(last)
            a(rms[:, 2:4], ssq[:, 2:4], ACT.Sqrt, bias=eps, scale=1.0 / QL)
            a(rms[:, 4:6], ssq[:, 4:6], ACT.Sqrt, bias=eps, scale=1.0 / KVL).then_inc(S["lat_rms"], 1)
            act.wait_ge(S["qc_ps"], 1)
            for b in range(2):
                last = nc.scalar.copy(qcT[:, 2 * b:2 * b + 2, :], ps[:, b, :].rearrange("p (a s) -> p a s", a=2))
            last.then_inc(S["qc_sb"], 1)
            act.wait_ge(S["kc_ps"], 1)
            for b in range(2):
                last = nc.scalar.copy(kcT[:, 2 * b:2 * b + 2, :], ps[:, 2 + b, :].rearrange("p (a s) -> p a s", a=2))
            last.then_inc(S["kc_sb"], 1)
            act.wait_ge(S["vc_ps"], 1)
            for t in range(TH):
                last = nc.scalar.copy(v_b[:, t, :], ps[:, 4 + t, :])
            last.then_inc(S["vc_sb"], 1)
            act.wait_ge(S["q_ps"], 1)
            for t in range(TH):
                for n in range(2):
                    last = nc.scalar.copy(q_t[:, t, 4 * n:4 * n + 4, :],
                                          ps[:, 2 * t + n, 0:4 * QK].rearrange("p (h d) -> p h d", h=4))
            last.then_inc(S["q_sb"], 1)
            act.wait_ge(S["kv_ps"], 1)
            for t in range(TH):
                for n in range(2):
                    nc.scalar.copy(
                        v_a[:, t, 4 * n * VD:4 * (n + 1) * VD].rearrange("p (h d) -> p h d", h=4),
                        ps[:, 4 + 2 * t + n, :].rearrange("p (h d) -> p h d", h=4)[:, :, NOPE:]).then_inc(S["v_sb"], 1)
            for i in range(4):
                act.wait_ge(S["qk_ps"], 5 + i)
                n, t = i // 2, i % 2
                nc.scalar.copy(kT[:, 4 * n:4 * n + 4, t * P:(t + 1) * P],
                               ps[0:QK, 4 + i, :].rearrange("p (h s) -> p h s", h=4)).then_inc(S["qT_act"], 1)

            def exps(i):
                mixer, b, heads = GROUPS[i]
                K = (b + 1) * P
                act.wait_ge(S["max_ok"], i + 1)
                if i >= 3:
                    act.wait_ge(S["pT_ps"], i - 2)
                for n, h in enumerate(heads):
                    r = (2 * mixer + b) * HEADS + h
                    last = a(p_sb[:, i % 3, n * K:(n + 1) * K], s_sb[:, i % 3, n * K:(n + 1) * K], ACT.Exp,
                             bias=nmax[:, 4 * (i % 3) + n:4 * (i % 3) + n + 1], accum_out=rsum[:, r:r + 1])
                last.then_inc(S["exp_ok"], 1)

            exps(0)
            for i in range(len(GROUPS)):
                if i + 1 < len(GROUPS):
                    exps(i + 1)
                if i % 2 == 0:
                    act.wait_ge(S["pT_ps"], i + 1)
                    if i >= 2:
                        act.wait_ge(S["pv_ps"], i - 1)
                    nc.scalar.copy(pT[:, 0, :], ps[:, 2, :]).then_inc(S["pT_act"], 1)
            for b in range(2):
                act.wait_ge(S["oT_ps"], b + 1)
                nc.scalar.copy(oT[:, 2 * b:2 * b + 2, :], ps[:, b, :].rearrange("p (a s) -> p a s", a=2)).then_inc(S["oT_act"], 1)
            act.wait_ge(S["oT_ps"], 4)
            a(spare, eps, ACT.Sqrt)
            for t in range(TH):
                act.wait_ge(S["wo_ps"], t + 1)
                link(a(h2[:, t, :].rearrange("p (n c) -> p n c", n=2), ps[:, 4 + 2 * t:6 + 2 * t, :], ACT.Square,
                       accum_out=ssq[:, t:t + 1]))
                a(rms[:, t:t + 1], ssq[:, t:t + 1], ACT.Sqrt, bias=eps, scale=1.0 / D).then_inc(S["o_rms"], 1)
                act.wait_ge(S["x1_ok"], t + 1)
                link(a(h2[:, t, :], xs[:, t, :], ACT.Square, accum_out=ssq[:, 2 + t:3 + t]))
                a(rms[:, 2 + t:3 + t], ssq[:, 2 + t:3 + t], ACT.Sqrt, bias=eps, scale=1.0 / D).then_inc(S["x1_rms"], 1)
                if t == 0:
                    act.wait_ge(S["h2_ok"], 2)
                    nc.scalar.copy(hb[:, 0, 0, :], h2[:, 0, :]).then_inc(S["hb_ok"], 1)

            def h2_turned(t):
                for b in range(2):
                    act.wait_ge(S["h2T_ps"], 2 * t + b + 1)
                    nc.scalar.copy(h2T[:, 4 * b:4 * b + 4, t * P:(t + 1) * P],
                                   ps[:, 4 + 2 * t + b, :].rearrange("p (k s) -> p k s", k=4)).then_inc(S["h2T_sb"], 1)

            def part(t, i):
                if i:
                    act.wait_ge(S["hb_sub"], 2 * t + i)
                nc.scalar.copy(hb[:, t, i, :], h2[:, t, :]).then_inc(S["hb_ok"], 1)

            h2_turned(0)
            part(0, 1)
            act.wait_ge(S["h2_ok"], 4)
            part(1, 0)
            part(0, 2)
            h2_turned(1)
            part(1, 1)
            act.wait_ge(S["gate_ok"], 1)
            for t in range(TH):
                last = a(gates[:, t, 0:TOPK], top[:, t, 0:TOPK], ACT.Exp, bias=nb_neg[:, t:t + 1],
                         accum_out=gsum[:, t:t + 1])
            last.then_inc(S["g_exp"], 1)
            part(1, 2)

            act.wait_ge(S["gath_ps"], 1)
            nc.scalar.copy(xgT, ps[:, 4, :]).then_inc(S["xg_ok"], 1)
            act.wait_ge(S["tab_ok"], 1)
            total = act.value_load(tab[0:1, T_J + E:T_J + E + 1], min_val=E, max_val=JOBS)
            with act.Fori(0, total) as job:
                act.wait_ge(S["gm_ok"], job + 1)
                a(sg, gm, ACT.Sigmoid, scale=ALPHA).then_inc(S["sig_ok"], 1)
                act.wait_ge(S["selT_ps"], job + 1)
                nc.scalar.copy(selGT, ps[:, 6, 0:SEQ]).then_inc(S["selT_sb"], 1)
                act.wait_ge(S["gath_ps"], job + 2)
                nc.scalar.copy(xgT, ps[:, 4, :]).then_inc(S["xg_ok"], 1)
                act.wait_ge(used[UNITS - 1], job + 1)
                nc.scalar.copy(y_sb, ps[:, 6, :]).then_inc(S["y_sb"], 1)

            a(spare, eps, ACT.Sqrt)
            for t in range(TH):
                act.wait_ge(S["comb_ps"], t + 1)
                link(a(ring[:, 0, t * D:(t + 1) * D].rearrange("p (n c) -> p n c", n=2), ps[:, 2 * t:2 * t + 2, :],
                       ACT.Square, accum_out=ssq[:, t:t + 1]))
                a(rms[:, t:t + 1], ssq[:, t:t + 1], ACT.Sqrt, bias=eps, scale=1.0 / D).then_inc(S["f_rms"], 1)

        @block.vector
        def _(dve):
            v = nc.vector
            chain = [0]

            def link(ins):
                chain[0] += 1
                ins.then_inc(S["chain_v"], 1)
                dve.wait_ge(S["chain_v"], chain[0])

            dve.wait_ge(S["c_exp"], 1)
            link(v.tensor_scalar(ecc, ecc, 1.0, None, ALU.add))
            link(v.reciprocal(rcc, ecc))
            link(v.tensor_tensor(rcc, rcc, cc, ALU.mult))
            v.tensor_copy(silu_c[:, :, :], rcc.unsqueeze(2).to_broadcast([P, KC, 32])).then_inc(S["silu"], 1)
            dve.wait_ge(S["x_rms"], 1)
            link(v.reciprocal(rstd[:, 0:2], rms[:, 0:2]))
            for t in range(TH):
                last = v.tensor_scalar(xn[:, t, :], xs[:, t, :], rstd[:, t:t + 1], None, ALU.mult)
            last.then_inc(S["xn_ok"], 1)

            def mod_row(i, vec, bank, col):
                dve.wait_ge(S["ada_ps"], i + 1)
                if i == 0:
                    dve.wait_ge(L["bada"], 16)
                    dve.wait_ge(L["gain"], 64)
                first = v.tensor_tensor(mod[:, vec, :], ps[:, bank, col:col + QW], mod[:, vec, :], ALU.add)
                if vec in GAINED:
                    link(first)
                    plus = 1.0 if vec in (SC1, SC2) else 0.0
                    first = v.scalar_tensor_tensor(mod[:, vec, :], mod[:, vec, :], plus,
                                                   gain[:, GAINED.index(vec), :], ALU.add, ALU.mult)
                first.then_inc(S["mod_ok"], 1)

            def ada_sums(vec):
                w = ada_w(ada_at[vec])
                dve.wait_ge(L[ada_in[vec]][0], 16)
                link(v.tensor_scalar(w[:, 0, :], w[:, 0, :], rcc[:, 0:1], None, ALU.mult))
                for j in range(1, KC):
                    if j == KC // 2:
                        dve.wait_ge(L[ada_in[vec]][1], 16)
                    last = v.scalar_tensor_tensor(w[:, 0, :], w[:, j, :], rcc[:, j:j + 1], w[:, 0, :],
                                                  ALU.mult, ALU.add)
                    if j < KC - 1:
                        link(last)
                last.then_inc(S["sums_ok"], 1)

            mod_row(0, SH1, 4, 0)
            mod_row(1, SC1, 5, 0)
            dve.wait_ge(S["col_ps"], 1)
            v.tensor_copy(cols, ps[:, 6, 0:2 * KC]).then_inc(S["col_ok"], 1)
            dve.wait_ge(S["col_ok"], 1)
            dve.wait_ge(S["xT_ps"], 4)
            for k in range(4):
                v.tensor_scalar(hT[:, k, :], ps[:, k // 2, (k % 2) * SEQ:(k % 2 + 1) * SEQ],
                                cols[:, KC + k:KC + k + 1], cols[:, k:k + 1], ALU.mult, ALU.add).then_inc(S["hT_dve"], 1)
            dve.wait_ge(S["lat_rms"], 1)
            link(v.reciprocal(rstd[:, 2:6], rms[:, 2:6]))
            for t in range(TH):
                v.tensor_scalar(za[:, t, 0:QL], za[:, t, 0:QL], rstd[:, 2 + t:3 + t], None, ALU.mult)
                last = v.tensor_scalar(za[:, t, QL:QL + KVL], za[:, t, QL:QL + KVL], rstd[:, 4 + t:5 + t], None, ALU.mult)
            last.then_inc(S["lat_n"], 1)
            ada_sums(GT1)
            mod_row(2, GT1, 0, 0)
            dve.wait_ge(S["lat_ps"], 1)
            dve.wait_ge(L["gcol"], 32)
            for k in range(2):
                v.tensor_scalar(cqT[:, k, :], ps[:, 6, k * SEQ:(k + 1) * SEQ], gq_col[:, k:k + 1], None, ALU.mult)
            v.tensor_scalar(ckvT, ps[:, 7, 0:SEQ], gkv_col, None, ALU.mult).then_inc(S["lat_T"], 1)

            def rotate(x1, x2, shape, t, tmp):
                cs = cst[:, C_ROPE + 2 * HALF * t:C_ROPE + 2 * HALF * t + HALF]
                sn = cst[:, C_ROPE + 2 * HALF * t + HALF:C_ROPE + 2 * HALF * (t + 1)]
                if len(shape) == 3:
                    cs, sn = cs.unsqueeze(1).to_broadcast(shape), sn.unsqueeze(1).to_broadcast(shape)
                v.tensor_tensor(tmp[0], x1, cs, ALU.mult)
                v.tensor_tensor(tmp[1], x2, sn, ALU.mult)
                v.tensor_tensor(tmp[2], x2, cs, ALU.mult)
                link(v.tensor_tensor(tmp[3], x1, sn, ALU.mult))
                v.tensor_tensor(x1, tmp[0], tmp[1], ALU.subtract)
                return v.tensor_tensor(x2, tmp[2], tmp[3], ALU.add)

            for t in range(TH):
                kr = za[:, t, QL + KVL:ZA]
                link(rotate(kr[:, 0:HALF], kr[:, HALF:ROPE], [P, HALF], t, [rope_t[:, i, 0, :] for i in range(4)]))
            ada_sums(SH2)
            dve.wait_ge(S["q_sb"], 1)
            for t in range(TH):
                last = rotate(q_t[:, t, :, NOPE:NOPE + HALF], q_t[:, t, :, NOPE + HALF:QK], [P, HEADS, HALF], t,
                              [rope_t[:, i] for i in range(4)])
                if t == 0:
                    link(last)
            last.then_inc(S["q_rot"], 1)
            dve.wait_ge(S["kv_ps"], 1)
            for t in range(TH):
                v.tensor_copy(k_t[:, t, :, NOPE:QK],
                              za[:, t, QL + KVL:ZA].unsqueeze(1).to_broadcast([P, HEADS, ROPE]))
                for n in range(2):
                    dve.wait_ge(S["v_sb"], 2 * t + n + 1)
                    v.tensor_copy(k_t[:, t, 4 * n:4 * n + 4, 0:NOPE],
                                  ps[:, 4 + 2 * t + n, :].rearrange("p (h d) -> p h d", h=4)[:, :, 0:NOPE]).then_inc(
                                      S["k_sb"], 1)
            mod_row(3, SH2, 3, 0)
            for i in range(4):
                dve.wait_ge(S["qk_ps"], 1 + i)
                n, t = i // 2, i % 2
                v.tensor_copy(qT[:, 4 * n:4 * n + 4, t * P:(t + 1) * P],
                              ps[0:QK, i, :].rearrange("p (h s) -> p h s", h=4)).then_inc(S["qT_dve"], 1)

            def soften(i):
                mixer, b, heads = GROUPS[i]
                K, n = (b + 1) * P, len(heads)
                if i == 0:
                    dve.wait_ge(L["relb"], 32)
                dve.wait_ge(S["sc_ps"], i + 1)
                if i >= 3:
                    dve.wait_ge(S["exp_ok"], i - 2)
                if mixer == 0:
                    add = cst[:, C_MASK + (1 - b) * P:C_MASK + 2 * P].unsqueeze(1).to_broadcast([P, n, K])
                    scale = QK ** -0.5
                else:
                    step = heads[1] - heads[0]
                    add = bias[:, heads[0]:heads[-1] + 1:step, K - 1::-1]
                    scale = 64 ** -0.5
                s3 = s_sb[:, i % 3, :].rearrange("p (n k) -> p n k", n=n)
                v.scalar_tensor_tensor(s3, ps[:, SC_BANK[i % 3], :].rearrange("p (n k) -> p n k", n=n), scale, add,
                                       ALU.mult, ALU.add).then_inc(S["sc_sb"], 1)
                dve.wait_ge(S["sc_sb"], i + 1)
                v.tensor_reduce(nmax[:, 4 * (i % 3):4 * (i % 3) + n], s3, AX.X, ALU.max,
                                negate=True).then_inc(S["max_ok"], 1)

            for i in range(3):
                soften(i)
            for i, (mixer, b, heads) in enumerate(GROUPS):
                if i % 2 == 1:
                    dve.wait_ge(S["pT_ps"], i + 1)
                    if i >= 2:
                        dve.wait_ge(S["pv_ps"], i - 1)
                    v.tensor_copy(pT[:, 1, :], ps[:, 3, :]).then_inc(S["pT_dve"], 1)
                if i + 3 < len(GROUPS):
                    soften(i + 3)
                for after, n, v2, col in ((4, 4, SC2, 0), (8, 5, GT2, QW)):
                    if i == after:
                        mod_row(n, v2, 7, col)
                if i + 1 == len(GROUPS) or GROUPS[i + 1][:2] != (mixer, b):
                    part = 2 * mixer + b
                    dve.wait_ge(S["exp_ok"], i + 1)
                    link(v.reciprocal(rrec, rsum[:, part * HEADS:(part + 1) * HEADS]))
                    dve.wait_ge(S["pv_ps"], i + 1)
                    v.tensor_tensor(o_sb[:, b, mixer * 512:(mixer + 1) * 512].rearrange("p (h d) -> p h d", h=HEADS),
                                    ps[:, 4 + part % 2, :].rearrange("p (h d) -> p h d", h=HEADS),
                                    rrec.unsqueeze(2).to_broadcast([P, HEADS, VD]), ALU.mult).then_inc(S["o_ok"], 1)
            for b in range(2):
                dve.wait_ge(S["oT_ps"], b + 3)
                v.tensor_copy(oT[:, 4 + 2 * b:6 + 2 * b, :],
                              ps[:, 2 + b, :].rearrange("p (a s) -> p a s", a=2)).then_inc(S["oT_dve"], 1)

            for t in range(TH):
                dve.wait_ge(S["o_rms"], t + 1)
                link(v.reciprocal(rstd[:, t:t + 1], rms[:, t:t + 1]))
                dve.wait_ge(L[f"bc{GT1}"], 16)
                link(v.scalar_tensor_tensor(h2[:, t, :].rearrange("p (n c) -> p n c", n=2), ps[:, 4 + 2 * t:6 + 2 * t, :],
                                            rstd[:, t:t + 1], bc[GT1].rearrange("p (n c) -> p n c", n=2),
                                            ALU.mult, ALU.mult))
                v.tensor_tensor(xs[:, t, :], xs[:, t, :], h2[:, t, :], ALU.add).then_inc(S["x1_ok"], 1)
                dve.wait_ge(S["x1_rms"], t + 1)
                link(v.reciprocal(rstd[:, 2 + t:3 + t], rms[:, 2 + t:3 + t]))
                dve.wait_ge(L[f"bc{SC2}"], 16)
                dve.wait_ge(L[f"bc{SH2}"], 16)
                link(v.scalar_tensor_tensor(h2[:, t, :], xs[:, t, :], rstd[:, 2 + t:3 + t], bc[SC2],
                                            ALU.mult, ALU.mult))
                for n in range(2):
                    cols_n = slice(n * D // 2, (n + 1) * D // 2)
                    v.tensor_tensor(h2[:, t, cols_n], h2[:, t, cols_n], bc[SH2][:, cols_n], ALU.add).then_inc(
                        S["h2_ok"], 1)

            dve.wait_ge(S["lg_ps"], 1)
            dve.wait_ge(L["wr"], 32)
            link(v.tensor_tensor(lg, ps[:, 0, 0:TH * E].rearrange("p (t e) -> p t e", t=TH),
                                 brt.unsqueeze(1).to_broadcast([P, TH, E]), ALU.add))
            for t in range(TH):
                last = v.max(top[:, t, :], lg[:, t, :])
            link(last)
            v.tensor_scalar(nb_neg, top[:, :, 0], -1.0, None, ALU.mult).then_inc(S["gate_ok"], 1)
            for t in range(TH):
                last = v.max_index(topi[:, t, :], top[:, t, :], lg[:, t, :])
            link(last)
            link(v.tensor_copy(topf, topi))
            four = [P, TH, TOPK, E]
            link(v.tensor_tensor(eq, iota[:, 0:E].unsqueeze(1).unsqueeze(1).to_broadcast(four),
                                 topf[:, :, 0:TOPK].unsqueeze(3).to_broadcast(four), ALU.is_equal))
            v.tensor_reduce(M, eq.rearrange("p t j e -> p t e j"), AX.X, ALU.add).then_inc(S["M_ok"], 1)
            dve.wait_ge(S["g_exp"], 1)
            link(v.reciprocal(gsum, gsum))
            for t in range(TH):
                last = v.tensor_scalar(gates[:, t, 0:TOPK], gates[:, t, 0:TOPK], gsum[:, t:t + 1], None, ALU.mult)
            link(last)
            link(v.tensor_tensor(eq, eq, gates[:, :, 0:TOPK].unsqueeze(3).to_broadcast(four), ALU.mult))
            v.tensor_reduce(G, eq.rearrange("p t j e -> p t e j"), AX.X, ALU.add).then_inc(S["G_ok"], 1)
            dve.wait_ge(S["cnt_ps"], 1)
            link(v.tensor_copy(nbc[:, 12:13], ps[0:E, 1, 0:1]))
            link(v.tensor_scalar(nbc[:, 0:8], iota[0:E, 0:SEQ:FEW], nbc[:, 12:13], None, ALU.is_lt))
            link(v.tensor_reduce(nbc[:, 8:10], nbc[:, 0:8].rearrange("p (b a) -> p a b", a=2), AX.X, ALU.add))
            link(v.tensor_scalar(nbc[:, 8:9], nbc[:, 8:9], 1.0, None, ALU.max))
            v.tensor_tensor(nbc[:, 10:11], nbc[:, 9:10], nbc[:, 8:9], ALU.subtract).then_inc(S["nb_ok"], 1)
            link(v.scalar_tensor_tensor(posm, ps[:, 1, E:3 * E].rearrange("p (t e) -> p t e", t=TH), 1.0, M,
                                        ALU.add, ALU.mult))
            v.tensor_scalar(posm, posm, -1.0, None, ALU.add).then_inc(S["pos_ok"], 1)
            def expert_and_slots(job):
                ex = dve.value_load(tab[0:1, bass.ds(T_E + job, 1)], min_val=0, max_val=E - 1)
                first = dve.value_load(tab[0:1, bass.ds(T_B + job, 1)], min_val=0, max_val=2 * SEQ - SLOT)
                return ex, cst[:, bass.ds(C_IOTA + first, SLOT)]

            def select_tokens(ex, slots):
                v.tensor_copy(bsel, cst[0:3 * E, bass.ds(C_SEL3 + ex, 1)].to_broadcast([3 * E, SLOT]))
                for t in range(TH):
                    last = v.tensor_scalar(sel[:, t, :], slots, posm[:, t, bass.ds(ex, 1)], None, ALU.is_equal)
                last.then_inc(S["sel_ok"], 1)

            def select_gates(ex, slots):
                for t in range(TH):
                    last = v.tensor_scalar(selG[:, t, :, :], slots.unsqueeze(1).to_broadcast([P, 2, SLOT]),
                                           posm[:, t, bass.ds(ex, 1)], G[:, t, bass.ds(ex, 1)], ALU.is_equal, ALU.mult)
                last.then_inc(S["selG_ok"], 1)

            dve.wait_ge(S["pos_ok"], 1)
            select_tokens(0, iota[:, 0:SLOT])
            dve.wait_ge(S["end_ps"], 1)
            j_col = cst[0:JOBS, C_J:C_J + 1]
            j_ex, j_blk, j_few, j_out = (jt[:, 3 * E + i:3 * E + i + 1] for i in (0, 1, 2, 4))
            v.tensor_scalar(jt[:, 2 * E:3 * E], ps[0:JOBS, 3, 2 * E:3 * E], j_col, None, ALU.is_le)
            link(v.tensor_scalar(jt[:, 0:E], ps[0:JOBS, 3, 0:E], j_col, None, ALU.is_le))
            link(v.tensor_tensor(jt[:, E:2 * E], jt[:, 0:E], ps[0:JOBS, 3, E:2 * E], ALU.mult))
            link(v.tensor_reduce(jt[:, 3 * E:3 * E + 3], jt[:, 0:3 * E].rearrange("p (a e) -> p a e", a=3), AX.X,
                                 ALU.add))
            v.tensor_tensor(j_few, j_few, j_ex, ALU.subtract)
            link(v.tensor_tensor(j_blk, j_col, j_blk, ALU.subtract))
            v.tensor_scalar(j_ex, j_ex, float(E - 1), None, ALU.min)
            link(v.tensor_scalar(j_blk, j_blk, float(MAXBLK - 1), float(SLOT), ALU.min, ALU.mult))
            v.scalar_tensor_tensor(j_out, j_few, float(SEQ), j_blk, ALU.mult, ALU.add).then_inc(S["je_ok"], 1)
            dve.wait_ge(S["row_ps"], 1)
            v.tensor_copy(tab[:, 0:T_B + JOBS], ps[0:1, 5, 0:T_B + JOBS]).then_inc(S["tab_ok"], 1)
            dve.wait_ge(S["tab_ok"], 1)

            ex, slots = expert_and_slots(0)
            dve.wait_ge(S["GT_ps"], 1)
            v.tensor_copy(GT, ps[0:E, 2, 0:SEQ]).then_inc(S["GT_sb"], 1)
            select_gates(ex, slots)
            total = dve.value_load(tab[0:1, T_J + E:T_J + E + 1], min_val=E, max_val=JOBS)
            with dve.Fori(0, total) as job:
                ex, slots = expert_and_slots(job + 1)
                dve.wait_ge(S["gate_ps"], job + 1)
                v.tensor_scalar(gm, ps[:, 4, :], LIMIT, None, ALU.min).then_inc(S["gm_ok"], 1)
                select_tokens(ex, slots)
                dve.wait_ge(S["sig_ok"], job + 1)
                v.tensor_tensor(gm, gm, sg, ALU.mult)
                dve.wait_ge(used[GU_UNITS - 1], job + 1)
                v.tensor_scalar(up1, ps[:, 5, :], LIMIT, -LIMIT, ALU.min, ALU.max).then_inc(S["up_ok"], 1)
                dve.wait_ge(S["up_ok"], job + 1)
                v.scalar_tensor_tensor(act_b, up1, 1.0, gm, ALU.add, ALU.mult).then_inc(S["act_ok"], 1)
                dve.wait_ge(S["actT_ps"], job + 1)
                v.tensor_copy(actT, ps[:, 7, :]).then_inc(S["actT_sb"], 1)
                select_gates(ex, slots)

            for t in range(TH):
                dve.wait_ge(S["f_rms"], t + 1)
                link(v.reciprocal(rstd[:, t:t + 1], rms[:, t:t + 1]))
                last = v.scalar_tensor_tensor(out_sb[:, t, :].rearrange("p (n c) -> p n c", n=2),
                                              ps[:, 2 * t:2 * t + 2, :], rstd[:, t:t + 1],
                                              bc[GT2].rearrange("p (n c) -> p n c", n=2), ALU.mult, ALU.mult)
                if t == 0:
                    last.then_inc(S["res_mul"], 1)
                else:
                    link(last)
                    v.tensor_tensor(out_sb[:, t, :], out_sb[:, t, :], xs[:, t, :], ALU.add).then_inc(S["res_ok"], 1)


_INS = ['x', 'c', 'w_ada', 'b_ada', 'g_pre_mix', 'g_post_mix', 'g_pre_ffn', 'g_post_ffn', 'w_in', 'g_q', 'w_qb',
        'g_kv', 'w_kvb', 'rel_bias', 'w_o', 'w_router', 'b_router', 'w_gu', 'b_gu', 'w_down', 'b_down']
_OUTS = [((1, SEQ, D), 'float32')]


def kernel(**inputs):
    import numpy as _np
    import concourse.bacc as _bacc
    from concourse import mybir as _mybir
    from concourse.bass_utils import run_bass_kernel_spmd as _run

    nc = _bacc.Bacc("TRN2", target_bir_lowering=False, num_devices=1)
    arrays, args = {}, []
    for name in _INS + ['consts']:
        a = shape_constants() if name == 'consts' else _np.ascontiguousarray(inputs[name])
        arrays[f"in_{name}_dram"] = a
        args.append(nc.dram_tensor(f"in_{name}_dram", a.shape, _mybir.dt.from_np(a.dtype), kind="ExternalInput").ap())
    for i, (shape, dtype) in enumerate(_OUTS):
        dt = _mybir.dt.from_np(_np.dtype(dtype))
        args.append(nc.dram_tensor(f"out_{i}_dram", shape, dt, kind="ExternalOutput").ap())
    build(nc, *args)
    r = _run(nc, [arrays], core_ids=[0])
    got = tuple(r.results[0][f"out_{i}_dram"] for i in range(len(_OUTS)))
    return got[0]
```
